# Optimizing a Trainium2 kernel written in Bass

```python
import jax, jax.numpy as jnp
from jax import lax
import numpy as np

D_MODEL = 1024
BATCH = 1
SEQ = 1024
DEPTH = 1

D_MIX = D_MODEL
D_SGU = D_MIX // 2
SGU_HEADS = 8
SGU_HEAD_DIM = D_SGU // SGU_HEADS
SGU_CHUNK = 128
D_GLA = D_MIX - D_SGU
GLA_HEADS = 4
GLA_DK = D_GLA // 2
GLA_HEAD_K = GLA_DK // GLA_HEADS
GLA_HEAD_V = D_GLA // GLA_HEADS
GLA_GATE_RANK = 16
GLA_TAU = 16.0
GLA_CHUNK = 64
D_IN = 2 * D_SGU + 2 * GLA_DK + 2 * D_GLA + GLA_GATE_RANK
N_EXPERTS = 32
TOP_K = 4
D_EXPERT = D_MODEL
SWIGLU_LIMIT = 7.0
SWIGLU_ALPHA = 1.702
MOE_BLOCK = 128
EPS = 1e-6

kernel_name = "hybrid_sgu_gla_moe_block"

def rms_norm(x, g):
    xf = x.astype(jnp.float32)
    y = xf * lax.rsqrt(jnp.mean(xf * xf, axis=-1, keepdims=True) + EPS)
    return (y * g.astype(jnp.float32)).astype(x.dtype)

def spatial_gating(u, v, g_v, w_s, b_s):
    B, S, _ = u.shape
    N = S // SGU_CHUNK
    vh = rms_norm(v.reshape(B, S, SGU_HEADS, SGU_HEAD_DIM), g_v.reshape(SGU_HEADS, SGU_HEAD_DIM))
    vc = vh.reshape(B, N, SGU_CHUNK, SGU_HEADS, SGU_HEAD_DIM)
    w_causal = jnp.tril(w_s)
    sv = jnp.einsum('hts,bnshd->bnthd', w_causal, vc) + b_s.T[None, None, :, :, None]
    return (u.reshape(B, N, SGU_CHUNK, SGU_HEADS, SGU_HEAD_DIM) * sv).reshape(B, S, D_SGU)

def gated_linear_attention(q, k, v, log_a):
    B, S, H, dk = q.shape
    dv = v.shape[-1]
    N = S // GLA_CHUNK
    dt = q.dtype

    def chunk(t):
        return t.reshape(B, N, GLA_CHUNK, H, t.shape[-1]).transpose(0, 3, 1, 2, 4)

    qc, kc, vc = chunk(q) * (GLA_HEAD_K ** -0.5), chunk(k), chunk(v)
    bcum = jnp.cumsum(chunk(log_a).astype(jnp.float32), axis=3)
    blast = bcum[:, :, :, -1:, :]
    q_s = qc * jnp.exp(bcum).astype(dt)
    k_s = kc * jnp.exp(-bcum).astype(dt)
    k_dec = kc * jnp.exp(blast - bcum).astype(dt)
    scores = jnp.einsum('bhnid,bhnjd->bhnij', q_s, k_s)
    causal = jnp.tril(jnp.ones((GLA_CHUNK, GLA_CHUNK), dtype=bool))
    scores = jnp.where(causal, scores, jnp.zeros((), dt))
    intra = jnp.einsum('bhnij,bhnjv->bhniv', scores, vc)
    d_state = jnp.einsum('bhncd,bhncv->bhndv', k_dec, vc)
    decay = jnp.exp(blast[:, :, :, 0, :]).astype(d_state.dtype)

    def step(state, inp):
        dn, dsn = inp
        return dn[..., None] * state + dsn, state

    init = jnp.zeros((B, H, dk, dv), d_state.dtype)
    _, prev = lax.scan(step, init, (jnp.moveaxis(decay, 2, 0), jnp.moveaxis(d_state, 2, 0)))
    prev = jnp.moveaxis(prev, 0, 2)
    inter = jnp.einsum('bhncd,bhndv->bhncv', q_s, prev)
    o = intra + inter
    return o.transpose(0, 2, 3, 1, 4).reshape(B, S, H, dv)

def moe_ffn(xn, w_router, b_router, w_gate, b_gate, w_up, b_up, w_down, b_down):
    B, S, D = xn.shape
    T = B * S
    xt = xn.reshape(T, D)
    logits = (xt @ w_router + b_router).astype(jnp.float32)
    top_v, top_i = lax.top_k(logits, TOP_K)
    probs = jax.nn.softmax(top_v, axis=-1).astype(xn.dtype)
    TK = T * TOP_K
    flat_e = top_i.reshape(TK)
    flat_tok = jnp.repeat(jnp.arange(T, dtype=jnp.int32), TOP_K)
    flat_w = probs.reshape(TK)
    order = jnp.argsort(flat_e, stable=True)
    sorted_e = flat_e[order]
    counts = jnp.bincount(flat_e, length=N_EXPERTS)
    start = jnp.cumsum(counts) - counts
    padded = ((counts + MOE_BLOCK - 1) // MOE_BLOCK) * MOE_BLOCK
    pend = jnp.cumsum(padded)
    pstart = pend - padded
    dest = pstart[sorted_e] + (jnp.arange(TK, dtype=jnp.int32) - start[sorted_e])
    n_blocks = -(-TK // MOE_BLOCK) + N_EXPERTS
    P = n_blocks * MOE_BLOCK
    tok_buf = jnp.zeros((P,), jnp.int32).at[dest].set(flat_tok[order])
    w_buf = jnp.zeros((P,), xn.dtype).at[dest].set(flat_w[order])
    block_e = jnp.clip(jnp.searchsorted(pend, jnp.arange(n_blocks) * MOE_BLOCK, side='right'), 0, N_EXPERTS - 1)
    x_blocks = xt[tok_buf].reshape(n_blocks, MOE_BLOCK, D)

    def expert_block(args):
        xb, e = args
        g = jnp.minimum(xb @ w_gate[e] + b_gate[e], SWIGLU_LIMIT)
        u = jnp.clip(xb @ w_up[e] + b_up[e], -SWIGLU_LIMIT, SWIGLU_LIMIT)
        hdn = (u + 1.0) * (g * jax.nn.sigmoid(SWIGLU_ALPHA * g))
        return hdn @ w_down[e] + b_down[e]

    out = lax.map(expert_block, (x_blocks, block_e)).reshape(P, D)
    y = jnp.zeros((T, D), out.dtype).at[tok_buf].add(out * w_buf[:, None])
    return y.reshape(B, S, D)

def setup_inputs(seed: int = 0) -> dict:
    key = jax.random.key(seed)
    ks = jax.random.split(key, 26)
    f32 = jnp.float32
    L = DEPTH

    def nrm(k, shape, scale):
        return jax.random.normal(k, shape, f32) * scale

    def gain(k, shape):
        return 1.0 + 0.05 * jax.random.normal(k, shape, f32)

    return {
        "x": jax.random.normal(ks[0], (BATCH, SEQ, D_MODEL), f32),
        "c": jax.random.normal(ks[1], (BATCH, D_MODEL), f32),
        "w_ada": nrm(ks[2], (L, D_MODEL, 6 * D_MODEL), 0.5 * D_MODEL ** -0.5),
        "b_ada": nrm(ks[3], (L, 6 * D_MODEL), 0.02),
        "g_pre_mix": gain(ks[4], (L, D_MODEL)),
        "w_in": nrm(ks[5], (L, D_MODEL, D_IN), D_MODEL ** -0.5),
        "g_sgu_v": gain(ks[6], (L, D_SGU)),
        "w_s": nrm(ks[7], (L, SGU_HEADS, SGU_CHUNK, SGU_CHUNK), SGU_CHUNK ** -0.5),
        "b_s": gain(ks[8], (L, SGU_HEADS, SGU_CHUNK)),
        "w_gk2": nrm(ks[9], (L, GLA_GATE_RANK, GLA_DK), GLA_GATE_RANK ** -0.5),
        "b_gk": nrm(ks[10], (L, GLA_DK), 0.1),
        "g_gla_out": gain(ks[11], (L, GLA_HEAD_V)),
        "w_out": nrm(ks[12], (L, D_MIX, D_MODEL), D_MIX ** -0.5),
        "g_post_mix": gain(ks[13], (L, D_MODEL)),
        "g_pre_ffn": gain(ks[14], (L, D_MODEL)),
        "w_router": nrm(ks[15], (L, D_MODEL, N_EXPERTS), D_MODEL ** -0.5),
        "b_router": nrm(ks[16], (L, N_EXPERTS), 0.01),
        "w_gate": nrm(ks[17], (L, N_EXPERTS, D_MODEL, D_EXPERT), D_MODEL ** -0.5),
        "b_gate": nrm(ks[18], (L, N_EXPERTS, D_EXPERT), 0.01),
        "w_up": nrm(ks[19], (L, N_EXPERTS, D_MODEL, D_EXPERT), D_MODEL ** -0.5),
        "b_up": nrm(ks[20], (L, N_EXPERTS, D_EXPERT), 0.01),
        "w_down": nrm(ks[21], (L, N_EXPERTS, D_EXPERT, D_MODEL), D_EXPERT ** -0.5),
        "b_down": nrm(ks[22], (L, N_EXPERTS, D_MODEL), 0.01),
        "g_post_ffn": gain(ks[23], (L, D_MODEL)),
    }

def reference(x, c, w_ada, b_ada, g_pre_mix, w_in, g_sgu_v, w_s, b_s, w_gk2, b_gk, g_gla_out, w_out,
              g_post_mix, g_pre_ffn, w_router, b_router, w_gate, b_gate, w_up, b_up, w_down, b_down, g_post_ffn):
    B, S, _ = x.shape
    split_at = list(np.cumsum([D_SGU, D_SGU, GLA_DK, GLA_DK, D_GLA, D_GLA]))
    h = x
    for l in range(DEPTH):
        mods = jax.nn.silu(c) @ w_ada[l] + b_ada[l]
        shift1, scale1, gate1, shift2, scale2, gate2 = [m[:, None, :] for m in jnp.split(mods, 6, axis=-1)]

        n = rms_norm(h, g_pre_mix[l]) * (1.0 + scale1) + shift1
        proj = n @ w_in[l]
        u_s, v_s, q, k, v, r, g_low = jnp.split(proj, split_at, axis=-1)
        a_out = spatial_gating(jax.nn.gelu(u_s), jax.nn.gelu(v_s), g_sgu_v[l], w_s[l], b_s[l])
        log_a = jax.nn.log_sigmoid((g_low @ w_gk2[l] + b_gk[l]).astype(jnp.float32)) / GLA_TAU
        o = gated_linear_attention(q.reshape(B, S, GLA_HEADS, GLA_HEAD_K),
                                   k.reshape(B, S, GLA_HEADS, GLA_HEAD_K),
                                   v.reshape(B, S, GLA_HEADS, GLA_HEAD_V),
                                   log_a.reshape(B, S, GLA_HEADS, GLA_HEAD_K))
        o = rms_norm(o, g_gla_out[l]).reshape(B, S, D_GLA) * jax.nn.silu(r)
        mix = jnp.concatenate([a_out, o], axis=-1) @ w_out[l]
        h = h + gate1 * rms_norm(mix, g_post_mix[l])

        n2 = rms_norm(h, g_pre_ffn[l]) * (1.0 + scale2) + shift2
        f = moe_ffn(n2, w_router[l], b_router[l], w_gate[l], b_gate[l], w_up[l], b_up[l], w_down[l], b_down[l])
        h = h + gate2 * rms_norm(f, g_post_ffn[l])
    return h


_drawn_inputs = setup_inputs


def setup_inputs(seed=0):
    import zlib

    import numpy as np

    out = dict(_drawn_inputs(seed))
    spreads = {}
    factors = {'g_sgu_v': 3.391,
     'b_s': 2.865,
     'b_gk': 2.676,
     'g_gla_out': 2.751,
     'b_router': 2.708,
     'b_gate': 8.0,
     'b_up': 8.0,
     'b_down': 8.0,
     'g_post_ffn': 4.039}
    for name, (base, spread) in spreads.items():
        noise = np.random.default_rng([zlib.crc32(name.encode()), seed]).standard_normal(out[name].shape)
        drawn = base * np.exp(spread * noise) if base else spread * noise
        out[name] = __import__('jax').numpy.asarray(drawn.astype(out[name].dtype))
    for name, factor in factors.items():
        out[name] = (out[name] * factor).astype(out[name].dtype)
    return out
```

```python
from contextlib import ExitStack

import concourse.bass as bass
from concourse import mybir

F32 = mybir.dt.float32
I32 = mybir.dt.int32
U32 = mybir.dt.uint32
ALU = mybir.AluOpType
ACT = mybir.ActivationFunctionType
AX_X = mybir.AxisListType.X

P = 128
D = 1024
KD = D // P
T = 1024
NT = T // P
DS = 512
SH, SHD = 8, 64
GH, GV = 4, 128
DK = 64
CH = 64
RANK = 16
DIN = 2576
E = 32
TOPK = 4
BLK = 3
CAP = BLK * P
NCHUNK = -(-T // CAP)
COLS = NCHUNK * BLK
TPITCH = 512
NCOL = (E + 1) * COLS
EMPTY = 1 << 20
NOVER = (NCHUNK - 1) * E
WIDTHS = [w for w in range(64, 320, 32) if w < CAP] + [CAP]
LIMIT = 7.0
ALPHA = 1.702
EPS = 1e-6
SPARE = KD * DIN


class Chain:

    def __init__(self, eng, sem):
        self.eng, self.sem, self.n = eng, sem, 0

    def restart(self):
        self.eng.sem_clear(self.sem)
        self.n = 0

    def settle(self):
        self.n += 1
        self.eng.sem_inc(self.sem, 1)
        self.eng.wait_ge(self.sem, self.n)

    def link(self, ins):
        self.n += 1
        ins.then_inc(self.sem, 1)
        self.eng.wait_ge(self.sem, self.n)


def hybrid_block(nc, a, out):
    ctx = ExitStack()
    with ctx:
        def sb(name, shape, dt=F32):
            return ctx.enter_context(nc.sbuf_tensor(name, shape, dt))

        def sem(name):
            return ctx.enter_context(nc.semaphore(name))

        def dram(name, shape, dt=F32):
            return nc.dram_tensor(name, shape, dt, kind="Internal").ap()

        h_dram = dram("h_dram", (T, D))
        n2_dram = dram("n2_dram", (T, D))
        y_dram = dram("y_dram", (T * TOPK, D))
        slot_dram = dram("slot_dram", (P * TPITCH, 1), I32)
        gate2_dram = dram("gate2_dram", (1, D))

        W = sb("W", [P, 6 * 4096])
        WO = sb("WO", [P, 8192])
        BIG = sb("BIG", [P, 6144])
        w_in = W[:, 0:SPARE].rearrange("p (k n) -> p k n", k=KD)
        pieces = [W[:, s * 4096:(s + 1) * 4096] for s in range(6)]
        spare_at = [SPARE]

        def spare(*shape):
            size = 1
            for n in shape:
                size *= n
            lo = spare_at[0]
            spare_at[0] = lo + size
            assert lo + size <= 6 * 4096
            v = W[:, lo:lo + size]
            if len(shape) == 2:
                v = v.rearrange("p (a b) -> p a b", a=shape[0])
            if len(shape) == 3:
                v = v.rearrange("p (a b c) -> p a b c", a=shape[0], b=shape[1])
            return v

        ada = [WO[:, s * 4096:(s + 1) * 4096].rearrange("p (k n) -> p k n", k=KD) for s in range(2)]
        w_out = WO[:, :].rearrange("p (k n) -> p k n", k=KD)
        xg = WO[:, 0:BLK * D].rearrange("p (b d) -> p b d", b=BLK)
        xT = WO[:, BLK * D:2 * BLK * D].rearrange("p (k n) -> p k n", k=KD)
        g_sb = WO[:, 6144:6144 + 2 * CAP].rearrange("p (a n) -> p a n", a=2)
        u_sb = WO[:, 6144 + 2 * CAP:6144 + 4 * CAP].rearrange("p (a n) -> p a n", a=2)
        rows = BIG[:, 0:4096].rearrange("p (a j n) -> p a j n", a=2, j=4)
        adarow = BIG[:, 0:2048].rearrange("p (a n) -> p a n", a=2)
        g2row, gprow = BIG[:, 2048:3072], BIG[:, 3072:4096]
        nT = BIG[:, 4096:5120].rearrange("p (k n) -> p k n", k=KD)
        catT = BIG[:, 5120:6144].rearrange("p (k n) -> p k n", k=KD)
        cbc = catT
        yo = BIG[:, 0:BLK * D].rearrange("p (b d) -> p b d", b=BLK)
        hT = BIG[:, BLK * D:2 * BLK * D].rearrange("p (k n) -> p k n", k=KD)

        xh = sb("xh", [P, 2, D])
        xn = sb("xn", [P, D])
        cat = sb("cat", [P, D])
        s_sb = cat[:, 0:2 * CAP].rearrange("p (a n) -> p a n", a=2)
        gate1 = sb("gate1", [P, D])
        A2 = sb("A2", [P, D])
        B2 = sb("B2", [P, D])
        gidx = B2[:, 0:NCOL].bitcast(I32)
        wsT = spare(SH, P)
        keep = spare(GH, P)
        vsq = spare(DS)
        Sm = spare(GH, P)
        state = spare(2, 2, P)
        zb = spare(2, P)
        az = spare(2, P)
        kdT = spare(2, P)
        osq = sb("osq", [P, DS])
        glT = sb("glT", [RANK, P])
        wgk = sb("wgk", [RANK, 2 * P])
        bgkT = sb("bgkT", [P, 2])
        bc = sb("bc", [P, 2, P])
        eb = sb("eb", [P, 2, P])
        enb = sb("enb", [P, 2, P])
        dec = sb("dec", [P, 2, P])
        qz = sb("qz", [P, 2, 2, P])
        ks = sb("ks", [P, 2, P])
        kdz = sb("kdz", [P, 2, 2 * P])
        gv_row = sb("gv_row", [P, DS])
        go_row = sb("go_row", [P, GV])
        bsT = sb("bsT", [P, SH])
        wr = sb("wr", [P, KD, E])
        br = sb("br", [P, E])
        ident = sb("ident", [P, P])
        ones = sb("ones", [P, P])
        before = sb("before", [P, P])
        reset = sb("reset", [P, 2 * P])
        ccol = sb("ccol", [P, KD])
        siluc = sb("siluc", [P, KD])
        badac = sb("badac", [P, 2, KD])
        gpre = sb("gpre", [P, KD])
        A1 = sb("A1", [P, KD])
        B1 = sb("B1", [P, KD])
        eps = sb("eps", [P, 1])
        xs = sb("xs", [P, 4])
        vs = sb("vs", [P, 3, SH])
        os_ = sb("os_", [P, 3, GH])
        ms = sb("ms", [P, 8])
        iotaE = sb("iotaE", [P, E])
        iotaEi = sb("iotaEi", [P, E], I32)
        vals = sb("vals", [P, NT, TOPK], I32)
        vcur = sb("vcur", [P, TOPK], I32)
        lg = sb("lg", [P, E])
        top8 = sb("top8", [P, 8])
        ti8 = sb("ti8", [P, 8], U32)
        tif = sb("tif", [P, TOPK])
        dif4 = sb("dif4", [P, TOPK])
        ex4 = sb("ex4", [P, TOPK])
        exsum = sb("exsum", [P, 2])
        oneh = sb("oneh", [P, TOPK, E])
        tmpk = sb("tmpk", [P, TOPK, E])
        chosen = sb("chosen", [P, E])
        csum = sb("csum", [P, E])
        cum = sb("cum", [P, E])
        rank = sb("rank", [P, TOPK])
        ranki = sb("ranki", [P, TOPK], I32)
        ia = sb("ia", [P, TOPK], I32)
        ib = sb("ib", [P, TOPK], I32)
        ic = sb("ic", [P, TOPK], I32)
        iab = sb("iab", [P, TOPK], I32)
        slot = sb("slot", [P, TOPK], I32)
        sslot = sb("sslot", [P, TOPK], I32)
        probs = sb("probs", [P, NT, TOPK])
        wden = sb("wden", [P, NT, E])
        pcur = sb("pcur", [P, TOPK])
        wcur = sb("wcur", [P, E])
        wdT = sb("wdT", [E, P])
        bgT = sb("bgT", [P, E, KD])
        buT = sb("buT", [P, E, KD])
        bcur = sb("bcur", [P, 2, KD])
        sidx = sb("sidx", [P, NCOL], I32)
        scol = sb("scol", [P, BLK], I32)
        scur = sb("scur", [P, BLK], I32)
        gcur = sb("gcur", [P, BLK], I32)
        cnti = sb("cnti", [1, E + 1], I32)
        overn = sb("overn", [1, NOVER], I32)
        overo = sb("overo", [1, NOVER], I32)
        overf = osq[0:1, 0:3 * NOVER].rearrange("p (a n) -> p a n", a=3)
        overt = sb("overt", [1, 1], I32)

        ps = [ctx.enter_context(nc.psum_tensor(f"ps{i}", [P, 512], F32)) for i in range(8)]
        T0, T1, R0, R1, QK, ZB, SG, OB = ps
        TD = ps[4:8]

        c_in = sem("c_in")
        c2_in = sem("c2_in")
        x_loaded = sem("x_loaded")
        wout_in = sem("wout_in")
        h_stored = sem("h_stored")
        n2_stored = sem("n2_stored")
        n2_free = sem("n2_free")
        pool_c = sem("pool_c")
        dve_c = sem("dve_c")
        act_c = sem("act_c")
        const_ready = sem("const_ready")
        silu_ready = sem("silu_ready")
        cbc_ready = sem("cbc_ready")
        ada_done = sem("ada_done")
        ada_evac = sem("ada_evac")
        adat_done = sem("adat_done")
        gate2_stored = sem("gate2_stored")
        mods_ready = sem("mods_ready")
        wst_done = sem("wst_done")
        wst_evac = sem("wst_evac")
        wst_masked = sem("wst_masked")
        xstat = sem("xstat")
        xn_ready = sem("xn_ready")
        xt_done = sem("xt_done")
        nT_ready = sem("nT_ready")
        u_done = sem("u_done")
        v_done = sem("v_done")
        vv_done = sem("vv_done")
        r_done = sem("r_done")
        qk_done = sem("qk_done")
        glow_done = sem("glow_done")
        gu_ready = sem("gu_ready")
        gv_ready = sem("gv_ready")
        vv_ready = sem("vv_ready")
        sr_ready = sem("sr_ready")
        vsum_ready = sem("vsum_ready")
        vrstd_ready = sem("vrstd_ready")
        vh_ready = sem("vh_ready")
        gl_ready = sem("gl_ready")
        z_done = sem("z_done")
        z_ready = sem("z_ready")
        lnz_ready = sem("lnz_ready")
        bc_ready = sem("bc_ready")
        exp_ready = sem("exp_ready")
        qks_ready = sem("qks_ready")
        kdt_done = sem("kdt_done")
        kdz_ready = sem("kdz_ready")
        s_done = sem("s_done")
        sm_ready = sem("sm_ready")
        ds_done = sem("ds_done")
        st1_ready = sem("st1_ready")
        st0_ready = sem("st0_ready")
        sgu_done = sem("sgu_done")
        o_done = sem("o_done")
        osq_ready = sem("osq_ready")
        osum_ready = sem("osum_ready")
        orstd_ready = sem("orstd_ready")
        cat_ready = sem("cat_ready")
        catt_done = sem("catt_done")
        catT_ready = sem("catT_ready")
        mix_done = sem("mix_done")
        mstat = sem("mstat")
        h_ready = sem("h_ready")
        hstat = sem("hstat")
        n2_ready = sem("n2_ready")
        n2t_done = sem("n2t_done")
        n2T_ready = sem("n2T_ready")
        lg_done = sem("lg_done")
        dif_ready = sem("dif_ready")
        ex_ready = sem("ex_ready")
        chosen_ready = sem("chosen_ready")
        cum_done = sem("cum_done")
        slot_ready = sem("slot_ready")
        slot_free = sem("slot_free")
        cnt_done = sem("cnt_done")
        cnt_ready = sem("cnt_ready")
        table_in = sem("table_in")
        gidx_ready = sem("gidx_ready")
        psum_init = sem("psum_init")
        xgt_done = sem("xgt_done")
        xTa = sem("xTa")
        xTd = sem("xTd")
        gup_done = sem("gup_done")
        gup_free = sem("gup_free")
        g_ready = sem("g_ready")
        sig_ready = sem("sig_ready")
        hid_ready = sem("hid_ready")
        down_done = sem("down_done")
        yo_ready = sem("yo_ready")
        yo_free = sem("yo_free")
        moe_done = sem("moe_done")
        bd_in = sem("bd_in")
        wcur_ready = sem("wcur_ready")
        wdt_done = sem("wdt_done")
        wdT_ready = sem("wdT_ready")
        bias_done = sem("bias_done")
        f_ready = sem("f_ready")
        fstat = sem("fstat")
        g2_in = sem("g2_in")
        g2_ready = sem("g2_ready")
        prefill_in = sem("prefill_in")
        ada_in = [sem(f"ada_in{i}") for i in range(2)]
        win_in = [sem(f"win_in{i}") for i in range(2)]
        scattered = [sem(f"scattered{k}") for k in range(TOPK)]
        piece_in = [sem(f"piece_in{s}") for s in range(6)]
        xg_in = [sem(f"xg_in{b}") for b in range(BLK)]
        y_stored = [sem(f"y_stored{b}") for b in range(BLK)]
        y_in = [sem(f"y_in{i}") for i in range(2)]
        hb_in = [sem(f"hb_in{i}") for i in range(2)]
        o_ready = [sem(f"o_ready{i}") for i in range(2)]
        out_stored = [sem(f"out_stored{i}") for i in range(2)]
        oslot_free = [sem(f"oslot_free{i}") for i in range(2)]
        const_in = sem("const_in")
        N_CONST = 17

        ADA = [(m, half) for m in (1, 0, 2, 3, 4, 5) for half in (0, 1)]
        EARLY = 4

        def x_rows(t):
            return a["x"][0, bass.ds(t * P, P), :]

        def xrow(t):
            return xh[:, bass.ds(t % 2, 1), :].rearrange("p a d -> p (a d)")

        def rowbuf(t, j):
            return rows[:, bass.ds(t % 2, 1), j, :].rearrange("p a n -> p (a n)")

        def stage4(i):
            lo = i * 6144
            return W[:, lo:lo + 4096], W[:, lo + 4096:lo + 5120], W[:, lo + 5120:lo + 6144]

        gate2 = W[:, 12288:13312]
        badarow = W[:, 13312:14336]
        gfrow = W[:, 14336:15360]
        junk4 = W[:, 15360:16384]
        bdown = W[0:E, 16384:17408]

        def bcast_row(src, n):
            return src.rearrange("(o n) -> o n", o=1).broadcast_to((P, n))

        def overflow(eng, body):
            over = eng.value_load(overt[0:1, 0:1], min_val=0, max_val=NOVER)
            with eng.If(over > 0):
                with eng.Fori(0, NOVER) as j:
                    left = eng.value_load(overn[0:1, bass.ds(j, 1)], min_val=-T, max_val=T)
                    nth = eng.value_load(overo[0:1, bass.ds(j, 1)], min_val=0, max_val=NOVER)
                    with eng.If(left > 0):
                        body(j % E, j // E + 1, nth, left)

        block = ctx.enter_context(nc.Block())

        @block.sync
        def _(sp):
            sp.dma_start(ccol[:], a["c"].rearrange("b (p k) -> p (b k)", k=KD)).then_inc(c_in, 16)
            sp.dma_start(xh[:, 0, :], x_rows(0)).then_inc(x_loaded, 16)
            for dst, src in (
                    (nT, a["w_s"][0].rearrange("h t s -> t h s")),
                    (xn[0:SH, 0:P], a["b_s"][0]),
                    (xn[0:2, P:2 * P], a["b_gk"][0].rearrange("(a p) -> a p", a=2)),
                    (cat[0:E, :], a["b_gate"][0]),
                    (xh[0:E, 1, :], a["b_up"][0]),
                    (badac[:], a["b_ada"][0, 0:2 * D].rearrange("(m p k) -> p m k", m=2, k=KD)),
                    (gpre[:], a["g_pre_mix"][0].rearrange("(p k) -> p k", k=KD)),
                    (wgk[:], a["w_gk2"][0]),
                    (wr[:], a["w_router"][0].rearrange("(p k) e -> p k e", k=KD)),
                    (gv_row[:], bcast_row(a["g_sgu_v"][0], DS)),
                    (go_row[:], bcast_row(a["g_gla_out"][0], GV)),
                    (br[:], bcast_row(a["b_router"][0], E)),
                    (gate1[:], bcast_row(a["b_ada"][0, 2 * D:3 * D], D)),
                    (B2[:], bcast_row(a["b_ada"][0, 3 * D:4 * D], D)),
                    (A2[:], bcast_row(a["b_ada"][0, 4 * D:5 * D], D)),
                    (gprow, bcast_row(a["g_post_mix"][0], D)),
                    (g2row, bcast_row(a["g_pre_ffn"][0], D))):
                sp.dma_start(dst, src).then_inc(const_in, 16)

            w_in_v = a["w_in"][0].rearrange("(p k) n -> p k n", k=KD)
            for n, (m, half) in enumerate(ADA):
                if n == EARLY:
                    for j, (lo, hi) in enumerate(((0, D), (D, DIN))):
                        sp.dma_start(w_in[:, :, lo:hi], w_in_v[:, :, lo:hi]).then_inc(win_in[j], 16)
                if n >= 2:
                    sp.wait_ge(ada_done, n - 1)
                col = m * D + half * 512
                sp.dma_start(ada[n % 2], a["w_ada"][0].rearrange("(p k) n -> p k n", k=KD)[:, :, col:col + 512]
                             ).then_inc(ada_in[n % 2], 16)
            sp.wait_ge(ada_done, len(ADA))
            sp.dma_start(w_out, a["w_out"][0].rearrange("(k p) n -> p k n", p=P)).then_inc(wout_in, 16)
            sp.wait_ge(wst_evac, 2)
            sp.wait_ge(x_loaded, 16)
            sp.dma_start(xh[:, 1, :], x_rows(1)).then_inc(x_loaded, 16)
            for half, buf in ((0, osq), (1, vsq)):
                sp.wait_ge(ada_evac, len(ADA) - 1 + half)
                sp.dma_start(gate2_dram[:, half * 512:(half + 1) * 512], buf[0:1, :]).then_inc(gate2_stored, 16)

            def store(t):
                sp.wait_ge(h_ready, t + 1)
                sp.dma_start(h_dram[bass.ds(t * P, P), :], xrow(t)).then_inc(h_stored, 16)
                sp.wait_ge(n2_ready, t + 1)
                sp.dma_start(n2_dram[bass.ds(t * P, P), :], xn[:]).then_inc(n2_stored, 16)
                sp.wait_ge(n2_stored, t * 16 + 16)
                sp.wait_ge(h_stored, t * 16 + 16)
                sp.sem_inc(n2_free, 1)

            sp.sem_inc(n2_free, 1)
            with sp.Fori(0, NT - 2) as t:
                store(t)
                sp.wait_ge(x_loaded, t * 16 + 32)
                sp.dma_start(xrow(t), x_rows(t + 2)).then_inc(x_loaded, 16)
            store(NT - 2)

            def load_expert(e, n):
                gate, up, down = (a[w][0, bass.ds(e, 1), :, :] for w in ("w_gate", "w_up", "w_down"))
                for s in range(6):
                    if n is not None:
                        if s < 2:
                            sp.wait_ge(gup_done, n * KD - 4)
                        elif s < 4:
                            sp.wait_ge(gup_done, n * KD)
                        else:
                            sp.wait_ge(down_done, n * BLK)
                    elif s == 5:
                        store(NT - 1)
                        sp.wait_ge(cat_ready, NT)
                    if s < 4:
                        src = (gate if s % 2 == 0 else up).rearrange("e (p k) f -> p (e k) f", k=KD)[
                            :, :, (s // 2) * 512:(s // 2) * 512 + 512]
                        dst = pieces[s].rearrange("p (k f) -> p k f", k=KD)
                    else:
                        src = down.rearrange("e (k p) d -> p (e k) d", p=P)[:, (s - 4) * 4:(s - 4) * 4 + 4, :]
                        dst = pieces[s].rearrange("p (k f) -> p k f", k=4)
                    sp.dma_start(dst, src).then_inc(piece_in[s], 16)

            sp.wait_ge(glow_done, NT)
            load_expert(0, None)
            with sp.Fori(1, E) as e:
                load_expert(e, e)

            sp.wait_ge(cnt_ready, 1)
            overflow(sp, lambda e, c, nth, left: load_expert(e, nth + E))

            sp.wait_ge(moe_done, 1)
            for dst, src in ((gate2, bcast_row(gate2_dram[0], D)),
                             (badarow, bcast_row(a["b_ada"][0, 5 * D:6 * D], D)),
                             (gfrow, bcast_row(a["g_post_ffn"][0], D)),
                             (bdown, a["b_down"][0])):
                sp.dma_start(dst, src).then_inc(g2_in, 16)

            def load_y(t, i):
                yb, hb, _ = stage4(i)
                sp.dma_start(yb, y_dram.rearrange("(t k) d -> t (k d)", k=TOPK)[bass.ds(t * P, P), :]
                             ).then_inc(y_in[i], 16)
                sp.dma_start(hb, h_dram[bass.ds(t * P, P), :]).then_inc(hb_in[i], 16)

            def store_out(j, i):
                sp.wait_ge(o_ready[i], j + 1)
                sp.dma_start(out[0, bass.ds(j * (2 * P) + i * P, P), :], stage4(i)[2]).then_inc(out_stored[i], 16)

            for i in range(2):
                load_y(i, i)
                sp.sem_inc(oslot_free[i], 1)
            with sp.Fori(0, NT // 2 - 1) as j:
                for i in range(2):
                    store_out(j, i)
                    load_y(j * 2 + (i + 2), i)
                    sp.wait_ge(out_stored[i], j * 16 + 16)
                    sp.sem_inc(oslot_free[i], 1)
            for i in range(2):
                store_out(NT // 2 - 1, i)
            for i in range(2):
                sp.wait_ge(out_stored[i], 16 * (NT // 2))

        @block.gpsimd
        def _(pool):
            ch = Chain(pool, pool_c)
            link = ch.link
            g = nc.gpsimd
            link(g.memset(ident[:], 0.0))
            link(g.affine_select(out=ident[:], in_=ident[:], compare_op=ALU.not_equal, fill=1.0, base=0,
                                 pattern=[[-1, P]], channel_multiplier=1))
            link(g.memset(ones[:], 1.0))
            link(g.memset(before[:], 1.0))
            link(g.affine_select(out=before[:], in_=before[:], compare_op=ALU.is_ge, fill=0.0, base=-1,
                                 pattern=[[1, P]], channel_multiplier=-1))
            link(g.memset(keep, 1.0))
            link(g.affine_select(out=keep, in_=keep, compare_op=ALU.is_ge, fill=0.0, base=0,
                                 pattern=[[0, GH], [1, P]], channel_multiplier=-1))
            link(g.memset(keep[0:CH, :, CH:P], 0.0))
            link(g.memset(reset[:], 1.0))
            for c in range(4):
                link(g.memset(reset[:, c * CH:c * CH + 1], 0.0))
            for z in (qz[:], kdz[:], Sm, state, csum[:]):
                link(g.memset(z, 0.0))
            link(g.memset(eps[:], EPS))
            link(g.iota(iotaEi[:], pattern=[[1, E]], base=0, channel_multiplier=0))
            link(g.tensor_copy(iotaE[:], iotaEi[:]))
            link(g.iota(vals[:], pattern=[[P * TOPK, NT], [1, TOPK]], base=0, channel_multiplier=TOPK))
            link(g.memset(sidx[:], EMPTY))
            pool.sem_inc(slot_free, 1)
            pool.sem_inc(const_ready, 1)
            slots = slot_dram.rearrange("(p c) o -> p (c o)", p=P)[:, 0:NCOL]
            g.dma_start(slots, sidx[:]).then_inc(prefill_in, 16)
            pool.wait_ge(wst_evac, 1)
            g.affine_select(out=wsT, in_=wsT, compare_op=ALU.is_ge, fill=0.0, base=0,
                            pattern=[[0, SH], [1, P]], channel_multiplier=-1).then_inc(wst_masked, 1)
            pool.wait_ge(prefill_in, 16)

            with pool.Fori(0, NT) as t:
                ch.restart()
                pool.wait_ge(slot_ready, t + 1)
                ch.settle()
                link(g.tensor_copy(sslot[:], slot[:]))
                for k in range(TOPK):
                    g.indirect_dma_start(out=slot_dram[:, :], out_offset=bass.IndirectOffsetOnAxis(ap=sslot[:, k:k + 1], axis=0),
                                         in_=vcur[:, k:k + 1], in_offset=None,
                                         bounds_check=P * TPITCH - 1, oob_is_err=False).then_inc(scattered[k], 16)
                for k in range(TOPK):
                    pool.wait_ge(scattered[k], t * 16 + 16)
                pool.sem_inc(slot_free, 1)

            g.dma_start(sidx[:], slots).then_inc(table_in, 16)
            pool.wait_ge(gidx_ready, 1)
            pool.wait_ge(cnt_ready, 1)
            pool.wait_ge(n2_stored, 16 * NT)
            pool.wait_ge(mix_done, NT)

            def gather(col):
                link(g.tensor_copy(gcur[:], gidx[:, bass.ds(col, BLK)]))
                for b in range(BLK):
                    g.indirect_dma_start(out=xg[:, b, :], out_offset=None, in_=n2_dram[:, :],
                                         in_offset=bass.IndirectOffsetOnAxis(ap=gcur[:, b:b + 1], axis=0),
                                         bounds_check=T - 1, oob_is_err=False).then_inc(xg_in[b], 16)

            def scatter(col, m):
                link(g.tensor_copy(scol[:], sidx[:, bass.ds(col, BLK)]))
                pool.wait_ge(yo_ready, m * BLK + (BLK + 1))
                ch.settle()
                link(g.tensor_copy(scur[:], scol[:]))
                for b in range(BLK):
                    g.indirect_dma_start(out=y_dram[:, :], out_offset=bass.IndirectOffsetOnAxis(ap=scur[:, b:b + 1], axis=0),
                                         in_=yo[:, b, :], in_offset=None,
                                         bounds_check=T * TOPK - 1, oob_is_err=False).then_inc(y_stored[b], 16)
                for b in range(BLK):
                    pool.wait_ge(y_stored[b], m * 16 + 16)
                pool.sem_inc(yo_free, 1)

            ch.restart()
            link(g.memset(xg, 0.0))
            gather(0)
            pool.sem_inc(yo_free, 1)
            with pool.Fori(0, E) as e:
                ch.restart()
                pool.wait_ge(xgt_done, e * (2 * BLK) + 2 * BLK)
                for b in range(BLK):
                    pool.wait_ge(xg_in[b], e * 16 + 16)
                ch.settle()
                gather(e * COLS + COLS)
                scatter(e * COLS, e)

            def again(e, c, nth, left):
                ch.restart()
                pool.wait_ge(xgt_done, nth * (2 * BLK) + (E + 1) * 2 * BLK)
                for b in range(BLK):
                    pool.wait_ge(xg_in[b], nth * 16 + (E + 1) * 16)
                ch.settle()
                gather(e * COLS + c * BLK)
                scatter(e * COLS + c * BLK, nth + E)

            overflow(pool, again)
            for b in range(BLK):
                pool.wait_ge(xg_in[b], 16 * (E + 1))
            pool.sem_inc(moe_done, 1)

        @block.tensor
        def _(pe):
            mm, tr = nc.tensor.matmul, nc.tensor.transpose

            def four(bank, src, k0=0):
                for k in range(4):
                    last = tr(bank[:, k * P:(k + 1) * P], src(k0 + k), ident[:])
                return last

            def by_k(buf):
                v = buf.rearrange("p (q k) -> p k q", k=KD)
                return lambda k: v[:, k, :]

            def ada_piece(n):
                pe.wait_ge(ada_in[n % 2], 16 * (n // 2 + 1))
                if n >= 2:
                    pe.wait_ge(ada_evac, n - 1)
                bank = (R0, R1)[n % 2]
                for k in range(KD):
                    last = mm(bank[:, :], cbc[:, k, :], ada[n % 2][:, k, :], start=(k == 0), stop=(k == KD - 1))
                last.then_inc(ada_done, 1)

            def project_rows(bank, lo, done):
                for k in range(KD):
                    last = mm(bank[:, :], nT[:, k, :], w_in[:, k, lo:lo + 512], start=(k == 0), stop=(k == KD - 1))
                last.then_inc(done, 1)

            def project_T():
                for j in range(4):
                    for k in range(KD):
                        last = mm(QK[:, j * P:(j + 1) * P], w_in[:, k, D + j * P:D + (j + 1) * P], nT[:, k, :],
                                  start=(k == 0), stop=(k == KD - 1))
                last.then_inc(qk_done, 1)
                for k in range(KD):
                    last = mm(ZB[0:RANK, 0:P], w_in[:, k, DIN - RANK:DIN], nT[:, k, :], start=(k == 0), stop=(k == KD - 1))
                last.then_inc(glow_done, 1)

            def transpose_x(t):
                pe.wait_ge(xn_ready, t + 1)
                four(T0, by_k(xn[:]))
                four(T1, by_k(xn[:]), 4).then_inc(xt_done, 1)

            pe.wait_ge(const_ready, 1)
            pe.wait_ge(const_in, 16 * N_CONST)
            four(T0, lambda k: nT[:, k, :])
            four(T1, lambda k: nT[:, k, :], 4).then_inc(wst_done, 1)
            pe.wait_ge(wst_evac, 1)
            tr(T0[:, 0:SH], xn[0:SH, 0:P], ident[0:SH, 0:SH])
            tr(T0[:, 16:18], xn[0:2, P:2 * P], ident[0:2, 0:2])
            for k in range(KD):
                tr(T0[:, 64 + k * E:64 + (k + 1) * E], cat[0:E, k * P:(k + 1) * P], ident[0:E, 0:E])
            for k in range(KD):
                last = tr(T1[:, 64 + k * E:64 + (k + 1) * E], xh[0:E, 1, k * P:(k + 1) * P], ident[0:E, 0:E])
            last.then_inc(wst_done, 1)
            pe.wait_ge(cbc_ready, 1)
            for n in range(EARLY):
                ada_piece(n)
            pe.wait_ge(ada_evac, EARLY)
            for q in range(2):
                for k in range(KD):
                    last = mm(SG[:, q * KD + k:q * KD + k + 1],
                              adarow[0:1, q, :].rearrange("p (q k) -> p k q", k=KD)[:, k, :], ones[0:1, 0:1],
                              start=True, stop=True)
            last.then_inc(adat_done, 1)
            transpose_x(0)
            pe.wait_ge(nT_ready, 1)
            pe.wait_ge(win_in[0], 16)
            project_rows(OB, 0, u_done)
            project_rows(T1, 512, v_done)
            pe.wait_ge(win_in[1], 16)
            pe.wait_ge(gu_ready, 1)
            project_rows(OB, 1536, vv_done)
            pe.wait_ge(gv_ready, 1)
            project_rows(T1, 2048, r_done)
            project_T()
            for n in range(EARLY, len(ADA)):
                ada_piece(n)
            pe.wait_ge(mods_ready, 1)
            pe.wait_ge(wst_masked, 1)
            pe.wait_ge(vv_ready, 1)
            pe.wait_ge(sr_ready, 1)
            pe.wait_ge(wout_in, 16)

            def tile(t, more):
                def value(h):
                    return rows[:, bass.ds(t % 2, 1), 2, h * GV:(h + 1) * GV].rearrange("p a n -> p (a n)")

                pe.wait_ge(gl_ready, t + 1)
                for j in range(2):
                    last = mm(ZB[:, P + j * P:P + (j + 1) * P], wgk[:, j * P:(j + 1) * P], glT[:], start=True, stop=True)
                last.then_inc(z_done, 1)
                if more:
                    transpose_x(t + 1)
                    pe.wait_ge(nT_ready, t + 2)
                    project_rows(R0, 0, u_done)
                pe.wait_ge(qks_ready, t + 1)
                for j in range(2):
                    last = tr(T0[:, j * P:(j + 1) * P], kdT[:, j, :], ident[:])
                last.then_inc(kdt_done, 1)
                for h in range(GH):
                    last = mm(OB[:, h * P:(h + 1) * P], ks[:, h // 2, :], qz[:, h % 2, h // 2, :], start=True, stop=True)
                last.then_inc(s_done, 1)
                if more:
                    project_rows(R1, 512, v_done)
                pe.wait_ge(kdz_ready, t + 1)
                for c, bank in ((0, T1), (1, ZB)):
                    for h in range(GH):
                        last = mm(bank[:, h * P:(h + 1) * P], kdz[:, c, (h // 2) * P:(h // 2 + 1) * P],
                                  value(h), start=True, stop=True)
                last.then_inc(ds_done, 1)
                pe.wait_ge(vh_ready, t + 1)
                for h in range(SH):
                    last = mm(SG[:, h * SHD:(h + 1) * SHD], wsT[:, h, :],
                              rows[:, bass.ds(t % 2, 1), 1, h * SHD:(h + 1) * SHD].rearrange("p a n -> p (a n)"),
                              start=True, stop=True)
                last.then_inc(sgu_done, 1)
                pe.wait_ge(sm_ready, t + 1)
                pe.wait_ge(st1_ready, t + 1)
                for h in range(GH):
                    mm(QK[:, h * GV:(h + 1) * GV], Sm[:, h, :], value(h), start=True, stop=False, skip_group_check=True)
                    for c in range(2):
                        last = mm(QK[c * CH:(c + 1) * CH, h * GV:(h + 1) * GV], qz[:, h % 2, h // 2, c * CH:(c + 1) * CH],
                                  state[:, c, h // 2, :], start=False, stop=(c == 1), skip_group_check=True)
                last.then_inc(o_done, 1)
                if more:
                    pe.wait_ge(gu_ready, t + 2)
                    project_rows(R0, 1536, vv_done)
                pe.wait_ge(cat_ready, t + 1)
                four(T0, lambda k: cat[:, k * P:(k + 1) * P])
                four(T1, lambda k: cat[:, k * P:(k + 1) * P], 4).then_inc(catt_done, 1)
                if more:
                    pe.wait_ge(gv_ready, t + 2)
                    project_rows(R1, 2048, r_done)
                    pe.wait_ge(vv_ready, t + 2)
                    pe.wait_ge(sr_ready, t + 2)
                pe.wait_ge(catT_ready, t + 1)
                for j, bank in ((0, R0), (1, R1)):
                    for k in range(KD):
                        last = mm(bank[:, :], catT[:, k, :], w_out[:, k, j * 512:(j + 1) * 512], start=(k == 0), stop=(k == KD - 1))
                last.then_inc(mix_done, 1)
                if more:
                    pe.wait_ge(st0_ready, t + 1)
                    project_T()
                pe.wait_ge(n2_ready, t + 1)
                four(T0, by_k(xn[:]))
                four(T1, by_k(xn[:]), 4).then_inc(n2t_done, 1)
                pe.wait_ge(n2T_ready, t + 1)
                for k in range(KD):
                    last = mm(OB[:, 0:E], nT[:, k, :], wr[:, k, :], start=(k == 0), stop=(k == KD - 1))
                last.then_inc(lg_done, 1)
                pe.wait_ge(chosen_ready, t + 1)
                mm(OB[:, E:2 * E], before[:], chosen[:], start=True, stop=False)
                mm(OB[:, E:2 * E], ones[:], csum[:], start=False, stop=True).then_inc(cum_done, 1)

            with pe.Fori(0, NT - 1) as t:
                tile(t, True)
            tile(NT - 1, False)
            pe.wait_ge(slot_ready, NT)
            mm(OB[:, 0:E], ones[:], csum[:], start=True, stop=True).then_inc(cnt_done, 1)

            def transpose_rows(m, cnt):
                for b in range(BLK):
                    if b == 2:
                        pe.wait_ge(xTa, m * BLK + 1)
                        pe.wait_ge(xTd, m * BLK + 1)

                    def full():
                        pe.wait_ge(xg_in[b], m * 16 + 16)
                        for half in range(2):
                            four(TD[(2 * b + half) % 4], by_k(xg[:, b, :]), 4 * half).then_inc(xgt_done, 1)

                    if b == 0:
                        full()
                    else:
                        with pe.If(cnt > b * P):
                            full()
                        with pe.Else():
                            for half in range(2):
                                mm(TD[(2 * b + half) % 4][:, 0:64], ident[:], ident[:, 0:64], start=True, stop=True
                                   ).then_inc(xgt_done, 1)

            def gate_up(m, width):
                for f in range(KD):
                    s = f // 4 * 2
                    if f % 4 == 0:
                        pe.wait_ge(piece_in[s], m * 16 + 16)
                        pe.wait_ge(piece_in[s + 1], m * 16 + 16)
                    pe.wait_ge(gup_free, m * KD + (f + 1))
                    for piece, bank in ((pieces[s], ps[f % 2]), (pieces[s + 1], ps[2 + f % 2])):
                        w = piece.rearrange("p (k f) -> p k f", k=KD)
                        for k in range(KD):
                            last = mm(bank[:, 0:width], w[:, k, (f % 4) * P:(f % 4 + 1) * P], xT[:, k, 0:width],
                                      start=(k == 0), stop=(k == KD - 1))
                    last.then_inc(gup_done, 1)

            def gate_up_by_count(m, cnt, widths=WIDTHS):
                if len(widths) == 1:
                    gate_up(m, widths[0])
                else:
                    mid = len(widths) // 2
                    with pe.If(cnt <= widths[mid - 1]):
                        gate_up_by_count(m, cnt, widths[:mid])
                    with pe.Else():
                        gate_up_by_count(m, cnt, widths[mid:])

            def down(m, cnt):
                for b in range(BLK):
                    lo, hi = (TD[2], TD[3]) if b % 2 == 0 else (TD[0], TD[1])
                    if b == 0:
                        pe.wait_ge(piece_in[4], m * 16 + 16)
                        pe.wait_ge(piece_in[5], m * 16 + 16)
                        pe.wait_ge(xTa, m * BLK + (BLK + 2))
                        pe.wait_ge(xTd, m * BLK + (BLK + 2))
                    if b == 1:
                        pe.wait_ge(xTa, m * BLK + (BLK + 3))
                        pe.wait_ge(xTd, m * BLK + (BLK + 3))

                    def full():
                        if b == 2:
                            pe.wait_ge(yo_ready, m * BLK + 2)
                        for t in range(KD):
                            if b == 0:
                                pe.wait_ge(hid_ready, m * KD + (t + 1))
                            w = pieces[4 + t // 4].rearrange("p (k f) -> p k f", k=4)
                            for j, bank in ((0, lo), (1, hi)):
                                last = mm(bank[:, :], hT[:, t, b * P:(b + 1) * P], w[:, t % 4, j * 512:(j + 1) * 512],
                                          start=(t == 0), stop=(t == KD - 1))
                        last.then_inc(down_done, 1)

                    if b == 0:
                        full()
                    else:
                        with pe.If(cnt > b * P):
                            full()
                        with pe.Else():
                            mm(ps[0][:, 0:64], ident[:], ident[:, 0:64], start=True, stop=True).then_inc(down_done, 1)

            def one_pass(m, cnt, following):
                pe.wait_ge(xTa, m * BLK + BLK)
                pe.wait_ge(xTd, m * BLK + BLK)
                gate_up_by_count(m, cnt)
                pe.wait_ge(yo_ready, m * BLK + 1)
                transpose_rows(m + 1, following)
                down(m, cnt)

            pe.wait_ge(cnt_ready, 1)
            pe.wait_ge(psum_init, 1)
            transpose_rows(0, pe.value_load(cnti[0:1, 0:1], min_val=0, max_val=T))
            with pe.Fori(0, E) as e:
                cnt = pe.value_load(cnti[0:1, bass.ds(e, 1)], min_val=0, max_val=T)
                following = pe.value_load(cnti[0:1, bass.ds(e + 1, 1)], min_val=0, max_val=T)
                one_pass(e, cnt, following)

            def again(e, c, nth, left):
                pe.wait_ge(yo_ready, nth * BLK + (E * BLK + 1))
                transpose_rows(nth + (E + 1), left)
                pe.wait_ge(xTa, nth * BLK + (E + 2) * BLK)
                pe.wait_ge(xTd, nth * BLK + (E + 2) * BLK)
                gate_up_by_count(nth + E, left)
                down(nth + E, left)

            overflow(pe, again)

            with pe.Fori(0, NT) as t:
                pe.wait_ge(wcur_ready, t + 1)
                tr(T0[0:E, 0:P], wcur[:], ident[:]).then_inc(wdt_done, 1)
                pe.wait_ge(wdT_ready, t + 1)
                for j, bank in ((0, R0), (1, R1)):
                    last = mm(bank[:, :], wdT[:], bdown[:, j * 512:(j + 1) * 512], start=True, stop=True)
                last.then_inc(bias_done, 1)

        @block.scalar
        def _(act):
            ch = Chain(act, act_c)
            link = ch.link
            A = nc.scalar.activation

            def rstd(dst, src, n, done):
                link(A(dst, src, ACT.Ln, bias=eps[:, 0:1], scale=1.0 / n))
                A(dst, dst, ACT.Exp, scale=-0.5).then_inc(done, 1)

            def x_stats_next(t):
                act.wait_ge(n2_free, t + 1)
                link(A(xn[:], xrow(t + 1), ACT.Square, accum_out=xs[:, 0:1]))
                rstd(xs[:, 1:2], xs[:, 0:1], D, xstat)

            def gelu_uv(t, u, v):
                act.wait_ge(u_done, t + 1)
                A(rowbuf(t, 0), u[:, :], ACT.Gelu_apprx_tanh).then_inc(gu_ready, 1)
                act.wait_ge(v_done, t + 1)
                A(rowbuf(t, 1), v[:, :], ACT.Gelu_apprx_tanh).then_inc(gv_ready, 1)

            def v_rstd(t):
                act.wait_ge(vsum_ready, t + 1)
                rstd(vs[:, 1, :], vs[:, 0, :], SHD, vrstd_ready)

            def copy_value(t, bank):
                act.wait_ge(vv_done, t + 1)
                A(rowbuf(t, 2), bank[:, :], ACT.Copy).then_inc(vv_ready, 1)

            def silu_r(t, bank):
                act.wait_ge(r_done, t + 1)
                A(rowbuf(t, 3), bank[:, :], ACT.Silu).then_inc(sr_ready, 1)

            def copy_glow(t):
                act.wait_ge(glow_done, t + 1)
                A(glT[:], ZB[0:RANK, 0:P], ACT.Copy).then_inc(gl_ready, 1)

            act.sem_inc(yo_ready, 1)
            act.wait_ge(const_ready, 1)
            act.wait_ge(c_in, 16)
            A(siluc[:], ccol[:], ACT.Silu).then_inc(silu_ready, 1)
            act.wait_ge(x_loaded, 16)
            act.wait_ge(wst_evac, 2)
            link(A(xn[:], xrow(0), ACT.Square, accum_out=xs[:, 0:1]))
            rstd(xs[:, 1:2], xs[:, 0:1], D, xstat)
            gelu_uv(0, OB, T1)
            v_rstd(0)
            copy_value(0, OB)
            silu_r(0, T1)
            copy_glow(0)
            act.wait_ge(mods_ready, 1)

            def tile(t, more):
                ch.restart()
                if more:
                    act.wait_ge(x_loaded, t * 16 + 32)
                    act.wait_ge(xt_done, t + 1)
                    x_stats_next(t)
                act.wait_ge(z_ready, t + 1)
                link(A(az, zb, ACT.Abs))
                link(A(az, az, ACT.Exp, scale=-1.0))
                A(az, az, ACT.Ln, bias=1.0).then_inc(lnz_ready, 1)
                act.wait_ge(bc_ready, t + 1)
                A(eb[:], bc[:], ACT.Exp, scale=1.0 / 16)
                A(enb[:], bc[:], ACT.Exp, scale=-1.0 / 16)
                A(dec[:], zb, ACT.Exp, scale=-1.0 / 16).then_inc(exp_ready, 1)
                if more:
                    gelu_uv(t + 1, R0, R1)
                act.wait_ge(o_done, t + 1)
                A(osq[:], QK[:, :], ACT.Square).then_inc(osq_ready, 1)
                act.wait_ge(osum_ready, t + 1)
                rstd(os_[:, 1, :], os_[:, 0, :], GV, orstd_ready)
                if more:
                    v_rstd(t + 1)
                    copy_value(t + 1, R0)
                    silu_r(t + 1, R1)
                act.wait_ge(mix_done, t + 1)
                link(A(osq[:], R0[:, :], ACT.Square, accum_out=ms[:, 0:1]))
                link(A(osq[:], R1[:, :], ACT.Square, accum_out=ms[:, 1:2]))
                link(A(ms[:, 2:3], ms[:, 0:1], ACT.Identity, bias=ms[:, 1:2]))
                rstd(ms[:, 3:4], ms[:, 2:3], D, mstat)
                if more:
                    copy_glow(t + 1)
                act.wait_ge(h_ready, t + 1)
                link(A(cat[:], xrow(t), ACT.Square, accum_out=ms[:, 4:5]))
                rstd(ms[:, 5:6], ms[:, 4:5], D, hstat)
                act.wait_ge(dif_ready, t + 1)
                A(ex4[:], dif4[:], ACT.Exp, accum_out=exsum[:, 0:1]).then_inc(ex_ready, 1)

            with act.Fori(0, NT - 1) as t:
                tile(t, True)
            tile(NT - 1, False)

            def fills(m):
                for b in range(BLK):
                    act.wait_ge(xgt_done, m * (2 * BLK) + (2 * b + 1))
                    A(xT[:, 0:4, b * P:(b + 1) * P], TD[2 * b % 4][:, :].rearrange("p (k n) -> p k n", k=4),
                      ACT.Copy).then_inc(xTa, 1)

            def sigmoids(m):
                for f in range(KD):
                    act.wait_ge(g_ready, m * KD + (f + 1))
                    A(s_sb[:, f % 2, :], g_sb[:, f % 2, :], ACT.Sigmoid, scale=ALPHA).then_inc(sig_ready, 1)

            def down_rows(m):
                act.wait_ge(yo_free, m + 1)
                for b in range(BLK):
                    lo, hi = (TD[2], TD[3]) if b % 2 == 0 else (TD[0], TD[1])
                    act.wait_ge(down_done, m * BLK + (b + 1))
                    A(yo[:, b, 0:512], lo[:, :], ACT.Copy)
                    A(yo[:, b, 512:D], hi[:, :], ACT.Copy).then_inc(yo_ready, 1)

            act.wait_ge(cnt_ready, 1)
            act.wait_ge(psum_init, 1)
            fills(0)
            with act.Fori(0, E) as e:
                sigmoids(e)
                fills(e + 1)
                down_rows(e)

            def again(e, c, nth, left):
                fills(nth + (E + 1))
                sigmoids(nth + E)
                down_rows(nth + E)

            overflow(act, again)

            with act.Fori(0, NT) as t:
                ch.restart()
                act.wait_ge(f_ready, t + 1)
                fb = W[:, bass.ds((t % 2) * 6144, D)]
                link(A(junk4, fb, ACT.Square, accum_out=ms[:, 0:1]))
                rstd(ms[:, 1:2], ms[:, 0:1], D, fstat)

        @block.vector
        def _(dve):
            ch = Chain(dve, dve_c)
            link = ch.link
            v = nc.vector

            def b3(src, n):
                return src.unsqueeze(2).broadcast_to((P, src.shape[1], n))

            def normed_x(t):
                dve.wait_ge(xstat, t + 1)
                v.tensor_scalar(xn[:], xrow(t), xs[:, 1:2], None, ALU.mult).then_inc(xn_ready, 1)

            def modulate(t):
                dve.wait_ge(xt_done, t + 1)
                for k in range(KD):
                    bank = (T0, T1)[k // 4]
                    last = v.tensor_scalar(nT[:, k, :], bank[:, (k % 4) * P:(k % 4 + 1) * P], A1[:, k:k + 1], B1[:, k:k + 1],
                                           ALU.mult, ALU.add)
                last.then_inc(nT_ready, 1)

            def v_squares(t):
                dve.wait_ge(gv_ready, t + 1)
                link(v.tensor_tensor(vsq, rowbuf(t, 1), rowbuf(t, 1), ALU.mult))
                v.tensor_reduce(vs[:, 0, :], vsq.rearrange("p (h d) -> p h d", h=SH), AX_X, ALU.add).then_inc(vsum_ready, 1)

            def v_norm(t):
                dve.wait_ge(vrstd_ready, t + 1)
                r = rowbuf(t, 1)
                r3 = r.rearrange("p (h d) -> p h d", h=SH)
                link(v.tensor_tensor(r3, r3, b3(vs[:, 1, :], SHD), ALU.mult))
                v.tensor_tensor(r, r, gv_row[:], ALU.mult).then_inc(vh_ready, 1)

            def decay_state(src, dst, bank, at):
                for h in range(GH):
                    lo, j = (h % 2) * DK, h // 2
                    last = v.scalar_tensor_tensor(out=state[lo:lo + DK, dst, j, :], in0=state[lo:lo + DK, src, j, :],
                                                  scalar=eb[lo:lo + DK, j, at:at + 1], in1=bank[lo:lo + DK, h * P:(h + 1) * P],
                                                  op0=ALU.mult, op1=ALU.add)
                return last

            dve.wait_ge(const_ready, 1)
            dve.wait_ge(silu_ready, 1)
            v.tensor_copy(cbc, b3(siluc[:], P)).then_inc(cbc_ready, 1)
            dve.wait_ge(wst_done, 1)
            link(v.tensor_copy(wsT[:, 0:4, :], T0[:, :].rearrange("p (k n) -> p k n", k=4)))
            v.tensor_copy(wsT[:, 4:8, :], T1[:, :].rearrange("p (k n) -> p k n", k=4)).then_inc(wst_evac, 1)
            dve.wait_ge(wst_done, 2)
            link(v.tensor_copy(bsT[:], T0[:, 0:SH]))
            link(v.tensor_copy(bgkT[:], T0[:, 16:18]))
            link(v.tensor_copy(bgT[:], T0[:, 64:64 + KD * E].rearrange("p (k e) -> p e k", k=KD)))
            v.tensor_scalar(buT[:], T1[:, 64:64 + KD * E].rearrange("p (k e) -> p e k", k=KD), 1.0, None,
                            ALU.add).then_inc(wst_evac, 1)
            for n in range(EARLY):
                dve.wait_ge(ada_done, n + 1)
                v.tensor_copy(adarow[0:1, n // 2, (n % 2) * 512:(n % 2 + 1) * 512], (R0, R1)[n % 2][0:1, :]).then_inc(ada_evac, 1)
            dve.wait_ge(adat_done, 1)
            link(v.tensor_tensor(A1[:], SG[:, 0:KD], badac[:, 1, :], ALU.add))
            link(v.scalar_tensor_tensor(out=A1[:], in0=A1[:], scalar=1.0, in1=gpre[:], op0=ALU.add, op1=ALU.mult))
            link(v.tensor_tensor(B1[:], SG[:, KD:2 * KD], badac[:, 0, :], ALU.add))
            normed_x(0)
            modulate(0)
            v_squares(0)
            v_norm(0)
            for n in range(EARLY, len(ADA)):
                m, half = ADA[n]
                cols = slice(half * 512, (half + 1) * 512)
                bank = (R0, R1)[n % 2][:, :]
                dve.wait_ge(ada_done, n + 1)
                if m == 5:
                    v.tensor_copy((osq, vsq)[half][0:1, :], bank[0:1, :]).then_inc(ada_evac, 1)
                    continue
                dst = {2: gate1, 3: B2, 4: A2}[m][:, cols]
                v.tensor_tensor(dst, bank, dst, ALU.add).then_inc(ada_evac, 1)
                dve.wait_ge(ada_evac, n + 1)
                if m == 2:
                    link(v.tensor_tensor(dst, dst, gprow[:, cols], ALU.mult))
                if m == 4:
                    link(v.scalar_tensor_tensor(out=dst, in0=dst, scalar=1.0, in1=g2row[:, cols], op0=ALU.add, op1=ALU.mult))
            dve.wait_ge(gate2_stored, 32)
            dve.sem_inc(mods_ready, 1)

            def tile(t, more):
                ch.restart()
                dve.wait_ge(z_done, t + 1)
                for j in range(2):
                    last = v.tensor_scalar(zb[:, j, :], ZB[:, P + j * P:P + (j + 1) * P], bgkT[:, j:j + 1], None, ALU.add)
                last.then_inc(z_ready, 1)
                if more:
                    normed_x(t + 1)
                dve.wait_ge(lnz_ready, t + 1)
                link(v.scalar_tensor_tensor(out=zb, in0=zb, scalar=0.0, in1=az, op0=ALU.min, op1=ALU.subtract))
                link(v.tensor_tensor_scan(bc[:].rearrange("p a n -> p (a n)"), reset[:], zb.rearrange("p a n -> p (a n)"),
                                          0.0, ALU.mult, ALU.add))
                bc4 = bc[:].rearrange("p a (c n) -> p (a c) n", c=2)
                v.tensor_tensor(zb.rearrange("p a (c n) -> p (a c) n", c=2), bc4,
                                bc4[:, :, CH - 1:CH].broadcast_to((P, 4, CH)), ALU.subtract).then_inc(bc_ready, 1)
                if more:
                    modulate(t + 1)
                dve.wait_ge(exp_ready, t + 1)
                q = QK[:, 0:2 * P].rearrange("p (a n) -> p a n", a=2)
                k = QK[:, 2 * P:4 * P].rearrange("p (a n) -> p a n", a=2)
                for h in range(2):
                    lo = h * DK
                    v.scalar_tensor_tensor(out=qz[lo:lo + DK, h, :, :], in0=q[lo:lo + DK], scalar=DK ** -0.5,
                                           in1=eb[lo:lo + DK, :, :], op0=ALU.mult, op1=ALU.mult)
                v.tensor_tensor(ks[:], k, enb[:], ALU.mult)
                v.tensor_tensor(kdT, k, dec[:], ALU.mult).then_inc(qks_ready, 1)
                dve.wait_ge(kdt_done, t + 1)
                for c in range(2):
                    last = v.tensor_copy(kdz[c * CH:(c + 1) * CH, c, :], T0[c * CH:(c + 1) * CH, 0:2 * P])
                last.then_inc(kdz_ready, 1)
                dve.wait_ge(s_done, t + 1)
                ch.settle()
                v.copy_predicated(Sm, keep.bitcast(I32), OB[:, :].rearrange("p (h n) -> p h n", h=GH)).then_inc(sm_ready, 1)
                dve.wait_ge(ds_done, t + 1)
                decay_state(0, 1, T1, CH - 1).then_inc(st1_ready, 1)
                dve.wait_ge(sgu_done, t + 1)
                c3 = cat[:, 0:DS].rearrange("p (h d) -> p h d", h=SH)
                link(v.tensor_tensor(c3, SG[:, :].rearrange("p (h d) -> p h d", h=SH), b3(bsT[:], SHD), ALU.add))
                v.tensor_tensor(cat[:, 0:DS], cat[:, 0:DS], rowbuf(t, 0), ALU.mult)
                if more:
                    v_squares(t + 1)
                dve.wait_ge(osq_ready, t + 1)
                v.tensor_reduce(os_[:, 0, :], osq[:].rearrange("p (h d) -> p h d", h=GH), AX_X, ALU.add).then_inc(osum_ready, 1)
                dve.wait_ge(st1_ready, t + 1)
                decay_state(1, 0, ZB, P - 1).then_inc(st0_ready, 1)
                dve.wait_ge(orstd_ready, t + 1)
                o3 = cat[:, DS:D].rearrange("p (h d) -> p h d", h=GH)
                link(v.tensor_tensor(o3, QK[:, :].rearrange("p (h d) -> p h d", h=GH), b3(os_[:, 1, :], GV), ALU.mult))
                link(v.tensor_tensor(o3, o3, go_row[:].unsqueeze(1).broadcast_to((P, GH, GV)), ALU.mult))
                v.tensor_tensor(cat[:, DS:D], cat[:, DS:D], rowbuf(t, 3), ALU.mult).then_inc(cat_ready, 1)
                if more:
                    v_norm(t + 1)
                dve.wait_ge(catt_done, t + 1)
                v.tensor_copy(catT[:, 0:4, :], T0[:, :].rearrange("p (k n) -> p k n", k=4))
                v.tensor_copy(catT[:, 4:8, :], T1[:, :].rearrange("p (k n) -> p k n", k=4)).then_inc(catT_ready, 1)
                dve.wait_ge(mstat, t + 1)
                for j, bank in ((0, R0), (1, R1)):
                    link(v.scalar_tensor_tensor(out=cat[:, j * 512:(j + 1) * 512], in0=bank[:, :], scalar=ms[:, 3:4],
                                                in1=gate1[:, j * 512:(j + 1) * 512], op0=ALU.mult, op1=ALU.mult))
                v.tensor_tensor(xrow(t), xrow(t), cat[:], ALU.add).then_inc(h_ready, 1)
                dve.wait_ge(hstat, t + 1)
                if more:
                    dve.wait_ge(xt_done, t + 2)
                else:
                    dve.wait_ge(n2_free, t + 1)
                link(v.scalar_tensor_tensor(out=xn[:], in0=xrow(t), scalar=ms[:, 5:6], in1=A2[:], op0=ALU.mult, op1=ALU.mult))
                v.tensor_tensor(xn[:], xn[:], B2[:], ALU.add).then_inc(n2_ready, 1)
                dve.wait_ge(n2t_done, t + 1)
                v.tensor_copy(nT[:, 0:4, :], T0[:, :].rearrange("p (k n) -> p k n", k=4))
                v.tensor_copy(nT[:, 4:8, :], T1[:, :].rearrange("p (k n) -> p k n", k=4)).then_inc(n2T_ready, 1)
                dve.wait_ge(lg_done, t + 1)
                link(v.tensor_tensor(lg[:], OB[:, 0:E], br[:], ALU.add))
                link(v.max(top8[:], lg[:]))
                link(v.max_index(ti8[:], top8[:], lg[:]))
                link(v.tensor_copy(tif[:], ti8[:, 0:TOPK]))
                link(v.tensor_tensor(oneh[:], iotaE[:].unsqueeze(1).broadcast_to((P, TOPK, E)), b3(tif[:], E), ALU.is_equal))
                v.tensor_reduce(chosen[:], oneh[:].rearrange("p k e -> p e k"), AX_X, ALU.add).then_inc(chosen_ready, 1)
                v.tensor_scalar(dif4[:], top8[:, 0:TOPK], top8[:, 0:1], None, ALU.subtract).then_inc(dif_ready, 1)
                dve.wait_ge(ex_ready, t + 1)
                link(v.reciprocal(exsum[:, 1:2], exsum[:, 0:1]))
                pr = probs[:, bass.ds(t, 1), :].rearrange("p a k -> p (a k)")
                link(v.tensor_scalar(pcur[:], ex4[:], exsum[:, 1:2], None, ALU.mult))
                v.tensor_copy(pr, pcur[:])
                link(v.tensor_tensor(tmpk[:], oneh[:], b3(pcur[:], E), ALU.mult))
                link(v.tensor_reduce(wden[:, bass.ds(t, 1), :].rearrange("p a e -> p (a e)"),
                                     tmpk[:].rearrange("p k e -> p e k"), AX_X, ALU.add))
                dve.wait_ge(cum_done, t + 1)
                link(v.tensor_copy(cum[:], OB[:, E:2 * E]))
                link(v.tensor_tensor(csum[:], csum[:], chosen[:], ALU.add))
                link(v.tensor_tensor(tmpk[:], oneh[:], cum[:].unsqueeze(1).broadcast_to((P, TOPK, E)), ALU.mult))
                link(v.tensor_reduce(rank[:], tmpk[:], AX_X, ALU.add))
                link(v.tensor_copy(ranki[:], rank[:]))
                link(v.tensor_scalar(ia[:], ranki[:], P - 1, TPITCH.bit_length() - 1, ALU.bitwise_and, ALU.logical_shift_left))
                link(v.tensor_scalar(ib[:], ranki[:], P.bit_length() - 1, None, ALU.logical_shift_right))
                link(v.tensor_scalar(ic[:], tif[:], float(COLS), None, ALU.mult))
                link(v.tensor_tensor(iab[:], ia[:], ib[:], ALU.add))
                dve.wait_ge(slot_free, t + 1)
                link(v.tensor_copy(vcur[:], vals[:, bass.ds(t, 1), :].rearrange("p a k -> p (a k)")))
                v.tensor_tensor(slot[:], iab[:], ic[:], ALU.add).then_inc(slot_ready, 1)
                dve.wait_ge(slot_ready, t + 1)

            with dve.Fori(0, NT - 1) as t:
                tile(t, True)
            tile(NT - 1, False)

            dve.wait_ge(cnt_done, 1)
            link(v.memset(cnti[:, E:E + 1], 0))
            link(v.tensor_copy(cnti[:, 0:E], OB[0:1, 0:E]))
            for c in range(1, NCHUNK):
                link(v.tensor_scalar(overf[:, 0, (c - 1) * E:c * E], OB[0:1, 0:E], float(-c * CAP), None, ALU.add))
            link(v.tensor_copy(overn[:], overf[:, 0, :]))
            link(v.tensor_scalar(overf[:, 1, :], overf[:, 0, :], 0.0, None, ALU.is_gt))
            link(v.tensor_tensor_scan(overf[:, 2, :], ones[0:1, 0:NOVER], overf[:, 1, :], 0.0, ALU.mult, ALU.add))
            link(v.tensor_copy(overt[:], overf[:, 2, NOVER - 1:NOVER]))
            link(v.tensor_tensor(overf[:, 2, :], overf[:, 2, :], overf[:, 1, :], ALU.subtract))
            v.tensor_copy(overo[:], overf[:, 2, :]).then_inc(cnt_ready, 1)
            dve.wait_ge(table_in, 16)
            v.tensor_scalar(gidx, sidx[:], TOPK.bit_length() - 1, None, ALU.logical_shift_right).then_inc(gidx_ready, 1)
            for bank in ps:
                link(v.memset(bank[:, :], 0.0))
            dve.sem_inc(psum_init, 1)
            dve.sem_inc(gup_free, 2)

            def fills(m):
                for b in range(BLK):
                    dve.wait_ge(xgt_done, m * (2 * BLK) + (2 * b + 2))
                    v.tensor_copy(xT[:, 4:8, b * P:(b + 1) * P], TD[(2 * b + 1) % 4][:, :].rearrange("p (k n) -> p k n", k=4)
                                  ).then_inc(xTd, 1)

            def hidden(m, e):
                ch.restart()
                link(v.tensor_copy(bcur[:, 0, :], bgT[:, bass.ds(e, 1), :].rearrange("p a k -> p (a k)")))
                link(v.tensor_copy(bcur[:, 1, :], buT[:, bass.ds(e, 1), :].rearrange("p a k -> p (a k)")))

                def finish(f):
                    dve.wait_ge(sig_ready, m * KD + (f + 1))
                    link(v.tensor_tensor(g_sb[:, f % 2, :], g_sb[:, f % 2, :], s_sb[:, f % 2, :], ALU.mult))
                    v.scalar_tensor_tensor(out=hT[:, f, :], in0=u_sb[:, f % 2, :], scalar=1.0 - LIMIT, in1=g_sb[:, f % 2, :],
                                           op0=ALU.max, op1=ALU.mult).then_inc(hid_ready, 1)

                for f in range(KD):
                    if f >= 2:
                        dve.wait_ge(hid_ready, m * KD + (f - 1))
                    dve.wait_ge(gup_done, m * KD + (f + 1))
                    v.tensor_scalar(g_sb[:, f % 2, :], ps[f % 2][:, 0:CAP], bcur[:, 0, f:f + 1], LIMIT,
                                    ALU.add, ALU.min).then_inc(g_ready, 1)
                    v.tensor_scalar(u_sb[:, f % 2, :], ps[2 + f % 2][:, 0:CAP], bcur[:, 1, f:f + 1], LIMIT + 1.0,
                                    ALU.add, ALU.min).then_inc(gup_free, 1)
                    if f:
                        finish(f - 1)
                finish(KD - 1)
                dve.wait_ge(hid_ready, m * KD + KD)
                ch.settle()

            fills(0)
            with dve.Fori(0, E) as e:
                hidden(e, e)
                fills(e + 1)

            def again(e, c, nth, left):
                fills(nth + (E + 1))
                hidden(nth + E, e)

            overflow(dve, again)

            dve.wait_ge(g2_in, 64)
            ch.restart()
            link(v.tensor_tensor(gate2, gate2, badarow, ALU.add))
            link(v.tensor_tensor(gate2, gate2, gfrow, ALU.mult))

            with dve.Fori(0, NT // 2) as j:
                for i in range(2):
                    ch.restart()
                    t = j * 2 + i
                    yb, hb, ob = stage4(i)
                    link(v.tensor_copy(pcur[:], probs[:, bass.ds(t, 1), :].rearrange("p a k -> p (a k)")))
                    v.tensor_copy(wcur[:], wden[:, bass.ds(t, 1), :].rearrange("p a e -> p (a e)")).then_inc(wcur_ready, 1)
                    dve.wait_ge(wdt_done, t + 1)
                    v.tensor_copy(wdT[:], T0[0:E, 0:P]).then_inc(wdT_ready, 1)
                    dve.wait_ge(bias_done, t + 1)
                    dve.wait_ge(y_in[i], j * 16 + 16)
                    for c, bank in ((0, R0), (1, R1)):
                        last = v.scalar_tensor_tensor(out=yb[:, c * 512:(c + 1) * 512], in0=yb[:, c * 512:(c + 1) * 512],
                                                      scalar=pcur[:, 0:1], in1=bank[:, :], op0=ALU.mult, op1=ALU.add)
                    link(last)
                    for k in range(1, TOPK):
                        last = v.scalar_tensor_tensor(out=yb[:, 0:D], in0=yb[:, k * D:(k + 1) * D], scalar=pcur[:, k:k + 1],
                                                      in1=yb[:, 0:D], op0=ALU.mult, op1=ALU.add)
                        if k < TOPK - 1:
                            link(last)
                    last.then_inc(f_ready, 1)
                    dve.wait_ge(fstat, t + 1)
                    dve.wait_ge(hb_in[i], j * 16 + 16)
                    link(v.scalar_tensor_tensor(out=yb[:, 0:D], in0=yb[:, 0:D], scalar=ms[:, 1:2], in1=gate2,
                                                op0=ALU.mult, op1=ALU.mult))
                    dve.wait_ge(oslot_free[i], j + 1)
                    v.tensor_tensor(ob, yb[:, 0:D], hb, ALU.add).then_inc(o_ready[i], 1)


def kernel(**inputs):
    import numpy as np
    import concourse.bacc as bacc
    from concourse.bass_utils import run_bass_kernel_spmd as run

    nc = bacc.Bacc("TRN2", target_bir_lowering=False, num_devices=1)
    arrays, aps = {}, {}
    for name in inputs:
        array = np.ascontiguousarray(inputs[name])
        arrays["in_" + name] = array
        aps[name] = nc.dram_tensor("in_" + name, array.shape, mybir.dt.from_np(array.dtype), kind="ExternalInput").ap()
    out = nc.dram_tensor("out_h", (1, T, D), F32, kind="ExternalOutput").ap()
    hybrid_block(nc, aps, out)
    return run(nc, [arrays], core_ids=[0]).results[0]["out_h"]
```

```python
from contextlib import ExitStack

import concourse.bass as bass
from concourse import mybir

F32 = mybir.dt.float32
I32 = mybir.dt.int32
U32 = mybir.dt.uint32
ALU = mybir.AluOpType
ACT = mybir.ActivationFunctionType
AX_X = mybir.AxisListType.X

P = 128
D = 1024
KD = D // P
T = 1024
NT = T // P
DS = 512
SH, SHD = 8, 64
GH, GV = 4, 128
DK = 64
CH = 64
RANK = 16
DIN = 2576
E = 32
TOPK = 4
BLK = 3
CAP = BLK * P
NCHUNK = -(-T // CAP)
COLS = NCHUNK * BLK
TPITCH = 512
NCOL = (E + 1) * COLS
EMPTY = 1 << 20
NOVER = (NCHUNK - 1) * E
WIDTHS = [w for w in range(64, 320, 32) if w < CAP] + [CAP]
NS = 4
LIMIT = 7.0
ALPHA = 1.702
EPS = 1e-6
SPARE = KD * DIN


class Chain:

    def __init__(self, eng, sem):
        self.eng, self.sem, self.n = eng, sem, 0

    def restart(self):
        self.eng.sem_clear(self.sem)
        self.n = 0

    def settle(self):
        self.n += 1
        self.eng.sem_inc(self.sem, 1)
        self.eng.wait_ge(self.sem, self.n)

    def link(self, ins):
        self.n += 1
        ins.then_inc(self.sem, 1)
        self.eng.wait_ge(self.sem, self.n)


def hybrid_block(nc, a, out):
    ctx = ExitStack()
    with ctx:
        def sb(name, shape, dt=F32):
            return ctx.enter_context(nc.sbuf_tensor(name, shape, dt))

        def sem(name):
            return ctx.enter_context(nc.semaphore(name))

        def dram(name, shape, dt=F32):
            return nc.dram_tensor(name, shape, dt, kind="Internal").ap()

        h_dram = dram("h_dram", (T, D))
        n2_dram = dram("n2_dram", (T, D))
        y_dram = dram("y_dram", (T * TOPK, D))
        slot_dram = dram("slot_dram", (P * TPITCH, 1), I32)
        gate2_dram = dram("gate2_dram", (1, D))

        W = sb("W", [P, 6 * 4096])
        WO = sb("WO", [P, 8192])
        BIG = sb("BIG", [P, 6144])
        w_in = W[:, 0:SPARE].rearrange("p (k n) -> p k n", k=KD)
        pieces = [W[:, s * 4096:(s + 1) * 4096] for s in range(6)]
        spare_at = [SPARE]

        def spare(*shape):
            size = 1
            for n in shape:
                size *= n
            lo = spare_at[0]
            spare_at[0] = lo + size
            assert lo + size <= 6 * 4096
            v = W[:, lo:lo + size]
            if len(shape) == 2:
                v = v.rearrange("p (a b) -> p a b", a=shape[0])
            if len(shape) == 3:
                v = v.rearrange("p (a b c) -> p a b c", a=shape[0], b=shape[1])
            return v

        ada = [WO[:, s * 4096:(s + 1) * 4096].rearrange("p (k n) -> p k n", k=KD) for s in range(2)]
        w_out = WO[:, :].rearrange("p (k n) -> p k n", k=KD)
        xg = WO[:, 0:BLK * D].rearrange("p (b d) -> p b d", b=BLK)
        xT = WO[:, BLK * D:2 * BLK * D].rearrange("p (k n) -> p k n", k=KD)
        g_sb = WO[:, 6144:6144 + 2 * CAP].rearrange("p (a n) -> p a n", a=2)
        u_sb = WO[:, 6144 + 2 * CAP:6144 + 4 * CAP].rearrange("p (a n) -> p a n", a=2)
        rows = BIG[:, 0:4096].rearrange("p (a j n) -> p a j n", a=2, j=4)
        adarow = BIG[:, 0:2048].rearrange("p (a n) -> p a n", a=2)
        gprow = BIG[:, 3072:4096]
        nT = BIG[:, 4096:5120].rearrange("p (k n) -> p k n", k=KD)
        catT = BIG[:, 5120:6144].rearrange("p (k n) -> p k n", k=KD)
        cbc = catT
        yo = BIG[:, 0:BLK * D].rearrange("p (b d) -> p b d", b=BLK)
        hT = BIG[:, BLK * D:2 * BLK * D].rearrange("p (k n) -> p k n", k=KD)

        xh = sb("xh", [P, 3, D])
        xn = sb("xn", [P, D])
        hn = sb("hn", [P, D])
        cat = sb("cat", [P, D])
        s_sb = cat[:, 0:2 * CAP].rearrange("p (a n) -> p a n", a=2)
        gate1 = sb("gate1", [P, D])
        gidx = xn[:, 0:NCOL].bitcast(I32)
        wsT = spare(SH, P)
        keep = spare(GH, P)
        vsq = spare(DS)
        Sm = spare(GH, P)
        state = spare(2, 2, P)
        zb = spare(2, P)
        az = spare(2, P)
        kdT = spare(2, P)
        osq = sb("osq", [P, DS])
        glT = sb("glT", [RANK, P])
        wgk = sb("wgk", [RANK, 2 * P])
        bgkT = sb("bgkT", [P, 2])
        bc = sb("bc", [P, 2, P])
        eb = sb("eb", [P, 2, P])
        enb = sb("enb", [P, 2, P])
        dec = sb("dec", [P, 2, P])
        qz = sb("qz", [P, 2, 2, P])
        ks = sb("ks", [P, 2, P])
        kdz = sb("kdz", [P, 2, 2 * P])
        gv_row = sb("gv_row", [P, DS])
        go_row = sb("go_row", [P, GV])
        bsT = sb("bsT", [P, SH])
        wr = sb("wr", [P, KD, E])
        br = sb("br", [P, E])
        ident = sb("ident", [P, P])
        ones = sb("ones", [P, P])
        before = sb("before", [P, P])
        reset = sb("reset", [P, 2 * P])
        ccol = sb("ccol", [P, KD])
        siluc = sb("siluc", [P, KD])
        badac = sb("badac", [P, 4, KD])
        gpre = sb("gpre", [P, 2, KD])
        AB = sb("AB", [P, 4, KD])
        A1, B1, A2, B2 = (AB[:, j, :] for j in range(4))
        eps = sb("eps", [P, 1])
        xs = sb("xs", [P, 4])
        vs = sb("vs", [P, 3, SH])
        os_ = sb("os_", [P, 3, GH])
        ms = sb("ms", [P, 8])
        iotaE = sb("iotaE", [P, E])
        iotaEi = sb("iotaEi", [P, E], I32)
        vals = sb("vals", [P, NT, TOPK], I32)
        vcur = sb("vcur", [P, TOPK], I32)
        lg = sb("lg", [P, E])
        top8 = sb("top8", [P, 8])
        ti8 = sb("ti8", [P, 8], U32)
        tif = sb("tif", [P, TOPK])
        dif4 = sb("dif4", [P, TOPK])
        ex4 = sb("ex4", [P, TOPK])
        exsum = sb("exsum", [P, 2])
        oneh = sb("oneh", [P, TOPK, E])
        tmpk = sb("tmpk", [P, TOPK, E])
        chosen = sb("chosen", [P, E])
        csum = sb("csum", [P, E])
        cum = sb("cum", [P, E])
        rank = sb("rank", [P, TOPK])
        ranki = sb("ranki", [P, TOPK], I32)
        ia = sb("ia", [P, TOPK], I32)
        ib = sb("ib", [P, TOPK], I32)
        ic = sb("ic", [P, TOPK], I32)
        iab = sb("iab", [P, TOPK], I32)
        slot = sb("slot", [P, TOPK], I32)
        sslot = sb("sslot", [P, TOPK], I32)
        probs = sb("probs", [P, NT, TOPK])
        wden = sb("wden", [P, NT, E])
        pcur = sb("pcur", [P, TOPK])
        pcur4 = sb("pcur4", [P, NS * TOPK])
        bgT = sb("bgT", [P, E, KD])
        buT = sb("buT", [P, E, KD])
        bcur = sb("bcur", [P, 2, KD])
        sidx = sb("sidx", [P, NCOL], I32)
        scol = sb("scol", [P, BLK], I32)
        scur = sb("scur", [P, BLK], I32)
        gcur = sb("gcur", [P, BLK], I32)
        cnti = sb("cnti", [1, E + 1], I32)
        overn = sb("overn", [1, NOVER], I32)
        overo = sb("overo", [1, NOVER], I32)
        overf = osq[0:1, 0:3 * NOVER].rearrange("p (a n) -> p a n", a=3)
        overt = sb("overt", [1, 1], I32)

        ps = [ctx.enter_context(nc.psum_tensor(f"ps{i}", [P, 512], F32)) for i in range(8)]
        T0, T1, R0, R1, QK, ZB, SG, OB = ps
        TD = ps[4:8]

        c_in = sem("c_in")
        c2_in = sem("c2_in")
        x_loaded = sem("x_loaded")
        wout_in = sem("wout_in")
        h_stored = sem("h_stored")
        n2_stored = sem("n2_stored")
        pool_c = sem("pool_c")
        dve_c = sem("dve_c")
        sp_c = sem("sp_c")
        act_c = sem("act_c")
        const_ready = sem("const_ready")
        silu_ready = sem("silu_ready")
        cbc_ready = sem("cbc_ready")
        ada_done = sem("ada_done")
        ada_evac = sem("ada_evac")
        adat_done = sem("adat_done")
        gate2_stored = sem("gate2_stored")
        mods_ready = sem("mods_ready")
        wst_done = sem("wst_done")
        wst_evac = sem("wst_evac")
        wst_masked = sem("wst_masked")
        xstat = sem("xstat")
        xn_ready = sem("xn_ready")
        xt_done = sem("xt_done")
        nT_ready = sem("nT_ready")
        u_done = sem("u_done")
        v_done = sem("v_done")
        vv_done = sem("vv_done")
        r_done = sem("r_done")
        qk_done = sem("qk_done")
        glow_done = sem("glow_done")
        gu_ready = sem("gu_ready")
        gv_ready = sem("gv_ready")
        vv_ready = sem("vv_ready")
        sr_ready = sem("sr_ready")
        vsum_ready = sem("vsum_ready")
        vrstd_ready = sem("vrstd_ready")
        vh_ready = sem("vh_ready")
        gl_ready = sem("gl_ready")
        z_done = sem("z_done")
        z_ready = sem("z_ready")
        lnz_ready = sem("lnz_ready")
        bc_ready = sem("bc_ready")
        exp_ready = sem("exp_ready")
        qks_ready = sem("qks_ready")
        kdt_done = sem("kdt_done")
        kdz_ready = sem("kdz_ready")
        s_done = sem("s_done")
        sm_ready = sem("sm_ready")
        ds_done = sem("ds_done")
        st1_ready = sem("st1_ready")
        st0_ready = sem("st0_ready")
        sgu_done = sem("sgu_done")
        o_done = sem("o_done")
        osq_ready = sem("osq_ready")
        osum_ready = sem("osum_ready")
        orstd_ready = sem("orstd_ready")
        cat_ready = sem("cat_ready")
        catt_done = sem("catt_done")
        catTa = sem("catTa")
        catTd = sem("catTd")
        modt_done = sem("modt_done")
        hn_free = sem("hn_free")
        mix_done = sem("mix_done")
        mstat = sem("mstat")
        h_ready = sem("h_ready")
        hstat = sem("hstat")
        n2_ready = sem("n2_ready")
        n2t_done = sem("n2t_done")
        n2T_ready = sem("n2T_ready")
        lg_done = sem("lg_done")
        dif_ready = sem("dif_ready")
        ex_ready = sem("ex_ready")
        chosen_ready = sem("chosen_ready")
        cum_done = sem("cum_done")
        slot_ready = sem("slot_ready")
        slot_free = sem("slot_free")
        cnt_done = sem("cnt_done")
        cnt_ready = sem("cnt_ready")
        table_in = sem("table_in")
        gidx_ready = sem("gidx_ready")
        psum_init = sem("psum_init")
        xgt_done = sem("xgt_done")
        xTa = sem("xTa")
        xTd = sem("xTd")
        gup_done = sem("gup_done")
        gup_free = sem("gup_free")
        g_ready = sem("g_ready")
        sig_ready = sem("sig_ready")
        hid_ready = sem("hid_ready")
        down_done = sem("down_done")
        yo_ready = sem("yo_ready")
        yo_free = sem("yo_free")
        moe_done = sem("moe_done")
        bd_in = sem("bd_in")
        wcur_ready = sem("wcur_ready")
        wdt_done = sem("wdt_done")
        wdT_ready = sem("wdT_ready")
        bias_done = sem("bias_done")
        bias_read = sem("bias_read")
        f_ready = sem("f_ready")
        fstat = sem("fstat")
        g2_in = sem("g2_in")
        g2_ready = sem("g2_ready")
        prefill_in = sem("prefill_in")
        ada_in = [sem(f"ada_in{i}") for i in range(2)]
        win_in = [sem(f"win_in{i}") for i in range(2)]
        scattered = [sem(f"scattered{k}") for k in range(TOPK)]
        piece_in = [sem(f"piece_in{s}") for s in range(6)]
        xg_in = [sem(f"xg_in{b}") for b in range(BLK)]
        y_stored = [sem(f"y_stored{b}") for b in range(BLK)]
        y_in = [sem(f"y_in{i}") for i in range(NS)]
        hb_in = [sem(f"hb_in{i}") for i in range(NS)]
        o_ready = [sem(f"o_ready{i}") for i in range(NS)]
        out_stored = [sem(f"out_stored{i}") for i in range(NS)]
        oslot_free = [sem(f"oslot_free{i}") for i in range(NS)]
        const_in = sem("const_in")
        N_CONST = 16

        ADA = [(m, half) for m in (1, 0, 2, 3, 4, 5) for half in (0, 1)]
        EARLY = 4

        def x_rows(t):
            return a["x"][0, bass.ds(t * P, P), :]

        def xrow(t):
            return xh[:, bass.ds(t % 3, 1), :].rearrange("p a d -> p (a d)")

        def rowbuf(t, j):
            return rows[:, bass.ds(t % 2, 1), j, :].rearrange("p a n -> p (a n)")

        def stage4(i):
            lo = i * 6144
            return W[:, lo:lo + 4096], W[:, lo + 4096:lo + 5120], W[:, lo + 5120:lo + 6144]

        gate2 = gate1[:]
        badarow, gfrow, junk4 = hn[:], xh[:, 0, :], xh[:, 2, :]
        bdown = xh[0:E, 1, :]
        wdT = WO[0:E, 6144:6144 + NS * P]
        wcur = WO[:, 6144 + NS * P:6144 + NS * (P + E)]

        def bias_banks(i):
            return ((R0, R1), (T0, T1))[i % 2]

        def bcast_row(src, n):
            return src.rearrange("(o n) -> o n", o=1).broadcast_to((P, n))

        def overflow(eng, body):
            over = eng.value_load(overt[0:1, 0:1], min_val=0, max_val=NOVER)
            with eng.If(over > 0):
                with eng.Fori(0, NOVER) as j:
                    left = eng.value_load(overn[0:1, bass.ds(j, 1)], min_val=-T, max_val=T)
                    nth = eng.value_load(overo[0:1, bass.ds(j, 1)], min_val=0, max_val=NOVER)
                    with eng.If(left > 0):
                        body(j % E, j // E + 1, nth, left)

        block = ctx.enter_context(nc.Block())

        @block.sync
        def _(sp):
            sp.dma_start(ccol[:], a["c"].rearrange("b (p k) -> p (b k)", k=KD)).then_inc(c_in, 16)
            sp.dma_start(xh[:, 0, :], x_rows(0)).then_inc(x_loaded, 16)
            for dst, src in (
                    (nT, a["w_s"][0].rearrange("h t s -> t h s")),
                    (xn[0:SH, 0:P], a["b_s"][0]),
                    (xn[0:2, P:2 * P], a["b_gk"][0].rearrange("(a p) -> a p", a=2)),
                    (cat[0:E, :], a["b_gate"][0]),
                    (xh[0:E, 1, :], a["b_up"][0]),
                    (badac[:, 0:2, :], a["b_ada"][0, 0:2 * D].rearrange("(m p k) -> p m k", m=2, k=KD)),
                    (badac[:, 2:4, :], a["b_ada"][0, 3 * D:5 * D].rearrange("(m p k) -> p m k", m=2, k=KD)),
                    (gpre[:, 0, :], a["g_pre_mix"][0].rearrange("(p k) -> p k", k=KD)),
                    (gpre[:, 1, :], a["g_pre_ffn"][0].rearrange("(p k) -> p k", k=KD)),
                    (wgk[:], a["w_gk2"][0]),
                    (wr[:], a["w_router"][0].rearrange("(p k) e -> p k e", k=KD)),
                    (gv_row[:], bcast_row(a["g_sgu_v"][0], DS)),
                    (go_row[:], bcast_row(a["g_gla_out"][0], GV)),
                    (br[:], bcast_row(a["b_router"][0], E)),
                    (gate1[:], bcast_row(a["b_ada"][0, 2 * D:3 * D], D)),
                    (gprow, bcast_row(a["g_post_mix"][0], D))):
                sp.dma_start(dst, src).then_inc(const_in, 16)

            w_in_v = a["w_in"][0].rearrange("(p k) n -> p k n", k=KD)
            for n, (m, half) in enumerate(ADA):
                if n == EARLY:
                    for j, (lo, hi) in enumerate(((0, D), (D, DIN))):
                        sp.dma_start(w_in[:, :, lo:hi], w_in_v[:, :, lo:hi]).then_inc(win_in[j], 16)
                if n >= 2:
                    sp.wait_ge(ada_done, n - 1)
                col = m * D + half * 512
                sp.dma_start(ada[n % 2], a["w_ada"][0].rearrange("(p k) n -> p k n", k=KD)[:, :, col:col + 512]
                             ).then_inc(ada_in[n % 2], 16)
            sp.wait_ge(ada_done, len(ADA))
            sp.dma_start(w_out, a["w_out"][0].rearrange("(k p) n -> p k n", p=P)).then_inc(wout_in, 16)
            sp.wait_ge(wst_evac, 2)
            for t in (1, 2):
                sp.wait_ge(x_loaded, 16 * t)
                sp.dma_start(xh[:, t, :], x_rows(t)).then_inc(x_loaded, 16)
            for half, buf in ((0, osq), (1, vsq)):
                sp.wait_ge(ada_evac, len(ADA) - 1 + half)
                sp.dma_start(gate2_dram[:, half * 512:(half + 1) * 512], buf[0:1, :]).then_inc(gate2_stored, 16)

            ch = Chain(sp, sp_c)

            def store(t):
                ch.restart()
                sp.wait_ge(h_ready, t + 1)
                ch.settle()
                sp.dma_start(h_dram[bass.ds(t * P, P), :], xrow(t)).then_inc(h_stored, 16)
                sp.wait_ge(n2_ready, t + 1)
                sp.dma_start(n2_dram[bass.ds(t * P, P), :], hn[:]).then_inc(n2_stored, 16)
                sp.wait_ge(n2_stored, t * 16 + 16)
                sp.sem_inc(hn_free, 1)

            sp.sem_inc(hn_free, 1)
            with sp.Fori(0, NT - 3) as t:
                store(t)
                sp.wait_ge(h_stored, t * 16 + 16)
                ch.settle()
                sp.wait_ge(x_loaded, t * 16 + 48)
                ch.settle()
                sp.dma_start(xrow(t), x_rows(t + 3)).then_inc(x_loaded, 16)
            for t in range(NT - 3, NT - 1):
                store(t)

            def load_expert(e, n):
                gate, up, down = (a[w][0, bass.ds(e, 1), :, :] for w in ("w_gate", "w_up", "w_down"))
                for s in range(6):
                    if n is not None:
                        if s < 2:
                            sp.wait_ge(gup_done, n * KD - 4)
                        elif s < 4:
                            sp.wait_ge(gup_done, n * KD)
                        else:
                            sp.wait_ge(down_done, n * BLK)
                    elif s == 5:
                        store(NT - 1)
                        sp.wait_ge(cat_ready, NT)
                        sp.wait_ge(h_stored, 16 * NT)
                        sp.wait_ge(lg_done, NT)
                    if s < 4:
                        src = (gate if s % 2 == 0 else up).rearrange("e (p k) f -> p (e k) f", k=KD)[
                            :, :, (s // 2) * 512:(s // 2) * 512 + 512]
                        dst = pieces[s].rearrange("p (k f) -> p k f", k=KD)
                    else:
                        src = down.rearrange("e (k p) d -> p (e k) d", p=P)[:, (s - 4) * 4:(s - 4) * 4 + 4, :]
                        dst = pieces[s].rearrange("p (k f) -> p k f", k=4)
                    sp.dma_start(dst, src).then_inc(piece_in[s], 16)

            sp.wait_ge(glow_done, NT)
            load_expert(0, None)
            for dst, src in ((gate2, bcast_row(gate2_dram[0], D)),
                             (badarow, bcast_row(a["b_ada"][0, 5 * D:6 * D], D)),
                             (gfrow, bcast_row(a["g_post_ffn"][0], D)),
                             (bdown, a["b_down"][0])):
                sp.dma_start(dst, src).then_inc(g2_in, 16)
            with sp.Fori(1, E) as e:
                load_expert(e, e)

            sp.wait_ge(cnt_ready, 1)
            overflow(sp, lambda e, c, nth, left: load_expert(e, nth + E))

            sp.wait_ge(moe_done, 1)
            def load_y(t, i):
                yb, hb, _ = stage4(i)
                sp.dma_start(yb, y_dram.rearrange("(t k) d -> t (k d)", k=TOPK)[bass.ds(t * P, P), :]
                             ).then_inc(y_in[i], 16)
                sp.dma_start(hb, h_dram[bass.ds(t * P, P), :]).then_inc(hb_in[i], 16)

            def store_out(j, i):
                sp.wait_ge(o_ready[i], j + 1)
                sp.dma_start(out[0, (j * NS + i) * P:(j * NS + i + 1) * P, :], stage4(i)[2]).then_inc(out_stored[i], 16)

            for i in range(NS):
                load_y(i, i)
                sp.sem_inc(oslot_free[i], 1)
            for j in range(NT // NS):
                for i in range(NS):
                    store_out(j, i)
                    if j < NT // NS - 1:
                        load_y((j + 1) * NS + i, i)
                for i in range(NS):
                    sp.wait_ge(out_stored[i], (j + 1) * 16)
                    sp.sem_inc(oslot_free[i], 1)

        @block.gpsimd
        def _(pool):
            ch = Chain(pool, pool_c)
            link = ch.link
            g = nc.gpsimd
            link(g.memset(ident[:], 0.0))
            link(g.affine_select(out=ident[:], in_=ident[:], compare_op=ALU.not_equal, fill=1.0, base=0,
                                 pattern=[[-1, P]], channel_multiplier=1))
            link(g.memset(ones[:], 1.0))
            link(g.memset(before[:], 1.0))
            link(g.affine_select(out=before[:], in_=before[:], compare_op=ALU.is_ge, fill=0.0, base=-1,
                                 pattern=[[1, P]], channel_multiplier=-1))
            link(g.memset(keep, 1.0))
            link(g.affine_select(out=keep, in_=keep, compare_op=ALU.is_ge, fill=0.0, base=0,
                                 pattern=[[0, GH], [1, P]], channel_multiplier=-1))
            link(g.memset(keep[0:CH, :, CH:P], 0.0))
            link(g.memset(reset[:], 1.0))
            for c in range(4):
                link(g.memset(reset[:, c * CH:c * CH + 1], 0.0))
            for z in (qz[:], kdz[:], Sm, state, csum[:]):
                link(g.memset(z, 0.0))
            link(g.memset(eps[:], EPS))
            link(g.iota(iotaEi[:], pattern=[[1, E]], base=0, channel_multiplier=0))
            link(g.tensor_copy(iotaE[:], iotaEi[:]))
            link(g.iota(vals[:], pattern=[[P * TOPK, NT], [1, TOPK]], base=0, channel_multiplier=TOPK))
            link(g.memset(sidx[:], EMPTY))
            pool.sem_inc(slot_free, 1)
            pool.sem_inc(const_ready, 1)
            slots = slot_dram.rearrange("(p c) o -> p (c o)", p=P)[:, 0:NCOL]
            g.dma_start(slots, sidx[:]).then_inc(prefill_in, 16)
            pool.wait_ge(wst_evac, 1)
            g.affine_select(out=wsT, in_=wsT, compare_op=ALU.is_ge, fill=0.0, base=0,
                            pattern=[[0, SH], [1, P]], channel_multiplier=-1).then_inc(wst_masked, 1)
            pool.wait_ge(prefill_in, 16)

            with pool.Fori(0, NT) as t:
                ch.restart()
                pool.wait_ge(slot_ready, t + 1)
                ch.settle()
                link(g.tensor_copy(sslot[:], slot[:]))
                for k in range(TOPK):
                    g.indirect_dma_start(out=slot_dram[:, :], out_offset=bass.IndirectOffsetOnAxis(ap=sslot[:, k:k + 1], axis=0),
                                         in_=vcur[:, k:k + 1], in_offset=None,
                                         bounds_check=P * TPITCH - 1, oob_is_err=False).then_inc(scattered[k], 16)
                for k in range(TOPK):
                    pool.wait_ge(scattered[k], t * 16 + 16)
                pool.sem_inc(slot_free, 1)

            g.dma_start(sidx[:], slots).then_inc(table_in, 16)
            pool.wait_ge(gidx_ready, 1)
            pool.wait_ge(cnt_ready, 1)
            pool.wait_ge(n2_stored, 16 * NT)
            pool.wait_ge(mix_done, NT)

            def gather(col):
                link(g.tensor_copy(gcur[:], gidx[:, bass.ds(col, BLK)]))
                for b in range(BLK):
                    g.indirect_dma_start(out=xg[:, b, :], out_offset=None, in_=n2_dram[:, :],
                                         in_offset=bass.IndirectOffsetOnAxis(ap=gcur[:, b:b + 1], axis=0),
                                         bounds_check=T - 1, oob_is_err=False).then_inc(xg_in[b], 16)

            def scatter(col, m):
                link(g.tensor_copy(scol[:], sidx[:, bass.ds(col, BLK)]))
                pool.wait_ge(yo_ready, m * BLK + (BLK + 1))
                ch.settle()
                link(g.tensor_copy(scur[:], scol[:]))
                for b in range(BLK):
                    g.indirect_dma_start(out=y_dram[:, :], out_offset=bass.IndirectOffsetOnAxis(ap=scur[:, b:b + 1], axis=0),
                                         in_=yo[:, b, :], in_offset=None,
                                         bounds_check=T * TOPK - 1, oob_is_err=False).then_inc(y_stored[b], 16)
                for b in range(BLK):
                    pool.wait_ge(y_stored[b], m * 16 + 16)
                pool.sem_inc(yo_free, 1)

            ch.restart()
            link(g.memset(xg, 0.0))
            gather(0)
            pool.sem_inc(yo_free, 1)
            with pool.Fori(0, E) as e:
                ch.restart()
                pool.wait_ge(xgt_done, e * (2 * BLK) + 2 * BLK)
                for b in range(BLK):
                    pool.wait_ge(xg_in[b], e * 16 + 16)
                ch.settle()
                gather(e * COLS + COLS)
                scatter(e * COLS, e)

            def again(e, c, nth, left):
                ch.restart()
                pool.wait_ge(xgt_done, nth * (2 * BLK) + (E + 1) * 2 * BLK)
                for b in range(BLK):
                    pool.wait_ge(xg_in[b], nth * 16 + (E + 1) * 16)
                ch.settle()
                gather(e * COLS + c * BLK)
                scatter(e * COLS + c * BLK, nth + E)

            overflow(pool, again)
            for b in range(BLK):
                pool.wait_ge(xg_in[b], 16 * (E + 1))
            pool.sem_inc(moe_done, 1)

        @block.tensor
        def _(pe):
            mm, tr = nc.tensor.matmul, nc.tensor.transpose

            def four(bank, src, k0=0):
                for k in range(4):
                    last = tr(bank[:, k * P:(k + 1) * P], src(k0 + k), ident[:])
                return last

            def by_k(buf):
                v = buf.rearrange("p (q k) -> p k q", k=KD)
                return lambda k: v[:, k, :]

            def ada_piece(n):
                pe.wait_ge(ada_in[n % 2], 16 * (n // 2 + 1))
                if n >= 2:
                    pe.wait_ge(ada_evac, n - 1)
                bank = (R0, R1)[n % 2]
                for k in range(KD):
                    last = mm(bank[:, :], cbc[:, k, :], ada[n % 2][:, k, :], start=(k == 0), stop=(k == KD - 1))
                last.then_inc(ada_done, 1)

            def project_rows(bank, lo, done, n=None):
                for k in range(KD):
                    if n is not None and k % 4 == 0:
                        pe.wait_ge(nT_ready, n + k // 4)
                    last = mm(bank[:, :], nT[:, k, :], w_in[:, k, lo:lo + 512], start=(k == 0), stop=(k == KD - 1))
                last.then_inc(done, 1)

            def project_T():
                for j in range(4):
                    for k in range(KD):
                        last = mm(QK[:, j * P:(j + 1) * P], w_in[:, k, D + j * P:D + (j + 1) * P], nT[:, k, :],
                                  start=(k == 0), stop=(k == KD - 1))
                last.then_inc(qk_done, 1)
                for k in range(KD):
                    last = mm(ZB[0:RANK, 0:P], w_in[:, k, DIN - RANK:DIN], nT[:, k, :], start=(k == 0), stop=(k == KD - 1))
                last.then_inc(glow_done, 1)

            def transpose_x(t):
                pe.wait_ge(xn_ready, t + 1)
                four(T0, by_k(xn[:]))
                four(T1, by_k(xn[:]), 4).then_inc(xt_done, 1)

            pe.wait_ge(const_ready, 1)
            pe.wait_ge(const_in, 16 * N_CONST)
            four(T0, lambda k: nT[:, k, :])
            four(T1, lambda k: nT[:, k, :], 4).then_inc(wst_done, 1)
            pe.wait_ge(wst_evac, 1)
            tr(T0[:, 0:SH], xn[0:SH, 0:P], ident[0:SH, 0:SH])
            tr(T0[:, 16:18], xn[0:2, P:2 * P], ident[0:2, 0:2])
            for k in range(KD):
                tr(T0[:, 64 + k * E:64 + (k + 1) * E], cat[0:E, k * P:(k + 1) * P], ident[0:E, 0:E])
            for k in range(KD):
                last = tr(T1[:, 64 + k * E:64 + (k + 1) * E], xh[0:E, 1, k * P:(k + 1) * P], ident[0:E, 0:E])
            last.then_inc(wst_done, 1)
            pe.wait_ge(cbc_ready, 1)
            for n in range(EARLY):
                ada_piece(n)
            def modulation_columns(scale, shift, done):
                for q, row in ((0, scale), (1, shift)):
                    for k in range(KD):
                        last = mm(SG[:, q * KD + k:q * KD + k + 1], row.rearrange("o (p k) -> o p k", k=KD)[:, :, k],
                                  ones[0:1, 0:1], start=True, stop=True)
                last.then_inc(done, 1)

            pe.wait_ge(ada_evac, EARLY)
            modulation_columns(adarow[0:1, 0, :], adarow[0:1, 1, :], adat_done)
            transpose_x(0)
            pe.wait_ge(nT_ready, 2)
            pe.wait_ge(win_in[0], 16)
            project_rows(OB, 0, u_done)
            project_rows(T1, 512, v_done)
            pe.wait_ge(win_in[1], 16)
            pe.wait_ge(gu_ready, 1)
            project_rows(OB, 1536, vv_done)
            pe.wait_ge(gv_ready, 1)
            project_rows(T1, 2048, r_done)
            project_T()
            for n in range(EARLY, len(ADA)):
                ada_piece(n)
            pe.wait_ge(mods_ready, 1)
            modulation_columns(cat[0:1, :], hn[0:1, :], modt_done)
            pe.wait_ge(mods_ready, 2)
            pe.wait_ge(wst_masked, 1)
            pe.wait_ge(vv_ready, 1)
            pe.wait_ge(sr_ready, 1)
            pe.wait_ge(wout_in, 16)

            def tile(t, back, ahead):
                def value(h):
                    return rows[:, bass.ds(t % 2, 1), 2, h * GV:(h + 1) * GV].rearrange("p a n -> p (a n)")

                pe.wait_ge(gl_ready, t + 1)
                if ahead:
                    transpose_x(t + 1)
                for j in range(2):
                    last = mm(ZB[:, P + j * P:P + (j + 1) * P], wgk[:, j * P:(j + 1) * P], glT[:], start=True, stop=True)
                last.then_inc(z_done, 1)
                if ahead:
                    project_rows(SG, 0, u_done, t * 2 + 3)
                if back:
                    transpose_n2(t - 1)
                if ahead:
                    project_rows(R1, 512, v_done)
                if back:
                    pe.wait_ge(z_ready, t + 1)
                    logits(t - 1)
                pe.wait_ge(qks_ready, t + 1)
                for j in range(2):
                    last = tr(T0[:, j * P:(j + 1) * P], kdT[:, j, :], ident[:])
                last.then_inc(kdt_done, 1)
                for h in range(GH):
                    last = mm(OB[:, h * P:(h + 1) * P], ks[:, h // 2, :], qz[:, h % 2, h // 2, :], start=True, stop=True)
                last.then_inc(s_done, 1)
                if ahead:
                    pe.wait_ge(gu_ready, t + 2)
                pe.wait_ge(vh_ready, t + 1)
                for h in range(SH):
                    last = mm(SG[:, h * SHD:(h + 1) * SHD], wsT[:, h, :],
                              rows[:, bass.ds(t % 2, 1), 1, h * SHD:(h + 1) * SHD].rearrange("p a n -> p (a n)"),
                              start=True, stop=True)
                last.then_inc(sgu_done, 1)
                pe.wait_ge(kdz_ready, t + 1)
                for c, bank in ((0, T1), (1, ZB)):
                    for h in range(GH):
                        last = mm(bank[:, h * P:(h + 1) * P], kdz[:, c, (h // 2) * P:(h // 2 + 1) * P],
                                  value(h), start=True, stop=True)
                last.then_inc(ds_done, 1)
                if ahead:
                    project_rows(R0, 1536, vv_done)
                pe.wait_ge(sm_ready, t + 1)
                if back:
                    ranks(t - 1)
                pe.wait_ge(st1_ready, t + 1)
                for h in range(GH):
                    mm(QK[:, h * GV:(h + 1) * GV], Sm[:, h, :], value(h), start=True, stop=False, skip_group_check=True)
                    for c in range(2):
                        last = mm(QK[c * CH:(c + 1) * CH, h * GV:(h + 1) * GV], qz[:, h % 2, h // 2, c * CH:(c + 1) * CH],
                                  state[:, c, h // 2, :], start=False, stop=(c == 1), skip_group_check=True)
                last.then_inc(o_done, 1)
                if ahead:
                    pe.wait_ge(gv_ready, t + 2)
                    project_rows(R1, 2048, r_done)
                pe.wait_ge(cat_ready, t + 1)
                four(T0, lambda k: cat[:, k * P:(k + 1) * P]).then_inc(catt_done, 1)
                four(T1, lambda k: cat[:, k * P:(k + 1) * P], 4).then_inc(catt_done, 1)
                if ahead:
                    pe.wait_ge(vv_ready, t + 2)
                pe.wait_ge(catTd, t + 1)
                for k0, ready in ((0, None), (4, catTa)):
                    for j, bank in ((0, R0), (1, R1)):
                        if ahead and k0 == 0 and j == 1:
                            pe.wait_ge(sr_ready, t + 2)
                        if ready is not None and j == 0:
                            pe.wait_ge(ready, t + 1)
                        for k in range(k0, k0 + 4):
                            last = mm(bank[:, :], catT[:, k, :], w_out[:, k, j * 512:(j + 1) * 512],
                                      start=(k == 0), stop=(k == KD - 1), skip_group_check=True)
                last.then_inc(mix_done, 1)
                if ahead:
                    pe.wait_ge(st0_ready, t + 1)
                    project_T()

            def transpose_n2(t):
                pe.wait_ge(n2_ready, t + 1)
                four(T0, by_k(hn[:]))
                four(T1, by_k(hn[:]), 4).then_inc(n2t_done, 1)

            def logits(t):
                pe.wait_ge(n2T_ready, t * 2 + 2)
                for k in range(KD):
                    last = mm(ZB[:, 0:E], catT[:, k, :], wr[:, k, :], start=(k == 0), stop=(k == KD - 1))
                last.then_inc(lg_done, 1)

            def ranks(t):
                pe.wait_ge(chosen_ready, t + 1)
                mm(OB[:, 0:E], before[:], chosen[:], start=True, stop=False)
                mm(OB[:, 0:E], ones[:], csum[:], start=False, stop=True).then_inc(cum_done, 1)

            tile(0, False, 2)
            with pe.Fori(1, NT - 2) as t:
                tile(t, True, 2)
            tile(NT - 2, True, 1)
            tile(NT - 1, True, 0)
            transpose_n2(NT - 1)
            pe.wait_ge(st0_ready, NT)
            logits(NT - 1)
            ranks(NT - 1)
            pe.wait_ge(slot_ready, NT)
            mm(OB[:, 0:E], ones[:], csum[:], start=True, stop=True).then_inc(cnt_done, 1)

            def transpose_rows(m, cnt):
                for b in range(BLK):
                    if b == 2:
                        pe.wait_ge(xTa, m * BLK + 1)
                        pe.wait_ge(xTd, m * BLK + 1)

                    def full():
                        pe.wait_ge(xg_in[b], m * 16 + 16)
                        for half in range(2):
                            four(TD[(2 * b + half) % 4], by_k(xg[:, b, :]), 4 * half).then_inc(xgt_done, 1)

                    if b == 0:
                        full()
                    else:
                        with pe.If(cnt > b * P):
                            full()
                        with pe.Else():
                            for half in range(2):
                                mm(TD[(2 * b + half) % 4][:, 0:64], ident[:], ident[:, 0:64], start=True, stop=True
                                   ).then_inc(xgt_done, 1)

            def gate_up(m, width):
                for f in range(KD):
                    s = f // 4 * 2
                    if f % 4 == 0:
                        pe.wait_ge(piece_in[s], m * 16 + 16)
                        pe.wait_ge(piece_in[s + 1], m * 16 + 16)
                    pe.wait_ge(gup_free, m * KD + (f + 1))
                    for piece, bank in ((pieces[s], ps[f % 2]), (pieces[s + 1], ps[2 + f % 2])):
                        w = piece.rearrange("p (k f) -> p k f", k=KD)
                        for k in range(KD):
                            last = mm(bank[:, 0:width], w[:, k, (f % 4) * P:(f % 4 + 1) * P], xT[:, k, 0:width],
                                      start=(k == 0), stop=(k == KD - 1))
                    last.then_inc(gup_done, 1)

            def gate_up_by_count(m, cnt, widths=WIDTHS):
                if len(widths) == 1:
                    gate_up(m, widths[0])
                else:
                    mid = len(widths) // 2
                    with pe.If(cnt <= widths[mid - 1]):
                        gate_up_by_count(m, cnt, widths[:mid])
                    with pe.Else():
                        gate_up_by_count(m, cnt, widths[mid:])

            def down(m, cnt):
                for b in range(BLK):
                    lo, hi = (TD[2], TD[3]) if b % 2 == 0 else (TD[0], TD[1])
                    if b == 0:
                        pe.wait_ge(piece_in[4], m * 16 + 16)
                        pe.wait_ge(piece_in[5], m * 16 + 16)
                    if b < 2:
                        pe.wait_ge(xTa, m * BLK + (BLK + min(b + 2, BLK)))
                        pe.wait_ge(xTd, m * BLK + (BLK + min(b + 2, BLK)))

                    def full():
                        if b == 2:
                            pe.wait_ge(yo_ready, m * BLK + 2)
                        for t in range(KD):
                            if b == 0:
                                pe.wait_ge(hid_ready, m * KD + (t + 1))
                            w = pieces[4 + t // 4].rearrange("p (k f) -> p k f", k=4)
                            for j, bank in ((0, lo), (1, hi)):
                                last = mm(bank[:, :], hT[:, t, b * P:(b + 1) * P], w[:, t % 4, j * 512:(j + 1) * 512],
                                          start=(t == 0), stop=(t == KD - 1))
                        last.then_inc(down_done, 1)

                    if b == 0:
                        full()
                    else:
                        with pe.If(cnt > b * P):
                            full()
                        with pe.Else():
                            mm(ps[0][:, 0:64], ident[:], ident[:, 0:64], start=True, stop=True).then_inc(down_done, 1)

            def one_pass(m, cnt, following):
                pe.wait_ge(xTa, m * BLK + BLK)
                pe.wait_ge(xTd, m * BLK + BLK)
                gate_up_by_count(m, cnt)
                pe.wait_ge(yo_ready, m * BLK + 1)
                transpose_rows(m + 1, following)
                down(m, cnt)

            pe.wait_ge(cnt_ready, 1)
            pe.wait_ge(psum_init, 1)
            transpose_rows(0, pe.value_load(cnti[0:1, 0:1], min_val=0, max_val=T))
            with pe.Fori(0, E) as e:
                cnt = pe.value_load(cnti[0:1, bass.ds(e, 1)], min_val=0, max_val=T)
                following = pe.value_load(cnti[0:1, bass.ds(e + 1, 1)], min_val=0, max_val=T)
                one_pass(e, cnt, following)

            def again(e, c, nth, left):
                pe.wait_ge(yo_ready, nth * BLK + (E * BLK + 1))
                transpose_rows(nth + (E + 1), left)
                pe.wait_ge(xTa, nth * BLK + (E + 2) * BLK)
                pe.wait_ge(xTd, nth * BLK + (E + 2) * BLK)
                gate_up_by_count(nth + E, left)
                down(nth + E, left)

            overflow(pe, again)

            pe.wait_ge(g2_in, 64)
            with pe.Fori(0, NT // NS) as j:
                pe.wait_ge(wcur_ready, j + 1)
                for i in range(NS):
                    last = tr(T0[0:E, i * P:(i + 1) * P], wcur[:, i * E:(i + 1) * E], ident[:])
                last.then_inc(wdt_done, 1)
                pe.wait_ge(wdT_ready, j + 1)
                for i in range(NS):
                    if i >= 2:
                        pe.wait_ge(bias_read, j * NS + (i - 1))
                    for c, bank in enumerate(bias_banks(i)):
                        last = mm(bank[:, :], wdT[:, i * P:(i + 1) * P], bdown[:, c * 512:(c + 1) * 512], start=True, stop=True)
                    last.then_inc(bias_done, 1)

        @block.scalar
        def _(act):
            ch = Chain(act, act_c)
            link = ch.link
            A = nc.scalar.activation

            def root(dst, src, n, done):
                A(dst, src, ACT.Sqrt, bias=eps[:, 0:1], scale=1.0 / n).then_inc(done, 1)

            def x_stats(t):
                act.wait_ge(x_loaded, t * 16 + 16)
                act.wait_ge(xt_done, t)
                link(A(xn[:], xrow(t), ACT.Square, accum_out=xs[:, 0:1]))
                root(xs[:, 1:2], xs[:, 0:1], D, xstat)

            def gelu_uv(t, u, v):
                act.wait_ge(u_done, t + 1)
                A(rowbuf(t, 0), u[:, :], ACT.Gelu_apprx_tanh).then_inc(gu_ready, 1)
                act.wait_ge(v_done, t + 1)
                A(rowbuf(t, 1), v[:, :], ACT.Gelu_apprx_tanh).then_inc(gv_ready, 1)

            def v_root(t):
                act.wait_ge(vsum_ready, t + 1)
                root(vs[:, 1, :], vs[:, 0, :], SHD, vrstd_ready)

            def copy_value(t, bank):
                act.wait_ge(vv_done, t + 1)
                A(rowbuf(t, 2), bank[:, :], ACT.Copy).then_inc(vv_ready, 1)

            def silu_r(t, bank):
                act.wait_ge(r_done, t + 1)
                A(rowbuf(t, 3), bank[:, :], ACT.Silu).then_inc(sr_ready, 1)

            def copy_glow(t):
                act.wait_ge(glow_done, t + 1)
                A(glT[:], ZB[0:RANK, 0:P], ACT.Copy).then_inc(gl_ready, 1)

            act.sem_inc(yo_ready, 1)
            act.wait_ge(const_ready, 1)
            act.wait_ge(c_in, 16)
            A(siluc[:], ccol[:], ACT.Silu).then_inc(silu_ready, 1)
            act.wait_ge(x_loaded, 16)
            act.wait_ge(wst_evac, 2)
            link(A(xn[:], xrow(0), ACT.Square, accum_out=xs[:, 0:1]))
            root(xs[:, 1:2], xs[:, 0:1], D, xstat)
            gelu_uv(0, OB, T1)
            v_root(0)
            copy_value(0, OB)
            silu_r(0, T1)
            copy_glow(0)
            x_stats(1)
            act.wait_ge(mods_ready, 1)

            def tile(t, back, ahead):
                ch.restart()
                act.wait_ge(z_ready, t + 1)
                link(A(az, zb, ACT.Abs))
                link(A(az, az, ACT.Exp, scale=-1.0))
                A(az, az, ACT.Ln, bias=1.0).then_inc(lnz_ready, 1)
                act.wait_ge(bc_ready, t + 1)
                A(eb[:], bc[:], ACT.Exp, scale=1.0 / 16)
                A(enb[:], bc[:], ACT.Exp, scale=-1.0 / 16)
                A(dec[:], zb, ACT.Exp, scale=-1.0 / 16).then_inc(exp_ready, 1)
                if ahead:
                    gelu_uv(t + 1, SG, R1)
                if back:
                    exps(t - 1)
                if ahead:
                    v_root(t + 1)
                    copy_value(t + 1, R0)
                act.wait_ge(o_done, t + 1)
                A(osq[:], QK[:, :], ACT.Square).then_inc(osq_ready, 1)
                act.wait_ge(osum_ready, t + 1)
                root(os_[:, 1, :], os_[:, 0, :], GV, orstd_ready)
                if ahead:
                    silu_r(t + 1, R1)
                if ahead == 2:
                    x_stats(t + 2)
                act.wait_ge(catt_done, t * 2 + 2)
                A(catT[:, 4:8, :], T1[:, :].rearrange("p (k n) -> p k n", k=4), ACT.Copy).then_inc(catTa, 1)
                act.wait_ge(mix_done, t + 1)
                link(A(osq[:], R0[:, :], ACT.Square, accum_out=ms[:, 0:1]))
                link(A(osq[:], R1[:, :], ACT.Square, accum_out=ms[:, 1:2]))
                link(A(ms[:, 2:3], ms[:, 0:1], ACT.Identity, bias=ms[:, 1:2]))
                root(ms[:, 3:4], ms[:, 2:3], D, mstat)
                act.wait_ge(h_ready, t + 1)
                link(A(cat[:], xrow(t), ACT.Square, accum_out=ms[:, 4:5]))
                root(ms[:, 5:6], ms[:, 4:5], D, hstat)
                if ahead:
                    copy_glow(t + 1)

            def exps(t):
                act.wait_ge(dif_ready, t + 1)
                A(ex4[:], dif4[:], ACT.Exp, accum_out=exsum[:, 0:1]).then_inc(ex_ready, 1)

            tile(0, False, 2)
            with act.Fori(1, NT - 2) as t:
                tile(t, True, 2)
            tile(NT - 2, True, 1)
            tile(NT - 1, True, 0)
            exps(NT - 1)

            def fills(m):
                for b in range(BLK):
                    act.wait_ge(xgt_done, m * (2 * BLK) + (2 * b + 1))
                    for k in range(4):
                        last = A(xT[:, k, b * P:(b + 1) * P], TD[2 * b % 4][:, k * P:(k + 1) * P], ACT.Identity,
                                 bias=B2[:, k:k + 1], scale=A2[:, k:k + 1])
                    last.then_inc(xTa, 1)

            def sigmoids(m):
                for f in range(KD):
                    act.wait_ge(g_ready, m * KD + (f + 1))
                    A(s_sb[:, f % 2, :], g_sb[:, f % 2, :], ACT.Sigmoid, scale=ALPHA).then_inc(sig_ready, 1)

            def down_rows(m):
                act.wait_ge(yo_free, m + 1)
                for b in range(BLK):
                    lo, hi = (TD[2], TD[3]) if b % 2 == 0 else (TD[0], TD[1])
                    act.wait_ge(down_done, m * BLK + (b + 1))
                    A(yo[:, b, 0:512], lo[:, :], ACT.Copy)
                    A(yo[:, b, 512:D], hi[:, :], ACT.Copy).then_inc(yo_ready, 1)

            act.wait_ge(cnt_ready, 1)
            act.wait_ge(psum_init, 1)
            fills(0)
            with act.Fori(0, E) as e:
                sigmoids(e)
                fills(e + 1)
                down_rows(e)

            def again(e, c, nth, left):
                fills(nth + (E + 1))
                sigmoids(nth + E)
                down_rows(nth + E)

            overflow(act, again)

            act.wait_ge(g2_in, 64)
            with act.Fori(0, NT // NS) as j:
                ch.restart()
                for i in range(NS):
                    act.wait_ge(f_ready, j * NS + (i + 1))
                    link(A(junk4, stage4(i)[0][:, 0:D], ACT.Square, accum_out=os_[:, 0, i:i + 1]))
                    root(os_[:, 1, i:i + 1], os_[:, 0, i:i + 1], D, fstat)

        @block.vector
        def _(dve):
            ch = Chain(dve, dve_c)
            link = ch.link
            v = nc.vector

            def b3(src, n):
                return src.unsqueeze(2).broadcast_to((P, src.shape[1], n))

            def inverse(dst):
                link(v.reciprocal(dst, dst))

            def normed_x(t):
                dve.wait_ge(xstat, t + 1)
                inverse(xs[:, 1:2])
                v.tensor_scalar(xn[:], xrow(t), xs[:, 1:2], None, ALU.mult).then_inc(xn_ready, 1)

            def modulate(dst, A_, B_, done):
                for k in range(KD):
                    bank = (T0, T1)[k // 4]
                    last = v.tensor_scalar(dst[:, k, :], bank[:, (k % 4) * P:(k % 4 + 1) * P], A_[:, k:k + 1], B_[:, k:k + 1],
                                           ALU.mult, ALU.add)
                    if k % 4 == 3:
                        last.then_inc(done, 1)

            def next_nT(t):
                dve.wait_ge(xt_done, t + 1)
                modulate(nT, A1, B1, nT_ready)

            def v_squares(t):
                dve.wait_ge(gv_ready, t + 1)
                link(v.tensor_tensor(vsq, rowbuf(t, 1), rowbuf(t, 1), ALU.mult))
                v.tensor_reduce(vs[:, 0, :], vsq.rearrange("p (h d) -> p h d", h=SH), AX_X, ALU.add).then_inc(vsum_ready, 1)

            def v_norm(t):
                dve.wait_ge(vrstd_ready, t + 1)
                inverse(vs[:, 1, :])
                r = rowbuf(t, 1)
                r3 = r.rearrange("p (h d) -> p h d", h=SH)
                link(v.tensor_tensor(r3, r3, b3(vs[:, 1, :], SHD), ALU.mult))
                v.tensor_tensor(r, r, gv_row[:], ALU.mult).then_inc(vh_ready, 1)

            def decay_state(src, dst, bank, at):
                for h in range(GH):
                    lo, j = (h % 2) * DK, h // 2
                    last = v.scalar_tensor_tensor(out=state[lo:lo + DK, dst, j, :], in0=state[lo:lo + DK, src, j, :],
                                                  scalar=eb[lo:lo + DK, j, at:at + 1], in1=bank[lo:lo + DK, h * P:(h + 1) * P],
                                                  op0=ALU.mult, op1=ALU.add)
                return last

            dve.wait_ge(const_ready, 1)
            dve.wait_ge(silu_ready, 1)
            v.tensor_copy(cbc, b3(siluc[:], P)).then_inc(cbc_ready, 1)
            dve.wait_ge(wst_done, 1)
            link(v.tensor_copy(wsT[:, 0:4, :], T0[:, :].rearrange("p (k n) -> p k n", k=4)))
            v.tensor_copy(wsT[:, 4:8, :], T1[:, :].rearrange("p (k n) -> p k n", k=4)).then_inc(wst_evac, 1)
            dve.wait_ge(wst_done, 2)
            link(v.tensor_copy(bsT[:], T0[:, 0:SH]))
            link(v.tensor_copy(bgkT[:], T0[:, 16:18]))
            link(v.tensor_copy(bgT[:], T0[:, 64:64 + KD * E].rearrange("p (k e) -> p e k", k=KD)))
            v.tensor_scalar(buT[:], T1[:, 64:64 + KD * E].rearrange("p (k e) -> p e k", k=KD), 1.0, None,
                            ALU.add).then_inc(wst_evac, 1)
            for n in range(EARLY):
                dve.wait_ge(ada_done, n + 1)
                v.tensor_copy(adarow[0:1, n // 2, (n % 2) * 512:(n % 2 + 1) * 512], (R0, R1)[n % 2][0:1, :]).then_inc(ada_evac, 1)
            dve.wait_ge(adat_done, 1)
            def columns(j):
                link(v.tensor_tensor(AB[:, 2 * j, :], SG[:, 0:KD], badac[:, 2 * j + 1, :], ALU.add))
                link(v.scalar_tensor_tensor(out=AB[:, 2 * j, :], in0=AB[:, 2 * j, :], scalar=1.0, in1=gpre[:, j, :],
                                            op0=ALU.add, op1=ALU.mult))
                link(v.tensor_tensor(AB[:, 2 * j + 1, :], SG[:, KD:2 * KD], badac[:, 2 * j, :], ALU.add))

            columns(0)
            normed_x(0)
            next_nT(0)
            v_squares(0)
            v_norm(0)
            for n in range(EARLY, len(ADA)):
                m, half = ADA[n]
                cols = slice(half * 512, (half + 1) * 512)
                bank = (R0, R1)[n % 2][:, :]
                dve.wait_ge(ada_done, n + 1)
                if m != 2:
                    row = {3: hn[0:1, cols], 4: cat[0:1, cols], 5: (osq, vsq)[half][0:1, :]}[m]
                    v.tensor_copy(row, bank[0:1, :]).then_inc(ada_evac, 1)
                    continue
                dst = gate1[:, cols]
                v.tensor_tensor(dst, bank, dst, ALU.add).then_inc(ada_evac, 1)
                dve.wait_ge(ada_evac, n + 1)
                link(v.tensor_tensor(dst, dst, gprow[:, cols], ALU.mult))
            dve.wait_ge(gate2_stored, 32)
            dve.sem_inc(mods_ready, 1)
            dve.wait_ge(modt_done, 1)
            columns(1)
            dve.sem_inc(mods_ready, 1)
            normed_x(1)

            def tile(t, back, ahead):
                ch.restart()
                if back:
                    normed_h(t - 1)
                dve.wait_ge(z_done, t + 1)
                for j in range(2):
                    last = v.tensor_scalar(zb[:, j, :], ZB[:, P + j * P:P + (j + 1) * P], bgkT[:, j:j + 1], None, ALU.add)
                last.then_inc(z_ready, 1)
                if ahead:
                    next_nT(t + 1)
                dve.wait_ge(lnz_ready, t + 1)
                link(v.scalar_tensor_tensor(out=zb, in0=zb, scalar=0.0, in1=az, op0=ALU.min, op1=ALU.subtract))
                link(v.tensor_tensor_scan(bc[:].rearrange("p a n -> p (a n)"), reset[:], zb.rearrange("p a n -> p (a n)"),
                                          0.0, ALU.mult, ALU.add))
                bc4 = bc[:].rearrange("p a (c n) -> p (a c) n", c=2)
                v.tensor_tensor(zb.rearrange("p a (c n) -> p (a c) n", c=2), bc4,
                                bc4[:, :, CH - 1:CH].broadcast_to((P, 4, CH)), ALU.subtract).then_inc(bc_ready, 1)
                dve.wait_ge(exp_ready, t + 1)
                q = QK[:, 0:2 * P].rearrange("p (a n) -> p a n", a=2)
                k = QK[:, 2 * P:4 * P].rearrange("p (a n) -> p a n", a=2)
                for h in range(2):
                    lo = h * DK
                    v.scalar_tensor_tensor(out=qz[lo:lo + DK, h, :, :], in0=q[lo:lo + DK], scalar=DK ** -0.5,
                                           in1=eb[lo:lo + DK, :, :], op0=ALU.mult, op1=ALU.mult)
                v.tensor_tensor(ks[:], k, enb[:], ALU.mult)
                v.tensor_tensor(kdT, k, dec[:], ALU.mult).then_inc(qks_ready, 1)
                if back:
                    n2_columns(t - 1)
                    read_logits(t - 1)
                dve.wait_ge(kdt_done, t + 1)
                for c in range(2):
                    last = v.tensor_copy(kdz[c * CH:(c + 1) * CH, c, :], T0[c * CH:(c + 1) * CH, 0:2 * P])
                last.then_inc(kdz_ready, 1)
                dve.wait_ge(s_done, t + 1)
                ch.settle()
                v.copy_predicated(Sm, keep.bitcast(I32), OB[:, :].rearrange("p (h n) -> p h n", h=GH)).then_inc(sm_ready, 1)
                dve.wait_ge(ds_done, t + 1)
                decay_state(0, 1, T1, CH - 1).then_inc(st1_ready, 1)
                if back:
                    choose(t - 1)
                dve.wait_ge(sgu_done, t + 1)
                c3 = cat[:, 0:DS].rearrange("p (h d) -> p h d", h=SH)
                link(v.tensor_tensor(c3, SG[:, :].rearrange("p (h d) -> p h d", h=SH), b3(bsT[:], SHD), ALU.add))
                v.tensor_tensor(cat[:, 0:DS], cat[:, 0:DS], rowbuf(t, 0), ALU.mult)
                if ahead:
                    v_squares(t + 1)
                if back:
                    weigh(t - 1)
                    place(t - 1)
                dve.wait_ge(osq_ready, t + 1)
                v.tensor_reduce(os_[:, 0, :], osq[:].rearrange("p (h d) -> p h d", h=GH), AX_X, ALU.add).then_inc(osum_ready, 1)
                dve.wait_ge(st1_ready, t + 1)
                decay_state(1, 0, ZB, P - 1).then_inc(st0_ready, 1)
                dve.wait_ge(orstd_ready, t + 1)
                inverse(os_[:, 1, :])
                o3 = cat[:, DS:D].rearrange("p (h d) -> p h d", h=GH)
                link(v.tensor_tensor(o3, QK[:, :].rearrange("p (h d) -> p h d", h=GH), b3(os_[:, 1, :], GV), ALU.mult))
                link(v.tensor_tensor(o3, o3, go_row[:].unsqueeze(1).broadcast_to((P, GH, GV)), ALU.mult))
                v.tensor_tensor(cat[:, DS:D], cat[:, DS:D], rowbuf(t, 3), ALU.mult).then_inc(cat_ready, 1)
                if ahead:
                    v_norm(t + 1)
                dve.wait_ge(catt_done, t * 2 + 1)
                v.tensor_copy(catT[:, 0:4, :], T0[:, :].rearrange("p (k n) -> p k n", k=4)).then_inc(catTd, 1)
                if ahead == 2:
                    normed_x(t + 2)
                dve.wait_ge(mstat, t + 1)
                inverse(ms[:, 3:4])
                for j, bank in ((0, R0), (1, R1)):
                    link(v.scalar_tensor_tensor(out=cat[:, j * 512:(j + 1) * 512], in0=bank[:, :], scalar=ms[:, 3:4],
                                                in1=gate1[:, j * 512:(j + 1) * 512], op0=ALU.mult, op1=ALU.mult))
                v.tensor_tensor(xrow(t), xrow(t), cat[:], ALU.add).then_inc(h_ready, 1)

            def normed_h(t):
                dve.wait_ge(hstat, t + 1)
                inverse(ms[:, 5:6])
                dve.wait_ge(hn_free, t + 1)
                v.tensor_scalar(hn[:], xrow(t), ms[:, 5:6], None, ALU.mult).then_inc(n2_ready, 1)

            def n2_columns(t):
                dve.wait_ge(n2t_done, t + 1)
                modulate(catT, A2, B2, n2T_ready)

            def read_logits(t):
                dve.wait_ge(lg_done, t + 1)
                link(v.tensor_tensor(lg[:], ZB[:, 0:E], br[:], ALU.add))

            def choose(t):
                link(v.max(top8[:], lg[:]))
                link(v.max_index(ti8[:], top8[:], lg[:]))
                link(v.tensor_copy(tif[:], ti8[:, 0:TOPK]))
                link(v.tensor_tensor(oneh[:], iotaE[:].unsqueeze(1).broadcast_to((P, TOPK, E)), b3(tif[:], E), ALU.is_equal))
                v.tensor_reduce(chosen[:], oneh[:].rearrange("p k e -> p e k"), AX_X, ALU.add).then_inc(chosen_ready, 1)
                v.tensor_scalar(dif4[:], top8[:, 0:TOPK], top8[:, 0:1], None, ALU.subtract).then_inc(dif_ready, 1)

            def weigh(t):
                dve.wait_ge(ex_ready, t + 1)
                link(v.reciprocal(exsum[:, 1:2], exsum[:, 0:1]))
                pr = probs[:, bass.ds(t, 1), :].rearrange("p a k -> p (a k)")
                link(v.tensor_scalar(pcur[:], ex4[:], exsum[:, 1:2], None, ALU.mult))
                v.tensor_copy(pr, pcur[:])
                link(v.tensor_tensor(tmpk[:], oneh[:], b3(pcur[:], E), ALU.mult))
                link(v.tensor_reduce(wden[:, bass.ds(t, 1), :].rearrange("p a e -> p (a e)"),
                                     tmpk[:].rearrange("p k e -> p e k"), AX_X, ALU.add))

            def place(t):
                dve.wait_ge(cum_done, t + 1)
                link(v.tensor_copy(cum[:], OB[:, 0:E]))
                link(v.tensor_tensor(csum[:], csum[:], chosen[:], ALU.add))
                link(v.tensor_tensor(tmpk[:], oneh[:], cum[:].unsqueeze(1).broadcast_to((P, TOPK, E)), ALU.mult))
                link(v.tensor_reduce(rank[:], tmpk[:], AX_X, ALU.add))
                link(v.tensor_copy(ranki[:], rank[:]))
                link(v.tensor_scalar(ia[:], ranki[:], P - 1, TPITCH.bit_length() - 1, ALU.bitwise_and, ALU.logical_shift_left))
                link(v.tensor_scalar(ib[:], ranki[:], P.bit_length() - 1, None, ALU.logical_shift_right))
                link(v.tensor_scalar(ic[:], tif[:], float(COLS), None, ALU.mult))
                link(v.tensor_tensor(iab[:], ia[:], ib[:], ALU.add))
                dve.wait_ge(slot_free, t + 1)
                link(v.tensor_copy(vcur[:], vals[:, bass.ds(t, 1), :].rearrange("p a k -> p (a k)")))
                v.tensor_tensor(slot[:], iab[:], ic[:], ALU.add).then_inc(slot_ready, 1)
                dve.wait_ge(slot_ready, t + 1)

            tile(0, False, 2)
            with dve.Fori(1, NT - 2) as t:
                tile(t, True, 2)
            tile(NT - 2, True, 1)
            tile(NT - 1, True, 0)
            ch.restart()
            normed_h(NT - 1)
            n2_columns(NT - 1)
            read_logits(NT - 1)
            choose(NT - 1)
            weigh(NT - 1)
            place(NT - 1)

            dve.wait_ge(cnt_done, 1)
            link(v.memset(cnti[:, E:E + 1], 0))
            link(v.tensor_copy(cnti[:, 0:E], OB[0:1, 0:E]))
            for c in range(1, NCHUNK):
                link(v.tensor_scalar(overf[:, 0, (c - 1) * E:c * E], OB[0:1, 0:E], float(-c * CAP), None, ALU.add))
            link(v.tensor_copy(overn[:], overf[:, 0, :]))
            link(v.tensor_scalar(overf[:, 1, :], overf[:, 0, :], 0.0, None, ALU.is_gt))
            link(v.tensor_tensor_scan(overf[:, 2, :], ones[0:1, 0:NOVER], overf[:, 1, :], 0.0, ALU.mult, ALU.add))
            link(v.tensor_copy(overt[:], overf[:, 2, NOVER - 1:NOVER]))
            link(v.tensor_tensor(overf[:, 2, :], overf[:, 2, :], overf[:, 1, :], ALU.subtract))
            v.tensor_copy(overo[:], overf[:, 2, :]).then_inc(cnt_ready, 1)
            dve.wait_ge(table_in, 16)
            v.tensor_scalar(gidx, sidx[:], TOPK.bit_length() - 1, None, ALU.logical_shift_right).then_inc(gidx_ready, 1)
            for bank in ps:
                link(v.memset(bank[:, :], 0.0))
            dve.sem_inc(psum_init, 1)
            dve.sem_inc(gup_free, 2)

            def fills(m):
                for b in range(BLK):
                    dve.wait_ge(xgt_done, m * (2 * BLK) + (2 * b + 2))
                    for k in range(4, KD):
                        last = v.tensor_scalar(xT[:, k, b * P:(b + 1) * P], TD[(2 * b + 1) % 4][:, (k - 4) * P:(k - 3) * P],
                                               A2[:, k:k + 1], B2[:, k:k + 1], ALU.mult, ALU.add)
                    last.then_inc(xTd, 1)

            def hidden(m, e):
                ch.restart()
                link(v.tensor_copy(bcur[:, 0, :], bgT[:, bass.ds(e, 1), :].rearrange("p a k -> p (a k)")))
                link(v.tensor_copy(bcur[:, 1, :], buT[:, bass.ds(e, 1), :].rearrange("p a k -> p (a k)")))

                def finish(f):
                    dve.wait_ge(sig_ready, m * KD + (f + 1))
                    link(v.tensor_tensor(g_sb[:, f % 2, :], g_sb[:, f % 2, :], s_sb[:, f % 2, :], ALU.mult))
                    v.scalar_tensor_tensor(out=hT[:, f, :], in0=u_sb[:, f % 2, :], scalar=1.0 - LIMIT, in1=g_sb[:, f % 2, :],
                                           op0=ALU.max, op1=ALU.mult).then_inc(hid_ready, 1)

                for f in range(KD):
                    if f >= 2:
                        dve.wait_ge(hid_ready, m * KD + (f - 1))
                    dve.wait_ge(gup_done, m * KD + (f + 1))
                    v.tensor_scalar(g_sb[:, f % 2, :], ps[f % 2][:, 0:CAP], bcur[:, 0, f:f + 1], LIMIT,
                                    ALU.add, ALU.min).then_inc(g_ready, 1)
                    v.tensor_scalar(u_sb[:, f % 2, :], ps[2 + f % 2][:, 0:CAP], bcur[:, 1, f:f + 1], LIMIT + 1.0,
                                    ALU.add, ALU.min).then_inc(gup_free, 1)
                    if f:
                        finish(f - 1)
                finish(KD - 1)
                dve.wait_ge(hid_ready, m * KD + KD)
                ch.settle()

            fills(0)
            with dve.Fori(0, E) as e:
                hidden(e, e)
                fills(e + 1)

            def again(e, c, nth, left):
                fills(nth + (E + 1))
                hidden(nth + E, e)

            overflow(dve, again)

            dve.wait_ge(g2_in, 64)
            ch.restart()
            link(v.tensor_tensor(gate2, gate2, badarow, ALU.add))
            link(v.tensor_tensor(gate2, gate2, gfrow, ALU.mult))

            def weighted_sum(j, i):
                yb = stage4(i)[0]
                dve.wait_ge(bias_done, j * NS + (i + 1))
                dve.wait_ge(y_in[i], j * 16 + 16)
                w = pcur4[:, i * TOPK:(i + 1) * TOPK]
                for c, bank in enumerate(bias_banks(i)):
                    last = v.scalar_tensor_tensor(out=yb[:, c * 512:(c + 1) * 512], in0=yb[:, c * 512:(c + 1) * 512],
                                                  scalar=w[:, 0:1], in1=bank[:, :], op0=ALU.mult, op1=ALU.add)
                last.then_inc(bias_read, 1)
                dve.wait_ge(bias_read, j * NS + (i + 1))
                for k in range(1, TOPK):
                    last = v.scalar_tensor_tensor(out=yb[:, 0:D], in0=yb[:, k * D:(k + 1) * D], scalar=w[:, k:k + 1],
                                                  in1=yb[:, 0:D], op0=ALU.mult, op1=ALU.add)
                    if k < TOPK - 1:
                        link(last)
                last.then_inc(f_ready, 1)

            def finish(j, i):
                yb, hb, ob = stage4(i)
                dve.wait_ge(fstat, j * NS + (i + 1))
                inverse(os_[:, 1, i:i + 1])
                dve.wait_ge(hb_in[i], j * 16 + 16)
                link(v.scalar_tensor_tensor(out=yb[:, 0:D], in0=yb[:, 0:D], scalar=os_[:, 1, i:i + 1], in1=gate2,
                                            op0=ALU.mult, op1=ALU.mult))
                dve.wait_ge(oslot_free[i], j + 1)
                v.tensor_tensor(ob, yb[:, 0:D], hb, ALU.add).then_inc(o_ready[i], 1)

            with dve.Fori(0, NT // NS) as j:
                ch.restart()
                link(v.tensor_copy(pcur4[:], probs[:, bass.ds(j * NS, NS), :].rearrange("p a k -> p (a k)")))
                v.tensor_copy(wcur, wden[:, bass.ds(j * NS, NS), :].rearrange("p a e -> p (a e)")).then_inc(wcur_ready, 1)
                dve.wait_ge(wdt_done, j + 1)
                v.tensor_copy(wdT, T0[0:E, :]).then_inc(wdT_ready, 1)
                for i in range(NS):
                    weighted_sum(j, i)
                    if i:
                        finish(j, i - 1)
                finish(j, NS - 1)


def kernel(**inputs):
    import numpy as np
    import concourse.bacc as bacc
    from concourse.bass_utils import run_bass_kernel_spmd as run

    nc = bacc.Bacc("TRN2", target_bir_lowering=False, num_devices=1)
    arrays, aps = {}, {}
    for name in inputs:
        array = np.ascontiguousarray(inputs[name])
        arrays["in_" + name] = array
        aps[name] = nc.dram_tensor("in_" + name, array.shape, mybir.dt.from_np(array.dtype), kind="ExternalInput").ap()
    out = nc.dram_tensor("out_h", (1, T, D), F32, kind="ExternalOutput").ap()
    hybrid_block(nc, aps, out)
    return run(nc, [arrays], core_ids=[0]).results[0]["out_h"]
```

```python
from contextlib import ExitStack

import concourse.bass as bass
from concourse import mybir

F32 = mybir.dt.float32
I32 = mybir.dt.int32
U32 = mybir.dt.uint32
ALU = mybir.AluOpType
ACT = mybir.ActivationFunctionType
AX_X = mybir.AxisListType.X

P = 128
D = 1024
KD = D // P
T = 1024
NT = T // P
DS = 512
SH, SHD = 8, 64
GH, GV = 4, 128
DK = 64
CH = 64
RANK = 16
DIN = 2576
E = 32
TOPK = 4
BLK = 3
CAP = BLK * P
NCHUNK = -(-T // CAP)
COLS = NCHUNK * BLK
TPITCH = 512
NCOL = (E + 1) * COLS
EMPTY = 1 << 20
NOVER = (NCHUNK - 1) * E
WIDTHS = [w for w in range(64, 304, 16) if w < CAP] + [CAP]
NS = 4
LIMIT = 7.0
ALPHA = 1.702
EPS = 1e-6
SPARE = KD * DIN


class Chain:

    def __init__(self, eng, sem):
        self.eng, self.sem, self.n = eng, sem, 0

    def restart(self):
        self.eng.sem_clear(self.sem)
        self.n = 0

    def settle(self):
        self.n += 1
        self.eng.sem_inc(self.sem, 1)
        self.eng.wait_ge(self.sem, self.n)

    def link(self, ins):
        self.n += 1
        ins.then_inc(self.sem, 1)
        self.eng.wait_ge(self.sem, self.n)


def hybrid_block(nc, a, out):
    ctx = ExitStack()
    with ctx:
        def sb(name, shape, dt=F32):
            return ctx.enter_context(nc.sbuf_tensor(name, shape, dt))

        def sem(name):
            return ctx.enter_context(nc.semaphore(name))

        def dram(name, shape, dt=F32):
            return nc.dram_tensor(name, shape, dt, kind="Internal").ap()

        h_dram = dram("h_dram", (T, D))
        n2_dram = dram("n2_dram", (T, D))
        y_dram = dram("y_dram", (T * TOPK, D))
        slot_dram = dram("slot_dram", (P * TPITCH, 1), I32)
        gate2_dram = dram("gate2_dram", (1, D))

        W = sb("W", [P, 6 * 4096])
        WO = sb("WO", [P, 8192])
        BIG = sb("BIG", [P, 6144])
        w_in = W[:, 0:SPARE].rearrange("p (k n) -> p k n", k=KD)
        pieces = [W[:, s * 4096:(s + 1) * 4096] for s in range(6)]
        spare_at = [SPARE]

        def spare(*shape):
            size = 1
            for n in shape:
                size *= n
            lo = spare_at[0]
            spare_at[0] = lo + size
            assert lo + size <= 6 * 4096
            v = W[:, lo:lo + size]
            if len(shape) == 2:
                v = v.rearrange("p (a b) -> p a b", a=shape[0])
            if len(shape) == 3:
                v = v.rearrange("p (a b c) -> p a b c", a=shape[0], b=shape[1])
            return v

        ada = [WO[:, s * 4096:(s + 1) * 4096].rearrange("p (k n) -> p k n", k=KD // 2) for s in range(2)]
        w_out = WO[:, :].rearrange("p (k n) -> p k n", k=KD)
        xg = WO[:, 0:BLK * D].rearrange("p (b d) -> p b d", b=BLK)
        xT = WO[:, BLK * D:2 * BLK * D].rearrange("p (k n) -> p k n", k=KD)
        g_sb = WO[:, 6144:6144 + 2 * CAP].rearrange("p (a n) -> p a n", a=2)
        u_sb = WO[:, 6144 + 2 * CAP:6144 + 4 * CAP].rearrange("p (a n) -> p a n", a=2)
        rows = BIG[:, 0:4096].rearrange("p (a j n) -> p a j n", a=2, j=4)
        acc = BIG[:, 2048:4096].rearrange("p (a n) -> p a n", a=2)
        nT = BIG[:, 4096:5120].rearrange("p (k n) -> p k n", k=KD)
        catT = BIG[:, 5120:6144].rearrange("p (k n) -> p k n", k=KD)
        yo = BIG[:, 0:BLK * D].rearrange("p (b d) -> p b d", b=BLK)
        hT = BIG[:, BLK * D:2 * BLK * D].rearrange("p (k n) -> p k n", k=KD)

        xh = sb("xh", [P, 3, D])
        xn = sb("xn", [P, D])
        hn = sb("hn", [P, D])
        gprow = hn[:]
        cat = sb("cat", [P, D])
        s_sb = cat[:, 0:2 * CAP].rearrange("p (a n) -> p a n", a=2)
        gate1 = sb("gate1", [P, D])
        gidx = xn[:, 0:NCOL].bitcast(I32)
        wsT = spare(SH, P)
        keep = spare(GH, P)
        vsq = spare(DS)
        Sm = spare(GH, P)
        state = spare(2, 2, P)
        zb = spare(2, P)
        az = spare(2, P)
        kdT = spare(2, P)
        osq = sb("osq", [P, DS])
        glT = sb("glT", [RANK, P])
        wgk = sb("wgk", [RANK, 2 * P])
        bgkT = sb("bgkT", [P, 2])
        bc = sb("bc", [P, 2, P])
        eb = sb("eb", [P, 2, P])
        enb = sb("enb", [P, 2, P])
        dec = sb("dec", [P, 2, P])
        qz = sb("qz", [P, 2, 2, P])
        ks = sb("ks", [P, 2, P])
        kdz = sb("kdz", [P, 2, 2 * P])
        gv_row = sb("gv_row", [P, DS])
        go_row = sb("go_row", [P, GV])
        bsT = sb("bsT", [P, SH])
        wr = sb("wr", [P, KD, E])
        br = sb("br", [P, E])
        ident = sb("ident", [P, P])
        ones = sb("ones", [P, P])
        before = sb("before", [P, P])
        reset = sb("reset", [P, 2 * P])
        ccol = sb("ccol", [P, KD])
        siluc = sb("siluc", [P, KD])
        badac = sb("badac", [P, 6, KD])
        gcol = sb("gcol", [P, 3, KD])
        mods = sb("mods", [P, 6, KD])
        B1, A1, _, B2, A2, G2 = (mods[:, m, :] for m in range(6))
        eps = sb("eps", [P, 1])
        xs = sb("xs", [P, 4])
        vs = sb("vs", [P, 3, SH])
        os_ = sb("os_", [P, 3, GH])
        ms = sb("ms", [P, 8])
        iotaE = sb("iotaE", [P, E])
        iotaEi = sb("iotaEi", [P, E], I32)
        vals = sb("vals", [P, NT, TOPK], I32)
        vcur = sb("vcur", [P, TOPK], I32)
        lg = sb("lg", [P, E])
        top8 = sb("top8", [P, 8])
        ti8 = sb("ti8", [P, 8], U32)
        tif = sb("tif", [P, TOPK])
        dif4 = sb("dif4", [P, TOPK])
        ex4 = sb("ex4", [P, TOPK])
        exsum = sb("exsum", [P, 2])
        oneh = sb("oneh", [P, TOPK, E])
        tmpk = sb("tmpk", [P, TOPK, E])
        chosen = sb("chosen", [P, E])
        csum = sb("csum", [P, E])
        cum = sb("cum", [P, E])
        rank = sb("rank", [P, TOPK])
        ranki = sb("ranki", [P, TOPK], I32)
        ia = sb("ia", [P, TOPK], I32)
        ib = sb("ib", [P, TOPK], I32)
        ic = sb("ic", [P, TOPK], I32)
        iab = sb("iab", [P, TOPK], I32)
        slot = sb("slot", [P, TOPK], I32)
        sslot = sb("sslot", [P, TOPK], I32)
        probs = sb("probs", [P, NT, TOPK])
        wden = sb("wden", [P, NT, E])
        pcur = sb("pcur", [P, TOPK])
        pcur4 = sb("pcur4", [P, NS * TOPK])
        bgT = sb("bgT", [P, E, KD])
        buT = sb("buT", [P, E, KD])
        bcur = sb("bcur", [P, 2, KD])
        sidx = sb("sidx", [P, NCOL], I32)
        scol = sb("scol", [P, BLK], I32)
        scur = sb("scur", [P, BLK], I32)
        gcur = sb("gcur", [P, BLK], I32)
        cnti = sb("cnti", [1, E + 1], I32)
        overn = sb("overn", [1, NOVER], I32)
        overo = sb("overo", [1, NOVER], I32)
        overf = osq[0:1, 0:3 * NOVER].rearrange("p (a n) -> p a n", a=3)
        overt = sb("overt", [1, 1], I32)

        ps = [ctx.enter_context(nc.psum_tensor(f"ps{i}", [P, 512], F32)) for i in range(8)]
        T0, T1, R0, R1, QK, ZB, SG, OB = ps
        TD = ps[4:8]
        DOWN_BANKS = ((ps[1], ps[3]), (ps[6], ps[7]), (ps[4], ps[5]))

        c_in = sem("c_in")
        x_loaded = sem("x_loaded")
        wout_in = sem("wout_in")
        h_stored = sem("h_stored")
        n2_stored = sem("n2_stored")
        pool_c = sem("pool_c")
        dve_c = sem("dve_c")
        sp_c = sem("sp_c")
        act_c = sem("act_c")
        const_ready = sem("const_ready")
        silu_ready = sem("silu_ready")
        ada_read = sem("ada_read")
        acc_ready = sem("acc_ready")
        sums_done = sem("sums_done")
        ada_evac = sem("ada_evac")
        gate2_ready = sem("gate2_ready")
        gate2_stored = sem("gate2_stored")
        rows_in = sem("rows_in")
        wst_done = sem("wst_done")
        wst_evac = sem("wst_evac")
        wst_masked = sem("wst_masked")
        xstat = sem("xstat")
        xn_ready = sem("xn_ready")
        xt_done = sem("xt_done")
        nT_ready = sem("nT_ready")
        u_done = sem("u_done")
        v_done = sem("v_done")
        vv_done = sem("vv_done")
        r_done = sem("r_done")
        glow_done = sem("glow_done")
        gu_ready = sem("gu_ready")
        gv_ready = sem("gv_ready")
        vv_ready = sem("vv_ready")
        sr_ready = sem("sr_ready")
        vsum_ready = sem("vsum_ready")
        vrstd_ready = sem("vrstd_ready")
        vh_ready = sem("vh_ready")
        gl_ready = sem("gl_ready")
        z_done = sem("z_done")
        z_ready = sem("z_ready")
        lnz_ready = sem("lnz_ready")
        bc_ready = sem("bc_ready")
        exp_ready = sem("exp_ready")
        qks_ready = sem("qks_ready")
        kdt_done = sem("kdt_done")
        kdz_ready = sem("kdz_ready")
        s_done = sem("s_done")
        sm_ready = sem("sm_ready")
        ds_done = sem("ds_done")
        st1_ready = sem("st1_ready")
        st0_ready = sem("st0_ready")
        sgu_done = sem("sgu_done")
        o_done = sem("o_done")
        osq_ready = sem("osq_ready")
        osum_ready = sem("osum_ready")
        orstd_ready = sem("orstd_ready")
        cat_ready = sem("cat_ready")
        catt_done = sem("catt_done")
        catTa = sem("catTa")
        catTd = sem("catTd")
        hn_free = sem("hn_free")
        mix_done = sem("mix_done")
        mstat = sem("mstat")
        h_ready = sem("h_ready")
        hstat = sem("hstat")
        n2_ready = sem("n2_ready")
        n2t_done = sem("n2t_done")
        n2T_ready = sem("n2T_ready")
        lg_done = sem("lg_done")
        dif_ready = sem("dif_ready")
        ex_ready = sem("ex_ready")
        chosen_ready = sem("chosen_ready")
        cum_done = sem("cum_done")
        slot_ready = sem("slot_ready")
        slot_free = sem("slot_free")
        cnt_done = sem("cnt_done")
        cnt_ready = sem("cnt_ready")
        table_in = sem("table_in")
        gidx_ready = sem("gidx_ready")
        psum_init = sem("psum_init")
        xgt_done = sem("xgt_done")
        xTa = sem("xTa")
        xTd = sem("xTd")
        gup_done = sem("gup_done")
        gup_free = sem("gup_free")
        g_ready = sem("g_ready")
        sig_ready = sem("sig_ready")
        hid_ready = sem("hid_ready")
        down_done = sem("down_done")
        yo_ready = sem("yo_ready")
        yo_free = sem("yo_free")
        moe_done = sem("moe_done")
        wcur_ready = sem("wcur_ready")
        wdt_done = sem("wdt_done")
        wdT_ready = sem("wdT_ready")
        bias_done = sem("bias_done")
        bias_read = sem("bias_read")
        f_ready = sem("f_ready")
        fstat = sem("fstat")
        g2_in = sem("g2_in")
        prefill_in = sem("prefill_in")
        ada_in = [sem(f"ada_in{i}") for i in range(2)]
        win_in = [sem(f"win_in{i}") for i in range(2)]
        scattered = [sem(f"scattered{k}") for k in range(TOPK)]
        piece_in = [sem(f"piece_in{s}") for s in range(6)]
        xg_in = [sem(f"xg_in{b}") for b in range(BLK)]
        y_stored = [sem(f"y_stored{b}") for b in range(BLK)]
        y_in = [sem(f"y_in{i}") for i in range(NS)]
        hb_in = [sem(f"hb_in{i}") for i in range(NS)]
        o_ready = [sem(f"o_ready{i}") for i in range(NS)]
        out_stored = [sem(f"out_stored{i}") for i in range(NS)]
        oslot_free = [sem(f"oslot_free{i}") for i in range(NS)]
        const_in = sem("const_in")
        N_CONST = 14

        MODS = (1, 0, 2, 3, 4, 5)
        ADA = [(m, half) for m in MODS for half in (0, 1)]
        EARLY = 4
        MOD_BANKS = (R0, R1, (R0, R1), SG, R0, R1)

        def x_rows(t):
            return a["x"][0, bass.ds(t * P, P), :]

        def xrow(t):
            return xh[:, bass.ds(t % 3, 1), :].rearrange("p a d -> p (a d)")

        def rowbuf(t, j):
            return rows[:, bass.ds(t % 2, 1), j, :].rearrange("p a n -> p (a n)")

        def stage4(i):
            lo = i * 6144
            return W[:, lo:lo + 4096], W[:, lo + 4096:lo + 5120], W[:, lo + 5120:lo + 6144]

        gate2 = gate1[:]
        junk4 = xh[:, 2, :]
        bdown = xh[0:E, 1, :]
        wdT = WO[0:E, 6144:6144 + NS * P]
        wcur = WO[:, 6144 + NS * P:6144 + NS * (P + E)]

        def bias_banks(i):
            return ((R0, R1), (T0, T1))[i % 2]

        def bcast_row(src, n):
            return src.rearrange("(o n) -> o n", o=1).broadcast_to((P, n))

        def overflow(eng, body):
            over = eng.value_load(overt[0:1, 0:1], min_val=0, max_val=NOVER)
            with eng.If(over > 0):
                with eng.Fori(0, NOVER) as j:
                    left = eng.value_load(overn[0:1, bass.ds(j, 1)], min_val=-T, max_val=T)
                    nth = eng.value_load(overo[0:1, bass.ds(j, 1)], min_val=0, max_val=NOVER)
                    with eng.If(left > 0):
                        body(j % E, j // E + 1, nth, left)

        block = ctx.enter_context(nc.Block())

        @block.sync
        def _(sp):
            def load_ada(n):
                m, half = ADA[n]
                if n >= 2:
                    sp.wait_ge(ada_read, n - 1)
                sp.dma_start(ada[n % 2], a["w_ada"][0].rearrange("(p k) n -> p k n", k=KD)[
                                 :, half * (KD // 2):(half + 1) * (KD // 2), m * D:(m + 1) * D]).then_inc(ada_in[n % 2], 16)

            def column(src):
                return src.rearrange("(p k) -> p k", k=KD)

            sp.dma_start(ccol[:], a["c"].rearrange("b (p k) -> p (b k)", k=KD)).then_inc(c_in, 16)
            for n in range(2):
                load_ada(n)
            sp.dma_start(xh[:, 0, :], x_rows(0)).then_inc(x_loaded, 16)
            for dst, src in (
                    (nT, a["w_s"][0].rearrange("h t s -> t h s")),
                    (xn[0:SH, 0:P], a["b_s"][0]),
                    (xn[0:2, P:2 * P], a["b_gk"][0].rearrange("(a p) -> a p", a=2)),
                    (cat[0:E, :], a["b_gate"][0]),
                    (xh[0:E, 1, :], a["b_up"][0]),
                    (badac[:], a["b_ada"][0].rearrange("(m p k) -> p m k", m=6, k=KD)),
                    (gcol[:, 0, :], column(a["g_pre_mix"][0])),
                    (gcol[:, 1, :], column(a["g_pre_ffn"][0])),
                    (gcol[:, 2, :], column(a["g_post_ffn"][0])),
                    (wgk[:], a["w_gk2"][0]),
                    (wr[:], a["w_router"][0].rearrange("(p k) e -> p k e", k=KD)),
                    (gv_row[:], bcast_row(a["g_sgu_v"][0], DS)),
                    (go_row[:], bcast_row(a["g_gla_out"][0], GV)),
                    (br[:], bcast_row(a["b_router"][0], E))):
                sp.dma_start(dst, src).then_inc(const_in, 16)
            for n in range(2, EARLY):
                load_ada(n)
            w_in_v = a["w_in"][0].rearrange("(p k) n -> p k n", k=KD)
            for j, (lo, hi) in enumerate(((0, D), (D, DIN))):
                sp.dma_start(w_in[:, :, lo:hi], w_in_v[:, :, lo:hi]).then_inc(win_in[j], 16)
            sp.wait_ge(wst_evac, 2)
            for t in (1, 2):
                sp.wait_ge(x_loaded, 16 * t)
                sp.dma_start(xh[:, t, :], x_rows(t)).then_inc(x_loaded, 16)
            for dst, src in ((gate1[:], a["b_ada"][0, 2 * D:3 * D]), (gprow, a["g_post_mix"][0])):
                sp.dma_start(dst, bcast_row(src, D)).then_inc(rows_in, 16)
            for n in range(EARLY, len(ADA)):
                load_ada(n)
            sp.wait_ge(ada_read, len(ADA))
            sp.dma_start(w_out, a["w_out"][0].rearrange("(k p) n -> p k n", p=P)).then_inc(wout_in, 16)
            sp.wait_ge(gate2_ready, 1)
            sp.dma_start(column(gate2_dram[0]), G2).then_inc(gate2_stored, 16)

            ch = Chain(sp, sp_c)

            def store(t):
                ch.restart()
                sp.wait_ge(h_ready, t + 1)
                ch.settle()
                sp.dma_start(h_dram[bass.ds(t * P, P), :], xrow(t)).then_inc(h_stored, 16)
                sp.wait_ge(n2_ready, t + 1)
                sp.dma_start(n2_dram[bass.ds(t * P, P), :], hn[:]).then_inc(n2_stored, 16)
                sp.wait_ge(n2_stored, t * 16 + 16)
                sp.sem_inc(hn_free, 1)

            sp.sem_inc(hn_free, 1)
            with sp.Fori(0, NT - 3) as t:
                store(t)
                sp.wait_ge(h_stored, t * 16 + 16)
                ch.settle()
                sp.wait_ge(x_loaded, t * 16 + 48)
                ch.settle()
                sp.dma_start(xrow(t), x_rows(t + 3)).then_inc(x_loaded, 16)
            for t in range(NT - 3, NT - 1):
                store(t)

            def load_expert(e, n):
                gate, up, down = (a[w][0, bass.ds(e, 1), :, :] for w in ("w_gate", "w_up", "w_down"))
                for s in range(6):
                    if n is not None:
                        if s < 2:
                            sp.wait_ge(gup_done, n * KD - 4)
                        elif s < 4:
                            sp.wait_ge(gup_done, n * KD)
                        else:
                            sp.wait_ge(down_done, n * BLK)
                    elif s == 5:
                        store(NT - 1)
                        sp.wait_ge(cat_ready, NT)
                        sp.wait_ge(h_stored, 16 * NT)
                    if s < 4:
                        src = (gate if s % 2 == 0 else up).rearrange("e (p k) f -> p (e k) f", k=KD)[
                            :, :, (s // 2) * 512:(s // 2) * 512 + 512]
                        dst = pieces[s].rearrange("p (k f) -> p k f", k=KD)
                    else:
                        src = down.rearrange("e (k p) d -> p (e k) d", p=P)[:, (s - 4) * 4:(s - 4) * 4 + 4, :]
                        dst = pieces[s].rearrange("p (k f) -> p k f", k=4)
                    sp.dma_start(dst, src).then_inc(piece_in[s], 16)

            sp.wait_ge(glow_done, NT)
            load_expert(0, None)
            sp.wait_ge(gate2_stored, 16)
            for dst, src in ((gate2, bcast_row(gate2_dram[0], D)),
                             (bdown, a["b_down"][0])):
                sp.dma_start(dst, src).then_inc(g2_in, 16)
            with sp.Fori(1, E) as e:
                load_expert(e, e)

            sp.wait_ge(cnt_ready, 1)
            overflow(sp, lambda e, c, nth, left: load_expert(e, nth + E))

            sp.wait_ge(moe_done, 1)
            def load_y(t, i):
                yb, hb, _ = stage4(i)
                sp.dma_start(yb, y_dram.rearrange("(t k) d -> t (k d)", k=TOPK)[bass.ds(t * P, P), :]
                             ).then_inc(y_in[i], 16)
                sp.dma_start(hb, h_dram[bass.ds(t * P, P), :]).then_inc(hb_in[i], 16)

            def store_out(j, i):
                sp.wait_ge(o_ready[i], j + 1)
                sp.dma_start(out[0, (j * NS + i) * P:(j * NS + i + 1) * P, :], stage4(i)[2]).then_inc(out_stored[i], 16)

            for i in range(NS):
                load_y(i, i)
                sp.sem_inc(oslot_free[i], 1)
            for j in range(NT // NS):
                for i in range(NS):
                    store_out(j, i)
                    if j < NT // NS - 1:
                        load_y((j + 1) * NS + i, i)
                for i in range(NS):
                    sp.wait_ge(out_stored[i], (j + 1) * 16)
                    sp.sem_inc(oslot_free[i], 1)

        @block.gpsimd
        def _(pool):
            ch = Chain(pool, pool_c)
            link = ch.link
            g = nc.gpsimd
            link(g.memset(ident[:], 0.0))
            link(g.affine_select(out=ident[:], in_=ident[:], compare_op=ALU.not_equal, fill=1.0, base=0,
                                 pattern=[[-1, P]], channel_multiplier=1))
            link(g.memset(ones[:], 1.0))
            link(g.memset(before[:], 1.0))
            link(g.affine_select(out=before[:], in_=before[:], compare_op=ALU.is_ge, fill=0.0, base=-1,
                                 pattern=[[1, P]], channel_multiplier=-1))
            link(g.memset(keep, 1.0))
            link(g.affine_select(out=keep, in_=keep, compare_op=ALU.is_ge, fill=0.0, base=0,
                                 pattern=[[0, GH], [1, P]], channel_multiplier=-1))
            link(g.memset(keep[0:CH, :, CH:P], 0.0))
            link(g.memset(reset[:], 1.0))
            for c in range(4):
                link(g.memset(reset[:, c * CH:c * CH + 1], 0.0))
            for z in (qz[:], kdz[:], Sm, state, csum[:]):
                link(g.memset(z, 0.0))
            link(g.memset(eps[:], EPS))
            link(g.iota(iotaEi[:], pattern=[[1, E]], base=0, channel_multiplier=0))
            link(g.tensor_copy(iotaE[:], iotaEi[:]))
            link(g.iota(vals[:], pattern=[[P * TOPK, NT], [1, TOPK]], base=0, channel_multiplier=TOPK))
            link(g.memset(sidx[:], EMPTY))
            pool.sem_inc(slot_free, 1)
            pool.sem_inc(const_ready, 1)
            slots = slot_dram.rearrange("(p c) o -> p (c o)", p=P)[:, 0:NCOL]
            g.dma_start(slots, sidx[:]).then_inc(prefill_in, 16)
            pool.wait_ge(wst_evac, 1)
            g.affine_select(out=wsT, in_=wsT, compare_op=ALU.is_ge, fill=0.0, base=0,
                            pattern=[[0, SH], [1, P]], channel_multiplier=-1).then_inc(wst_masked, 1)
            pool.wait_ge(prefill_in, 16)

            with pool.Fori(0, NT) as t:
                ch.restart()
                pool.wait_ge(slot_ready, t + 1)
                ch.settle()
                link(g.tensor_copy(sslot[:], slot[:]))
                for k in range(TOPK):
                    g.indirect_dma_start(out=slot_dram[:, :], out_offset=bass.IndirectOffsetOnAxis(ap=sslot[:, k:k + 1], axis=0),
                                         in_=vcur[:, k:k + 1], in_offset=None,
                                         bounds_check=P * TPITCH - 1, oob_is_err=False).then_inc(scattered[k], 16)
                for k in range(TOPK):
                    pool.wait_ge(scattered[k], t * 16 + 16)
                pool.sem_inc(slot_free, 1)

            g.dma_start(sidx[:], slots).then_inc(table_in, 16)
            pool.wait_ge(gidx_ready, 1)
            pool.wait_ge(cnt_ready, 1)
            pool.wait_ge(n2_stored, 16 * NT)
            pool.wait_ge(mix_done, NT)

            def gather(col):
                link(g.tensor_copy(gcur[:], gidx[:, bass.ds(col, BLK)]))
                for b in range(BLK):
                    g.indirect_dma_start(out=xg[:, b, :], out_offset=None, in_=n2_dram[:, :],
                                         in_offset=bass.IndirectOffsetOnAxis(ap=gcur[:, b:b + 1], axis=0),
                                         bounds_check=T - 1, oob_is_err=False).then_inc(xg_in[b], 16)

            def scatter(col, m):
                link(g.tensor_copy(scol[:], sidx[:, bass.ds(col, BLK)]))
                pool.wait_ge(yo_ready, m * BLK + 2 * BLK)
                ch.settle()
                link(g.tensor_copy(scur[:], scol[:]))
                for b in range(BLK):
                    g.indirect_dma_start(out=y_dram[:, :], out_offset=bass.IndirectOffsetOnAxis(ap=scur[:, b:b + 1], axis=0),
                                         in_=yo[:, b, :], in_offset=None,
                                         bounds_check=T * TOPK - 1, oob_is_err=False).then_inc(y_stored[b], 16)
                for b in range(BLK):
                    pool.wait_ge(y_stored[b], m * 16 + 16)
                pool.sem_inc(yo_free, 1)

            def gather_next(e):
                pool.wait_ge(xgt_done, e * (2 * BLK) + 2 * BLK)
                for b in range(BLK):
                    pool.wait_ge(xg_in[b], e * 16 + 16)
                ch.settle()
                gather(e * COLS + COLS)

            ch.restart()
            link(g.memset(xg, 0.0))
            gather(0)
            pool.sem_inc(yo_free, 1)
            gather_next(0)
            with pool.Fori(1, E) as e:
                ch.restart()
                gather_next(e)
                scatter(e * COLS - COLS, e - 1)
            scatter((E - 1) * COLS, E - 1)

            def again(e, c, nth, left):
                ch.restart()
                pool.wait_ge(xgt_done, nth * (2 * BLK) + (E + 1) * 2 * BLK)
                for b in range(BLK):
                    pool.wait_ge(xg_in[b], nth * 16 + (E + 1) * 16)
                ch.settle()
                gather(e * COLS + c * BLK)
                scatter(e * COLS + c * BLK, nth + E)

            overflow(pool, again)
            for b in range(BLK):
                pool.wait_ge(xg_in[b], 16 * (E + 1))
            pool.sem_inc(moe_done, 1)

        @block.tensor
        def _(pe):
            mm, tr = nc.tensor.matmul, nc.tensor.transpose

            def four(bank, src, k0=0):
                for k in range(4):
                    last = tr(bank[:, k * P:(k + 1) * P], src(k0 + k), ident[:])
                return last

            def by_k(buf):
                v = buf.rearrange("p (q k) -> p k q", k=KD)
                return lambda k: v[:, k, :]

            def modulation(o):
                pe.wait_ge(acc_ready, o + 1)
                part = acc[:, o % 2, :]
                if MODS[o] == 2:
                    pe.wait_ge(ada_evac, 2)
                    for c, bank in ((0, R0), (1, R1)):
                        last = mm(bank[:, :], ones[:], part[:, c * 512:(c + 1) * 512], start=True, stop=True)
                else:
                    if o > 3:
                        pe.wait_ge(ada_evac, 3)
                    columns = part.rearrange("p (q j) -> p j q", j=KD)
                    for j in range(KD):
                        last = mm(MOD_BANKS[o][:, j:j + 1], columns[:, j, :], ones[:, 0:1], start=True, stop=True)
                last.then_inc(sums_done, 1)

            def project_rows(bank, lo, done, n=None):
                for k in range(KD):
                    if n is not None and k % 4 == 0:
                        pe.wait_ge(nT_ready, n + k // 4)
                    last = mm(bank[:, :], nT[:, k, :], w_in[:, k, lo:lo + 512], start=(k == 0), stop=(k == KD - 1))
                last.then_inc(done, 1)

            def project_T():
                for j in range(4):
                    for k in range(KD):
                        last = mm(QK[:, j * P:(j + 1) * P], w_in[:, k, D + j * P:D + (j + 1) * P], nT[:, k, :],
                                  start=(k == 0), stop=(k == KD - 1))
                for k in range(KD):
                    last = mm(ZB[0:RANK, 0:P], w_in[:, k, DIN - RANK:DIN], nT[:, k, :], start=(k == 0), stop=(k == KD - 1))
                last.then_inc(glow_done, 1)

            def transpose_x(t):
                pe.wait_ge(xn_ready, t + 1)
                four(T0, by_k(xn[:])).then_inc(xt_done, 1)
                four(T1, by_k(xn[:]), 4).then_inc(xt_done, 1)

            pe.wait_ge(const_ready, 1)
            pe.wait_ge(const_in, 16 * N_CONST)
            four(T0, lambda k: nT[:, k, :])
            four(T1, lambda k: nT[:, k, :], 4).then_inc(wst_done, 1)
            pe.wait_ge(wst_evac, 1)
            tr(T0[:, 0:SH], xn[0:SH, 0:P], ident[0:SH, 0:SH])
            tr(T0[:, 16:18], xn[0:2, P:2 * P], ident[0:2, 0:2])
            for k in range(KD):
                tr(T0[:, 64 + k * E:64 + (k + 1) * E], cat[0:E, k * P:(k + 1) * P], ident[0:E, 0:E])
            for k in range(KD):
                last = tr(T1[:, 64 + k * E:64 + (k + 1) * E], xh[0:E, 1, k * P:(k + 1) * P], ident[0:E, 0:E])
            last.then_inc(wst_done, 1)
            modulation(0)
            modulation(1)
            transpose_x(0)
            pe.wait_ge(nT_ready, 2)
            pe.wait_ge(win_in[0], 16)
            project_rows(OB, 0, u_done)
            project_rows(T1, 512, v_done)
            pe.wait_ge(win_in[1], 16)
            pe.wait_ge(gu_ready, 1)
            project_rows(OB, 1536, vv_done)
            pe.wait_ge(gv_ready, 1)
            project_rows(T1, 2048, r_done)
            project_T()
            for o in range(2, len(MODS)):
                modulation(o)
            pe.wait_ge(ada_evac, len(MODS))
            pe.wait_ge(wst_masked, 1)
            pe.wait_ge(vv_ready, 1)
            pe.wait_ge(sr_ready, 1)

            def tile(t, back, ahead):
                def value(h):
                    return rows[:, bass.ds(t % 2, 1), 2, h * GV:(h + 1) * GV].rearrange("p a n -> p (a n)")

                pe.wait_ge(gl_ready, t + 1)
                if ahead:
                    transpose_x(t + 1)
                for j in range(2):
                    last = mm(ZB[:, P + j * P:P + (j + 1) * P], wgk[:, j * P:(j + 1) * P], glT[:], start=True, stop=True)
                last.then_inc(z_done, 1)
                if ahead:
                    project_rows(SG, 0, u_done, t * 2 + 3)
                if back:
                    transpose_n2(t - 1)
                if ahead:
                    project_rows(R1, 512, v_done)
                if back:
                    pe.wait_ge(z_ready, t + 1)
                    logits(t - 1)
                pe.wait_ge(qks_ready, t + 1)
                for j in range(2):
                    last = tr(T0[:, j * P:(j + 1) * P], kdT[:, j, :], ident[:])
                last.then_inc(kdt_done, 1)
                for h in range(GH):
                    last = mm(OB[:, h * P:(h + 1) * P], ks[:, h // 2, :], qz[:, h % 2, h // 2, :], start=True, stop=True)
                last.then_inc(s_done, 1)
                if ahead:
                    pe.wait_ge(gu_ready, t + 2)
                pe.wait_ge(vh_ready, t + 1)
                for h in range(SH):
                    last = mm(SG[:, h * SHD:(h + 1) * SHD], wsT[:, h, :],
                              rows[:, bass.ds(t % 2, 1), 1, h * SHD:(h + 1) * SHD].rearrange("p a n -> p (a n)"),
                              start=True, stop=True)
                last.then_inc(sgu_done, 1)
                pe.wait_ge(kdz_ready, t + 1)
                for c, bank in ((0, T1), (1, ZB)):
                    for h in range(GH):
                        last = mm(bank[:, h * P:(h + 1) * P], kdz[:, c, (h // 2) * P:(h // 2 + 1) * P],
                                  value(h), start=True, stop=True)
                last.then_inc(ds_done, 1)
                if ahead:
                    project_rows(R0, 1536, vv_done)
                pe.wait_ge(sm_ready, t + 1)
                if back:
                    ranks(t - 1)
                pe.wait_ge(st1_ready, t + 1)
                for h in range(GH):
                    mm(QK[:, h * GV:(h + 1) * GV], Sm[:, h, :], value(h), start=True, stop=False, skip_group_check=True)
                    for c in range(2):
                        last = mm(QK[c * CH:(c + 1) * CH, h * GV:(h + 1) * GV], qz[:, h % 2, h // 2, c * CH:(c + 1) * CH],
                                  state[:, c, h // 2, :], start=False, stop=(c == 1), skip_group_check=True)
                last.then_inc(o_done, 1)
                if ahead:
                    pe.wait_ge(gv_ready, t + 2)
                    project_rows(R1, 2048, r_done)
                pe.wait_ge(cat_ready, t + 1)
                four(T0, lambda k: cat[:, k * P:(k + 1) * P]).then_inc(catt_done, 1)
                four(T1, lambda k: cat[:, k * P:(k + 1) * P], 4).then_inc(catt_done, 1)
                if ahead:
                    pe.wait_ge(vv_ready, t + 2)
                if not back:
                    pe.wait_ge(wout_in, 16)
                pe.wait_ge(catTd, t + 1)
                for k0, ready in ((0, None), (4, catTa)):
                    for j, bank in ((0, R0), (1, R1)):
                        if ahead and k0 == 0 and j == 1:
                            pe.wait_ge(sr_ready, t + 2)
                        if ready is not None and j == 0:
                            pe.wait_ge(ready, t + 1)
                        for k in range(k0, k0 + 4):
                            last = mm(bank[:, :], catT[:, k, :], w_out[:, k, j * 512:(j + 1) * 512],
                                      start=(k == 0), stop=(k == KD - 1), skip_group_check=True)
                last.then_inc(mix_done, 1)
                if ahead:
                    pe.wait_ge(st0_ready, t + 1)
                    project_T()

            def transpose_n2(t):
                pe.wait_ge(n2_ready, t + 1)
                four(T0, by_k(hn[:]))
                four(T1, by_k(hn[:]), 4).then_inc(n2t_done, 1)

            def logits(t):
                pe.wait_ge(n2T_ready, t * 2 + 2)
                for k in range(KD):
                    last = mm(ZB[:, 0:E], catT[:, k, :], wr[:, k, :], start=(k == 0), stop=(k == KD - 1))
                last.then_inc(lg_done, 1)

            def ranks(t):
                pe.wait_ge(chosen_ready, t + 1)
                mm(OB[:, 0:E], before[:], chosen[:], start=True, stop=False)
                mm(OB[:, 0:E], ones[:], csum[:], start=False, stop=True).then_inc(cum_done, 1)

            tile(0, False, 2)
            with pe.Fori(1, NT - 2) as t:
                tile(t, True, 2)
            tile(NT - 2, True, 1)
            tile(NT - 1, True, 0)
            transpose_n2(NT - 1)
            pe.wait_ge(st0_ready, NT)
            logits(NT - 1)
            ranks(NT - 1)
            pe.wait_ge(slot_ready, NT)
            mm(OB[:, 0:E], ones[:], csum[:], start=True, stop=True).then_inc(cnt_done, 1)

            def transpose_rows(m, cnt, passes):
                pe.wait_ge(gup_free, passes * KD + 1)
                for b in range(BLK):
                    def full():
                        if b == 2:
                            pe.wait_ge(xTa, m * BLK + 1)
                            pe.wait_ge(xTd, m * BLK + 1)
                        pe.wait_ge(xg_in[b], m * 16 + 16)
                        for half in range(2):
                            four(TD[(2 * b + half) % 4], by_k(xg[:, b, :]), 4 * half).then_inc(xgt_done, 1)

                    if b == 0:
                        full()
                    else:
                        with pe.If(cnt > b * P):
                            full()
                        with pe.Else():
                            for half in range(2):
                                mm(ps[0][:, 0:64], ident[:], ident[:, 0:64], start=True, stop=True).then_inc(xgt_done, 1)

            def gate_up(m, width):
                for f in range(KD):
                    s = f // 4 * 2
                    if f % 4 == 0:
                        pe.wait_ge(piece_in[s], m * 16 + 16)
                        pe.wait_ge(piece_in[s + 1], m * 16 + 16)
                    pe.wait_ge(gup_free, m * KD + (f + 1))
                    if f == 1:
                        pe.wait_ge(yo_ready, m * BLK + 1)
                    for piece, bank in ((pieces[s], ps[f % 2]), (pieces[s + 1], ps[2 + f % 2])):
                        w = piece.rearrange("p (k f) -> p k f", k=KD)
                        for k in range(KD):
                            last = mm(bank[:, 0:width], w[:, k, (f % 4) * P:(f % 4 + 1) * P], xT[:, k, 0:width],
                                      start=(k == 0), stop=(k == KD - 1))
                    last.then_inc(gup_done, 1)

            def gate_up_by_count(m, cnt, widths=WIDTHS):
                if len(widths) == 1:
                    gate_up(m, widths[0])
                else:
                    mid = len(widths) // 2
                    with pe.If(cnt <= widths[mid - 1]):
                        gate_up_by_count(m, cnt, widths[:mid])
                    with pe.Else():
                        gate_up_by_count(m, cnt, widths[mid:])

            def down(m, cnt):
                pe.wait_ge(piece_in[4], m * 16 + 16)
                pe.wait_ge(piece_in[5], m * 16 + 16)
                pe.wait_ge(gup_free, m * KD + (KD + 2))
                for b in range(BLK):
                    def full():
                        if b:
                            pe.wait_ge(xTa, m * BLK + (BLK + b + 1))
                            pe.wait_ge(xTd, m * BLK + (BLK + b + 1))
                        for t in range(KD):
                            if b == 0:
                                pe.wait_ge(hid_ready, m * KD + (t + 1))
                            w = pieces[4 + t // 4].rearrange("p (k f) -> p k f", k=4)
                            for j, bank in enumerate(DOWN_BANKS[b]):
                                last = mm(bank[:, :], hT[:, t, b * P:(b + 1) * P], w[:, t % 4, j * 512:(j + 1) * 512],
                                          start=(t == 0), stop=(t == KD - 1))
                        last.then_inc(down_done, 1)

                    if b == 0:
                        full()
                    else:
                        with pe.If(cnt > b * P):
                            full()
                        with pe.Else():
                            mm(ps[0][:, 0:64], ident[:], ident[:, 0:64], start=True, stop=True).then_inc(down_done, 1)

            def one_pass(m, cnt, following):
                pe.wait_ge(xTa, m * BLK + BLK)
                pe.wait_ge(xTd, m * BLK + BLK)
                gate_up_by_count(m, cnt)
                pe.wait_ge(yo_ready, m * BLK + BLK)
                transpose_rows(m + 1, following, m + 1)
                down(m, cnt)

            pe.wait_ge(cnt_ready, 1)
            pe.wait_ge(psum_init, 1)
            transpose_rows(0, pe.value_load(cnti[0:1, 0:1], min_val=0, max_val=T), 0)
            with pe.Fori(0, E) as e:
                cnt = pe.value_load(cnti[0:1, bass.ds(e, 1)], min_val=0, max_val=T)
                following = pe.value_load(cnti[0:1, bass.ds(e + 1, 1)], min_val=0, max_val=T)
                one_pass(e, cnt, following)

            def again(e, c, nth, left):
                pe.wait_ge(yo_ready, nth * BLK + (E * BLK + BLK))
                pe.wait_ge(xTa, nth * BLK + (E + 1) * BLK)
                pe.wait_ge(xTd, nth * BLK + (E + 1) * BLK)
                transpose_rows(nth + (E + 1), left, nth + E)
                pe.wait_ge(xTa, nth * BLK + (E + 2) * BLK)
                pe.wait_ge(xTd, nth * BLK + (E + 2) * BLK)
                gate_up_by_count(nth + E, left, WIDTHS[4::4] + [CAP])
                down(nth + E, left)

            overflow(pe, again)

            pe.wait_ge(g2_in, 32)
            with pe.Fori(0, NT // NS) as j:
                pe.wait_ge(wcur_ready, j + 1)
                for i in range(NS):
                    last = tr(T0[0:E, i * P:(i + 1) * P], wcur[:, i * E:(i + 1) * E], ident[:])
                last.then_inc(wdt_done, 1)
                pe.wait_ge(wdT_ready, j + 1)
                pe.wait_ge(moe_done, 1)
                for i in range(NS):
                    if i >= 2:
                        pe.wait_ge(bias_read, j * NS + (i - 1))
                    for c, bank in enumerate(bias_banks(i)):
                        last = mm(bank[:, :], wdT[:, i * P:(i + 1) * P], bdown[:, c * 512:(c + 1) * 512], start=True, stop=True)
                    last.then_inc(bias_done, 1)

        @block.scalar
        def _(act):
            ch = Chain(act, act_c)
            link = ch.link
            A = nc.scalar.activation

            def root(dst, src, n, done):
                A(dst, src, ACT.Sqrt, bias=eps[:, 0:1], scale=1.0 / n).then_inc(done, 1)

            def x_stats(t):
                act.wait_ge(x_loaded, t * 16 + 16)
                act.wait_ge(xt_done, t * 2)
                link(A(xn[:], xrow(t), ACT.Square, accum_out=xs[:, 0:1]))
                root(xs[:, 1:2], xs[:, 0:1], D, xstat)

            def gelu_uv(t, u, v):
                act.wait_ge(u_done, t + 1)
                A(rowbuf(t, 0), u[:, :], ACT.Gelu_apprx_tanh).then_inc(gu_ready, 1)
                act.wait_ge(v_done, t + 1)
                A(rowbuf(t, 1), v[:, :], ACT.Gelu_apprx_tanh).then_inc(gv_ready, 1)

            def v_root(t):
                act.wait_ge(vsum_ready, t + 1)
                root(vs[:, 1, :], vs[:, 0, :], SHD, vrstd_ready)

            def copy_value(t, bank):
                act.wait_ge(vv_done, t + 1)
                A(rowbuf(t, 2), bank[:, :], ACT.Copy).then_inc(vv_ready, 1)

            def silu_r(t, bank):
                act.wait_ge(r_done, t + 1)
                A(rowbuf(t, 3), bank[:, :], ACT.Silu).then_inc(sr_ready, 1)

            def copy_glow(t):
                act.wait_ge(glow_done, t + 1)
                A(glT[:], ZB[0:RANK, 0:P], ACT.Copy).then_inc(gl_ready, 1)

            act.sem_inc(yo_ready, BLK)
            act.wait_ge(c_in, 16)
            A(siluc[:], ccol[:], ACT.Silu).then_inc(silu_ready, 1)
            act.wait_ge(const_ready, 1)
            act.wait_ge(x_loaded, 16)
            act.wait_ge(wst_evac, 2)
            link(A(xn[:], xrow(0), ACT.Square, accum_out=xs[:, 0:1]))
            root(xs[:, 1:2], xs[:, 0:1], D, xstat)
            gelu_uv(0, OB, T1)
            v_root(0)
            x_stats(1)
            copy_value(0, OB)
            silu_r(0, T1)
            copy_glow(0)

            def tile(t, back, ahead):
                ch.restart()
                act.wait_ge(z_ready, t + 1)
                link(A(az, zb, ACT.Abs))
                link(A(az, az, ACT.Exp, scale=-1.0))
                A(az, az, ACT.Ln, bias=1.0).then_inc(lnz_ready, 1)
                act.wait_ge(bc_ready, t + 1)
                A(eb[:], bc[:], ACT.Exp, scale=1.0 / 16)
                A(enb[:], bc[:], ACT.Exp, scale=-1.0 / 16)
                A(dec[:], zb, ACT.Exp, scale=-1.0 / 16).then_inc(exp_ready, 1)
                if ahead:
                    gelu_uv(t + 1, SG, R1)
                if back:
                    exps(t - 1)
                if ahead:
                    v_root(t + 1)
                    copy_value(t + 1, R0)
                act.wait_ge(o_done, t + 1)
                A(osq[:], QK[:, :], ACT.Square).then_inc(osq_ready, 1)
                act.wait_ge(osum_ready, t + 1)
                root(os_[:, 1, :], os_[:, 0, :], GV, orstd_ready)
                if ahead:
                    silu_r(t + 1, R1)
                if ahead == 2:
                    x_stats(t + 2)
                act.wait_ge(catt_done, t * 2 + 2)
                A(catT[:, 4:8, :], T1[:, :].rearrange("p (k n) -> p k n", k=4), ACT.Copy).then_inc(catTa, 1)
                act.wait_ge(mix_done, t + 1)
                link(A(osq[:], R0[:, :], ACT.Square, accum_out=ms[:, 0:1]))
                link(A(osq[:], R1[:, :], ACT.Square, accum_out=ms[:, 1:2]))
                link(A(ms[:, 2:3], ms[:, 0:1], ACT.Identity, bias=ms[:, 1:2]))
                root(ms[:, 3:4], ms[:, 2:3], D, mstat)
                act.wait_ge(h_ready, t + 1)
                link(A(cat[:], xrow(t), ACT.Square, accum_out=ms[:, 4:5]))
                root(ms[:, 5:6], ms[:, 4:5], D, hstat)
                if ahead:
                    copy_glow(t + 1)

            def exps(t):
                act.wait_ge(dif_ready, t + 1)
                A(ex4[:], dif4[:], ACT.Exp, accum_out=exsum[:, 0:1]).then_inc(ex_ready, 1)

            tile(0, False, 2)
            with act.Fori(1, NT - 2) as t:
                tile(t, True, 2)
            tile(NT - 2, True, 1)
            tile(NT - 1, True, 0)
            exps(NT - 1)

            def fills(m):
                for b in range(BLK):
                    act.wait_ge(xgt_done, m * (2 * BLK) + (2 * b + 1))
                    for k in range(4):
                        last = A(xT[:, k, b * P:(b + 1) * P], TD[2 * b % 4][:, k * P:(k + 1) * P], ACT.Identity,
                                 bias=B2[:, k:k + 1], scale=A2[:, k:k + 1])
                    last.then_inc(xTa, 1)

            def sigmoids(m):
                for f in range(KD):
                    act.wait_ge(g_ready, m * KD + (f + 1))
                    A(s_sb[:, f % 2, :], g_sb[:, f % 2, :], ACT.Sigmoid, scale=ALPHA).then_inc(sig_ready, 1)

            def down_rows(m):
                act.wait_ge(yo_free, m + 1)
                for b in range(BLK):
                    lo, hi = DOWN_BANKS[b]
                    if b:
                        act.wait_ge(xTd, m * BLK + (BLK + b + 1))
                    act.wait_ge(down_done, m * BLK + (b + 1))
                    A(yo[:, b, 0:512], lo[:, :], ACT.Copy)
                    A(yo[:, b, 512:D], hi[:, :], ACT.Copy).then_inc(yo_ready, 1)

            act.wait_ge(cnt_ready, 1)
            act.wait_ge(psum_init, 1)
            fills(0)
            with act.Fori(0, E) as e:
                sigmoids(e)
                fills(e + 1)
                down_rows(e)

            def again(e, c, nth, left):
                fills(nth + (E + 1))
                sigmoids(nth + E)
                down_rows(nth + E)

            overflow(act, again)

            act.wait_ge(g2_in, 32)
            with act.Fori(0, NT // NS) as j:
                ch.restart()
                for i in range(NS):
                    act.wait_ge(f_ready, j * NS + (i + 1))
                    link(A(junk4, stage4(i)[0][:, 0:D], ACT.Square, accum_out=os_[:, 0, i:i + 1]))
                    root(os_[:, 1, i:i + 1], os_[:, 0, i:i + 1], D, fstat)

        @block.vector
        def _(dve):
            ch = Chain(dve, dve_c)
            link = ch.link
            v = nc.vector

            def b3(src, n):
                return src.unsqueeze(2).broadcast_to((P, src.shape[1], n))

            def inverse(dst):
                link(v.reciprocal(dst, dst))

            def normed_x(t):
                dve.wait_ge(xstat, t + 1)
                inverse(xs[:, 1:2])
                v.tensor_scalar(xn[:], xrow(t), xs[:, 1:2], None, ALU.mult).then_inc(xn_ready, 1)

            def modulate(dst, A_, B_, done, wait_half):
                for k in range(KD):
                    if k % 4 == 0:
                        wait_half(k // 4)
                    bank = (T0, T1)[k // 4]
                    last = v.tensor_scalar(dst[:, k, :], bank[:, (k % 4) * P:(k % 4 + 1) * P], A_[:, k:k + 1], B_[:, k:k + 1],
                                           ALU.mult, ALU.add)
                    if k % 4 == 3:
                        last.then_inc(done, 1)

            def next_nT(t):
                modulate(nT, A1, B1, nT_ready, lambda half: dve.wait_ge(xt_done, t * 2 + (half + 1)))

            def v_squares(t):
                dve.wait_ge(gv_ready, t + 1)
                link(v.tensor_tensor(vsq, rowbuf(t, 1), rowbuf(t, 1), ALU.mult))
                v.tensor_reduce(vs[:, 0, :], vsq.rearrange("p (h d) -> p h d", h=SH), AX_X, ALU.add).then_inc(vsum_ready, 1)

            def v_norm(t):
                dve.wait_ge(vrstd_ready, t + 1)
                inverse(vs[:, 1, :])
                r = rowbuf(t, 1)
                r3 = r.rearrange("p (h d) -> p h d", h=SH)
                link(v.tensor_tensor(r3, r3, b3(vs[:, 1, :], SHD), ALU.mult))
                v.tensor_tensor(r, r, gv_row[:], ALU.mult).then_inc(vh_ready, 1)

            def decay_state(src, dst, bank, at):
                for h in range(GH):
                    lo, j = (h % 2) * DK, h // 2
                    last = v.scalar_tensor_tensor(out=state[lo:lo + DK, dst, j, :], in0=state[lo:lo + DK, src, j, :],
                                                  scalar=eb[lo:lo + DK, j, at:at + 1], in1=bank[lo:lo + DK, h * P:(h + 1) * P],
                                                  op0=ALU.mult, op1=ALU.add)
                return last

            def accumulate(o):
                part = acc[:, o % 2, :]
                if o >= 2:
                    dve.wait_ge(sums_done, o - 1)
                for k in range(KD):
                    n = 2 * o + k // (KD // 2)
                    row = ada[n % 2][:, k % (KD // 2), :]
                    if k == 0:
                        dve.wait_ge(ada_in[0], 16 * (o + 1))
                        link(v.tensor_scalar(part, row, siluc[:, 0:1], None, ALU.mult))
                        continue
                    if k == KD // 2:
                        dve.sem_inc(ada_read, 1)
                        dve.wait_ge(ada_in[1], 16 * (o + 1))
                    link(v.scalar_tensor_tensor(out=part, in0=row, scalar=siluc[:, k:k + 1], in1=part,
                                                op0=ALU.mult, op1=ALU.add))
                dve.sem_inc(ada_read, 1)
                dve.sem_inc(acc_ready, 1)

            def finish_modulation(o):
                m = MODS[o]
                dve.wait_ge(sums_done, o + 1)
                if m == 2:
                    dve.wait_ge(rows_in, 32)
                    for c, bank in ((0, R0), (1, R1)):
                        link(v.tensor_tensor(gate1[:, c * 512:(c + 1) * 512], bank[:, :], gate1[:, c * 512:(c + 1) * 512], ALU.add))
                    dve.sem_inc(ada_evac, 1)
                    link(v.tensor_tensor(gate1[:], gate1[:], gprow, ALU.mult))
                    return
                dst = mods[:, m, :]
                link(v.tensor_tensor(dst, MOD_BANKS[o][:, 0:KD], badac[:, m, :], ALU.add))
                dve.sem_inc(ada_evac, 1)
                if m in (1, 4):
                    link(v.scalar_tensor_tensor(out=dst, in0=dst, scalar=1.0, in1=gcol[:, m // 4, :], op0=ALU.add, op1=ALU.mult))
                if m == 5:
                    link(v.tensor_tensor(dst, dst, gcol[:, 2, :], ALU.mult))
                    dve.sem_inc(gate2_ready, 1)

            dve.wait_ge(silu_ready, 1)
            accumulate(0)
            dve.wait_ge(const_ready, 1)
            dve.wait_ge(wst_done, 1)
            link(v.tensor_copy(wsT[:, 0:4, :], T0[:, :].rearrange("p (k n) -> p k n", k=4)))
            v.tensor_copy(wsT[:, 4:8, :], T1[:, :].rearrange("p (k n) -> p k n", k=4)).then_inc(wst_evac, 1)
            dve.wait_ge(wst_done, 2)
            link(v.tensor_copy(bsT[:], T0[:, 0:SH]))
            link(v.tensor_copy(bgkT[:], T0[:, 16:18]))
            link(v.tensor_copy(bgT[:], T0[:, 64:64 + KD * E].rearrange("p (k e) -> p e k", k=KD)))
            v.tensor_scalar(buT[:], T1[:, 64:64 + KD * E].rearrange("p (k e) -> p e k", k=KD), 1.0, None,
                            ALU.add).then_inc(wst_evac, 1)
            accumulate(1)
            finish_modulation(0)
            finish_modulation(1)
            normed_x(0)
            next_nT(0)
            v_squares(0)
            v_norm(0)
            normed_x(1)
            for o in range(2, len(MODS)):
                accumulate(o)
                if o > 2:
                    finish_modulation(o - 1)
            finish_modulation(len(MODS) - 1)

            def tile(t, back, ahead):
                ch.restart()
                if back:
                    normed_h(t - 1)
                dve.wait_ge(z_done, t + 1)
                for j in range(2):
                    last = v.tensor_scalar(zb[:, j, :], ZB[:, P + j * P:P + (j + 1) * P], bgkT[:, j:j + 1], None, ALU.add)
                last.then_inc(z_ready, 1)
                if ahead:
                    next_nT(t + 1)
                dve.wait_ge(lnz_ready, t + 1)
                link(v.scalar_tensor_tensor(out=zb, in0=zb, scalar=0.0, in1=az, op0=ALU.min, op1=ALU.subtract))
                link(v.tensor_tensor_scan(bc[:].rearrange("p a n -> p (a n)"), reset[:], zb.rearrange("p a n -> p (a n)"),
                                          0.0, ALU.mult, ALU.add))
                bc4 = bc[:].rearrange("p a (c n) -> p (a c) n", c=2)
                v.tensor_tensor(zb.rearrange("p a (c n) -> p (a c) n", c=2), bc4,
                                bc4[:, :, CH - 1:CH].broadcast_to((P, 4, CH)), ALU.subtract).then_inc(bc_ready, 1)
                dve.wait_ge(exp_ready, t + 1)
                q = QK[:, 0:2 * P].rearrange("p (a n) -> p a n", a=2)
                k = QK[:, 2 * P:4 * P].rearrange("p (a n) -> p a n", a=2)
                for h in range(2):
                    lo = h * DK
                    v.scalar_tensor_tensor(out=qz[lo:lo + DK, h, :, :], in0=q[lo:lo + DK], scalar=DK ** -0.5,
                                           in1=eb[lo:lo + DK, :, :], op0=ALU.mult, op1=ALU.mult)
                v.tensor_tensor(ks[:], k, enb[:], ALU.mult)
                v.tensor_tensor(kdT, k, dec[:], ALU.mult).then_inc(qks_ready, 1)
                if back:
                    n2_columns(t - 1)
                    read_logits(t - 1)
                dve.wait_ge(kdt_done, t + 1)
                for c in range(2):
                    last = v.tensor_copy(kdz[c * CH:(c + 1) * CH, c, :], T0[c * CH:(c + 1) * CH, 0:2 * P])
                last.then_inc(kdz_ready, 1)
                dve.wait_ge(s_done, t + 1)
                ch.settle()
                v.copy_predicated(Sm, keep.bitcast(I32), OB[:, :].rearrange("p (h n) -> p h n", h=GH)).then_inc(sm_ready, 1)
                dve.wait_ge(ds_done, t + 1)
                decay_state(0, 1, T1, CH - 1).then_inc(st1_ready, 1)
                if back:
                    choose(t - 1)
                dve.wait_ge(sgu_done, t + 1)
                c3 = cat[:, 0:DS].rearrange("p (h d) -> p h d", h=SH)
                link(v.tensor_tensor(c3, SG[:, :].rearrange("p (h d) -> p h d", h=SH), b3(bsT[:], SHD), ALU.add))
                v.tensor_tensor(cat[:, 0:DS], cat[:, 0:DS], rowbuf(t, 0), ALU.mult)
                if ahead:
                    v_squares(t + 1)
                if back:
                    weigh(t - 1)
                    place(t - 1)
                dve.wait_ge(osq_ready, t + 1)
                v.tensor_reduce(os_[:, 0, :], osq[:].rearrange("p (h d) -> p h d", h=GH), AX_X, ALU.add).then_inc(osum_ready, 1)
                dve.wait_ge(st1_ready, t + 1)
                decay_state(1, 0, ZB, P - 1).then_inc(st0_ready, 1)
                dve.wait_ge(orstd_ready, t + 1)
                inverse(os_[:, 1, :])
                o3 = cat[:, DS:D].rearrange("p (h d) -> p h d", h=GH)
                link(v.tensor_tensor(o3, QK[:, :].rearrange("p (h d) -> p h d", h=GH), b3(os_[:, 1, :], GV), ALU.mult))
                link(v.tensor_tensor(o3, o3, go_row[:].unsqueeze(1).broadcast_to((P, GH, GV)), ALU.mult))
                v.tensor_tensor(cat[:, DS:D], cat[:, DS:D], rowbuf(t, 3), ALU.mult).then_inc(cat_ready, 1)
                if ahead:
                    v_norm(t + 1)
                dve.wait_ge(catt_done, t * 2 + 1)
                v.tensor_copy(catT[:, 0:4, :], T0[:, :].rearrange("p (k n) -> p k n", k=4)).then_inc(catTd, 1)
                if ahead == 2:
                    normed_x(t + 2)
                dve.wait_ge(mstat, t + 1)
                inverse(ms[:, 3:4])
                for j, bank in ((0, R0), (1, R1)):
                    link(v.scalar_tensor_tensor(out=cat[:, j * 512:(j + 1) * 512], in0=bank[:, :], scalar=ms[:, 3:4],
                                                in1=gate1[:, j * 512:(j + 1) * 512], op0=ALU.mult, op1=ALU.mult))
                v.tensor_tensor(xrow(t), xrow(t), cat[:], ALU.add).then_inc(h_ready, 1)

            def normed_h(t):
                dve.wait_ge(hstat, t + 1)
                inverse(ms[:, 5:6])
                dve.wait_ge(hn_free, t + 1)
                v.tensor_scalar(hn[:], xrow(t), ms[:, 5:6], None, ALU.mult).then_inc(n2_ready, 1)

            def n2_columns(t):
                modulate(catT, A2, B2, n2T_ready, lambda half: dve.wait_ge(n2t_done, t + 1))

            def read_logits(t):
                dve.wait_ge(lg_done, t + 1)
                link(v.tensor_tensor(lg[:], ZB[:, 0:E], br[:], ALU.add))

            def choose(t):
                link(v.max(top8[:], lg[:]))
                link(v.max_index(ti8[:], top8[:], lg[:]))
                link(v.tensor_copy(tif[:], ti8[:, 0:TOPK]))
                link(v.tensor_tensor(oneh[:], iotaE[:].unsqueeze(1).broadcast_to((P, TOPK, E)), b3(tif[:], E), ALU.is_equal))
                v.tensor_reduce(chosen[:], oneh[:].rearrange("p k e -> p e k"), AX_X, ALU.add).then_inc(chosen_ready, 1)
                v.tensor_scalar(dif4[:], top8[:, 0:TOPK], top8[:, 0:1], None, ALU.subtract).then_inc(dif_ready, 1)

            def weigh(t):
                dve.wait_ge(ex_ready, t + 1)
                link(v.reciprocal(exsum[:, 1:2], exsum[:, 0:1]))
                pr = probs[:, bass.ds(t, 1), :].rearrange("p a k -> p (a k)")
                link(v.tensor_scalar(pcur[:], ex4[:], exsum[:, 1:2], None, ALU.mult))
                v.tensor_copy(pr, pcur[:])
                link(v.tensor_tensor(tmpk[:], oneh[:], b3(pcur[:], E), ALU.mult))
                link(v.tensor_reduce(wden[:, bass.ds(t, 1), :].rearrange("p a e -> p (a e)"),
                                     tmpk[:].rearrange("p k e -> p e k"), AX_X, ALU.add))

            def place(t):
                dve.wait_ge(cum_done, t + 1)
                link(v.tensor_copy(cum[:], OB[:, 0:E]))
                link(v.tensor_tensor(csum[:], csum[:], chosen[:], ALU.add))
                link(v.tensor_tensor(tmpk[:], oneh[:], cum[:].unsqueeze(1).broadcast_to((P, TOPK, E)), ALU.mult))
                link(v.tensor_reduce(rank[:], tmpk[:], AX_X, ALU.add))
                link(v.tensor_copy(ranki[:], rank[:]))
                link(v.tensor_scalar(ia[:], ranki[:], P - 1, TPITCH.bit_length() - 1, ALU.bitwise_and, ALU.logical_shift_left))
                link(v.tensor_scalar(ib[:], ranki[:], P.bit_length() - 1, None, ALU.logical_shift_right))
                link(v.tensor_scalar(ic[:], tif[:], float(COLS), None, ALU.mult))
                link(v.tensor_tensor(iab[:], ia[:], ib[:], ALU.add))
                dve.wait_ge(slot_free, t + 1)
                link(v.tensor_copy(vcur[:], vals[:, bass.ds(t, 1), :].rearrange("p a k -> p (a k)")))
                v.tensor_tensor(slot[:], iab[:], ic[:], ALU.add).then_inc(slot_ready, 1)
                dve.wait_ge(slot_ready, t + 1)

            tile(0, False, 2)
            with dve.Fori(1, NT - 2) as t:
                tile(t, True, 2)
            tile(NT - 2, True, 1)
            tile(NT - 1, True, 0)
            ch.restart()
            normed_h(NT - 1)
            n2_columns(NT - 1)
            read_logits(NT - 1)
            choose(NT - 1)
            weigh(NT - 1)
            place(NT - 1)

            dve.wait_ge(cnt_done, 1)
            link(v.memset(cnti[:, E:E + 1], 0))
            link(v.tensor_copy(cnti[:, 0:E], OB[0:1, 0:E]))
            for c in range(1, NCHUNK):
                link(v.tensor_scalar(overf[:, 0, (c - 1) * E:c * E], OB[0:1, 0:E], float(-c * CAP), None, ALU.add))
            link(v.tensor_copy(overn[:], overf[:, 0, :]))
            link(v.tensor_scalar(overf[:, 1, :], overf[:, 0, :], 0.0, None, ALU.is_gt))
            link(v.tensor_tensor_scan(overf[:, 2, :], ones[0:1, 0:NOVER], overf[:, 1, :], 0.0, ALU.mult, ALU.add))
            link(v.tensor_copy(overt[:], overf[:, 2, NOVER - 1:NOVER]))
            link(v.tensor_tensor(overf[:, 2, :], overf[:, 2, :], overf[:, 1, :], ALU.subtract))
            v.tensor_copy(overo[:], overf[:, 2, :]).then_inc(cnt_ready, 1)
            dve.wait_ge(table_in, 16)
            v.tensor_scalar(gidx, sidx[:], TOPK.bit_length() - 1, None, ALU.logical_shift_right).then_inc(gidx_ready, 1)
            for bank in ps:
                link(v.memset(bank[:, :], 0.0))
            dve.sem_inc(psum_init, 1)
            dve.sem_inc(gup_free, 2)

            def fills(m):
                for b in range(BLK):
                    dve.wait_ge(xgt_done, m * (2 * BLK) + (2 * b + 2))
                    for k in range(4, KD):
                        last = v.tensor_scalar(xT[:, k, b * P:(b + 1) * P], TD[(2 * b + 1) % 4][:, (k - 4) * P:(k - 3) * P],
                                               A2[:, k:k + 1], B2[:, k:k + 1], ALU.mult, ALU.add)
                    last.then_inc(xTd, 1)

            def hidden(m, e):
                ch.restart()
                link(v.tensor_copy(bcur[:, 0, :], bgT[:, bass.ds(e, 1), :].rearrange("p a k -> p (a k)")))
                link(v.tensor_copy(bcur[:, 1, :], buT[:, bass.ds(e, 1), :].rearrange("p a k -> p (a k)")))

                def finish(f):
                    dve.wait_ge(sig_ready, m * KD + (f + 1))
                    link(v.tensor_tensor(g_sb[:, f % 2, :], g_sb[:, f % 2, :], s_sb[:, f % 2, :], ALU.mult))
                    v.scalar_tensor_tensor(out=hT[:, f, :], in0=u_sb[:, f % 2, :], scalar=1.0 - LIMIT, in1=g_sb[:, f % 2, :],
                                           op0=ALU.max, op1=ALU.mult).then_inc(hid_ready, 1)

                for f in range(KD):
                    if f >= 2:
                        dve.wait_ge(hid_ready, m * KD + (f - 1))
                    dve.wait_ge(gup_done, m * KD + (f + 1))
                    v.tensor_scalar(g_sb[:, f % 2, :], ps[f % 2][:, 0:CAP], bcur[:, 0, f:f + 1], LIMIT,
                                    ALU.add, ALU.min).then_inc(g_ready, 1)
                    v.tensor_scalar(u_sb[:, f % 2, :], ps[2 + f % 2][:, 0:CAP], bcur[:, 1, f:f + 1], LIMIT + 1.0,
                                    ALU.add, ALU.min).then_inc(gup_free, 1)
                    if f:
                        finish(f - 1)
                finish(KD - 1)
                dve.wait_ge(hid_ready, m * KD + KD)
                ch.settle()

            fills(0)
            with dve.Fori(0, E) as e:
                hidden(e, e)
                fills(e + 1)

            def again(e, c, nth, left):
                fills(nth + (E + 1))
                hidden(nth + E, e)

            overflow(dve, again)

            dve.wait_ge(g2_in, 32)
            ch.restart()

            def weighted_sum(j, i):
                yb = stage4(i)[0]
                dve.wait_ge(bias_done, j * NS + (i + 1))
                dve.wait_ge(y_in[i], j * 16 + 16)
                w = pcur4[:, i * TOPK:(i + 1) * TOPK]
                for c, bank in enumerate(bias_banks(i)):
                    last = v.scalar_tensor_tensor(out=yb[:, c * 512:(c + 1) * 512], in0=yb[:, c * 512:(c + 1) * 512],
                                                  scalar=w[:, 0:1], in1=bank[:, :], op0=ALU.mult, op1=ALU.add)
                last.then_inc(bias_read, 1)
                dve.wait_ge(bias_read, j * NS + (i + 1))
                for k in range(1, TOPK):
                    last = v.scalar_tensor_tensor(out=yb[:, 0:D], in0=yb[:, k * D:(k + 1) * D], scalar=w[:, k:k + 1],
                                                  in1=yb[:, 0:D], op0=ALU.mult, op1=ALU.add)
                    if k < TOPK - 1:
                        link(last)
                last.then_inc(f_ready, 1)

            def finish(j, i):
                yb, hb, ob = stage4(i)
                dve.wait_ge(fstat, j * NS + (i + 1))
                inverse(os_[:, 1, i:i + 1])
                dve.wait_ge(hb_in[i], j * 16 + 16)
                link(v.scalar_tensor_tensor(out=yb[:, 0:D], in0=yb[:, 0:D], scalar=os_[:, 1, i:i + 1], in1=gate2,
                                            op0=ALU.mult, op1=ALU.mult))
                dve.wait_ge(oslot_free[i], j + 1)
                v.tensor_tensor(ob, yb[:, 0:D], hb, ALU.add).then_inc(o_ready[i], 1)

            with dve.Fori(0, NT // NS) as j:
                ch.restart()
                link(v.tensor_copy(pcur4[:], probs[:, bass.ds(j * NS, NS), :].rearrange("p a k -> p (a k)")))
                v.tensor_copy(wcur, wden[:, bass.ds(j * NS, NS), :].rearrange("p a e -> p (a e)")).then_inc(wcur_ready, 1)
                dve.wait_ge(wdt_done, j + 1)
                v.tensor_copy(wdT, T0[0:E, :]).then_inc(wdT_ready, 1)
                for i in range(NS):
                    weighted_sum(j, i)
                    if i:
                        finish(j, i - 1)
                finish(j, NS - 1)


def kernel(**inputs):
    import numpy as np
    import concourse.bacc as bacc
    from concourse.bass_utils import run_bass_kernel_spmd as run

    nc = bacc.Bacc("TRN2", target_bir_lowering=False, num_devices=1)
    arrays, aps = {}, {}
    for name in inputs:
        array = np.ascontiguousarray(inputs[name])
        arrays["in_" + name] = array
        aps[name] = nc.dram_tensor("in_" + name, array.shape, mybir.dt.from_np(array.dtype), kind="ExternalInput").ap()
    out = nc.dram_tensor("out_h", (1, T, D), F32, kind="ExternalOutput").ap()
    hybrid_block(nc, aps, out)
    return run(nc, [arrays], core_ids=[0]).results[0]["out_h"]
```
